# Optimizing a Trainium2 kernel written in Bass

```python
import jax, jax.numpy as jnp
from jax import lax
import numpy as np

D_MODEL = 1024
BATCH = 1
SEQ = 256
DEPTH = 2

N_A = DEPTH // 2
N_B = DEPTH - N_A
N_DENSE = (DEPTH + 1) // 2
N_MOE = DEPTH // 2

N_MEM = 256
M_HEADS = 4
M_HEAD_DIM = 64
M_W = M_HEADS * M_HEAD_DIM

A_HEADS = 4
A_QK_DIM = 96
A_V_DIM = 192
A_CHUNK = 64
A_QK_W = A_HEADS * A_QK_DIM
A_V_W = A_HEADS * A_V_DIM
A_IN = 2 * A_QK_W + 2 * A_V_W + 2 * A_HEADS + M_W
MIX_A = A_V_W + M_W

B_HEADS = 6
Q_LORA = 384
KV_LORA = 256
QK_NOPE = 128
QK_ROPE = 64
V_HEAD = 128
B_QK_HEAD = QK_NOPE + QK_ROPE
B_IN = Q_LORA + M_W
MIX_B = B_HEADS * V_HEAD + M_W
ROPE_THETA = 10000.0
Q_BLOCK = 128

D_FF = 3584
N_EXPERTS = 8
TOP_K = 2

EPS = 1e-6

kernel_name = "yoco_mlstm_mla_memory_moe_block"

def rms_norm(x, g):
    xf = x.astype(jnp.float32)
    y = xf * lax.rsqrt(jnp.mean(xf * xf, axis=-1, keepdims=True) + EPS)
    return (y * g.astype(jnp.float32)).astype(x.dtype)

def rope_angles(positions):
    inv = 1.0 / (ROPE_THETA ** (jnp.arange(0, QK_ROPE, 2, dtype=jnp.float32) / QK_ROPE))
    ang = positions.astype(jnp.float32)[..., None] * inv
    return jnp.cos(ang), jnp.sin(ang)

def apply_rope(x, cos, sin):
    x1, x2 = jnp.split(x.astype(jnp.float32), 2, axis=-1)
    return jnp.concatenate([x1 * cos - x2 * sin, x2 * cos + x1 * sin], axis=-1).astype(x.dtype)

def memory_kv(mem, norm_g, w_kv):
    B, M, _ = mem.shape
    kv = rms_norm(mem, norm_g) @ w_kv
    k, v = jnp.split(kv, 2, axis=-1)
    return k.reshape(B, M, M_HEADS, M_HEAD_DIM), v.reshape(B, M, M_HEADS, M_HEAD_DIM)

def memory_attention(q, mem_k, mem_v, q_g, k_g):
    B, S = q.shape[:2]
    q = rms_norm(q, q_g)
    k = rms_norm(mem_k, k_g)
    s = jnp.einsum('bshd,bmhd->bhsm', q, k).astype(jnp.float32) * (M_HEAD_DIM ** -0.5)
    p = jax.nn.softmax(s, axis=-1).astype(mem_v.dtype)
    return jnp.einsum('bhsm,bmhd->bshd', p, mem_v).reshape(B, S, M_W)

def mlstm_chunkwise(q, k, v, i_pre, f_pre):
    B, S, H, dk = q.shape
    dv = v.shape[-1]
    L = A_CHUNK
    NC = S // L
    f32 = jnp.float32

    def chunk(t):
        return t.astype(f32).reshape(B, NC, L, H, -1).transpose(0, 3, 1, 2, 4)

    def chunk_gate(t):
        return t.astype(f32).reshape(B, NC, L, H).transpose(0, 3, 1, 2)

    qc = chunk(q)
    kc = chunk(k) * (dk ** -0.5)
    vc = chunk(v)
    ig = chunk_gate(i_pre)
    lf = jax.nn.log_sigmoid(chunk_gate(f_pre))
    g = jnp.cumsum(lf, axis=-1)
    g_last = g[..., -1]

    w_loc = g_last[..., None] - g + ig
    m_loc = jnp.max(w_loc, axis=-1)
    e_loc = jnp.exp(w_loc - m_loc[..., None])
    C_loc = jnp.einsum('bhcld,bhcle->bhcde', vc * e_loc[..., None], kc)
    n_loc = jnp.einsum('bhcl,bhcle->bhce', e_loc, kc)

    def step(carry, xs):
        C, n, m = carry
        Cl, nl, ml, gl = xs
        m_new = jnp.maximum(gl + m, ml)
        a = jnp.exp(gl + m - m_new)
        b = jnp.exp(ml - m_new)
        C_new = a[..., None, None] * C + b[..., None, None] * Cl
        n_new = a[..., None] * n + b[..., None] * nl
        return (C_new, n_new, m_new), (C, n, m)

    init = (jnp.zeros((B, H, dv, dk), f32), jnp.zeros((B, H, dk), f32), jnp.zeros((B, H), f32))
    xs = (jnp.moveaxis(C_loc, 2, 0), jnp.moveaxis(n_loc, 2, 0),
          jnp.moveaxis(m_loc, 2, 0), jnp.moveaxis(g_last, 2, 0))
    _, (C_prev, n_prev, m_prev) = lax.scan(step, init, xs)
    C_prev = jnp.moveaxis(C_prev, 0, 2)
    n_prev = jnp.moveaxis(n_prev, 0, 2)
    m_prev = jnp.moveaxis(m_prev, 0, 2)

    a_log = g + m_prev[..., None]
    causal = jnp.tril(jnp.ones((L, L), dtype=bool))
    d_log = jnp.where(causal, g[..., :, None] - g[..., None, :] + ig[..., None, :], -jnp.inf)
    m_t = jnp.maximum(a_log, jnp.max(d_log, axis=-1))
    inter = jnp.exp(a_log - m_t)
    P = jnp.exp(d_log - m_t[..., None]) * jnp.einsum('bhctd,bhcsd->bhcts', qc, kc)
    num = inter[..., None] * jnp.einsum('bhcde,bhcte->bhctd', C_prev, qc) \
        + jnp.einsum('bhcts,bhcsd->bhctd', P, vc)
    den = inter * jnp.einsum('bhce,bhcte->bhct', n_prev, qc) + jnp.sum(P, axis=-1)
    h = num / jnp.maximum(jnp.abs(den), jnp.exp(-m_t))[..., None]
    return h.transpose(0, 2, 3, 1, 4).reshape(B, S, H, dv)

def mlstm_layer(x, norm_g, w_in, gate_bias, head_g, w_out, mem_k, mem_v, mq_g, mk_g):
    B, S, _ = x.shape
    proj = rms_norm(x, norm_g) @ w_in
    offs = [A_QK_W, 2 * A_QK_W, 2 * A_QK_W + A_V_W, 2 * A_QK_W + 2 * A_V_W,
            2 * A_QK_W + 2 * A_V_W + 2 * A_HEADS]
    q, k, v, o, ifg, mq = jnp.split(proj, offs, axis=-1)
    ifg = ifg + gate_bias
    i_pre, f_pre = ifg[..., :A_HEADS], ifg[..., A_HEADS:]
    hm = mlstm_chunkwise(q.reshape(B, S, A_HEADS, A_QK_DIM), k.reshape(B, S, A_HEADS, A_QK_DIM),
                         v.reshape(B, S, A_HEADS, A_V_DIM), i_pre, f_pre).astype(x.dtype)
    hm = rms_norm(hm, head_g.reshape(A_HEADS, A_V_DIM)).reshape(B, S, A_V_W)
    hm = hm * jax.nn.sigmoid(o)
    mo = memory_attention(mq.reshape(B, S, M_HEADS, M_HEAD_DIM), mem_k, mem_v, mq_g, mk_g)
    return x + jnp.concatenate([hm, mo], axis=-1) @ w_out

def shared_latent_kv(h, kv_norm, w_dkv, kv_a_norm, w_ukv, k_head_g, cos, sin):
    B, S, _ = h.shape
    z = rms_norm(h, kv_norm) @ w_dkv
    c_kv, k_rope = z[..., :KV_LORA], z[..., KV_LORA:]
    kv = (rms_norm(c_kv, kv_a_norm) @ w_ukv).reshape(B, S, B_HEADS, QK_NOPE + V_HEAD)
    k_nope, v = kv[..., :QK_NOPE], kv[..., QK_NOPE:]
    k = jnp.concatenate([k_nope, jnp.broadcast_to(k_rope[:, :, None, :], (B, S, B_HEADS, QK_ROPE))], axis=-1)
    k = rms_norm(k, k_head_g)
    k = jnp.concatenate([k[..., :QK_NOPE],
                         apply_rope(k[..., QK_NOPE:], cos[:, :, None], sin[:, :, None])], axis=-1)
    return k, v

def causal_block_attention(q, k, v):
    B, S, H, dq = q.shape
    scale = dq ** -0.5
    qt = q.transpose(0, 2, 1, 3)
    kt = k.transpose(0, 2, 1, 3)
    vt = v.transpose(0, 2, 1, 3)
    local_mask = jnp.tril(jnp.ones((Q_BLOCK, Q_BLOCK), dtype=bool))
    outs = []
    for blk in range(S // Q_BLOCK):
        start = blk * Q_BLOCK
        end = start + Q_BLOCK
        s = jnp.einsum('bhqd,bhkd->bhqk', qt[:, :, start:end], kt[:, :, :end]).astype(jnp.float32) * scale
        mask = jnp.concatenate([jnp.ones((Q_BLOCK, start), dtype=bool), local_mask], axis=1)
        p = jax.nn.softmax(jnp.where(mask, s, -jnp.inf), axis=-1).astype(v.dtype)
        outs.append(jnp.einsum('bhqk,bhkd->bqhd', p, vt[:, :, :end]))
    return jnp.concatenate(outs, axis=1)

def mla_layer(x, norm_g, w_in, q_a_g, w_uq, q_head_g, w_out, k_sh, v_sh, cos, sin,
              mem_k, mem_v, mq_g, mk_g):
    B, S, _ = x.shape
    proj = rms_norm(x, norm_g) @ w_in
    cq, mq = proj[..., :Q_LORA], proj[..., Q_LORA:]
    q = (rms_norm(cq, q_a_g) @ w_uq).reshape(B, S, B_HEADS, B_QK_HEAD)
    q = rms_norm(q, q_head_g)
    q = jnp.concatenate([q[..., :QK_NOPE],
                         apply_rope(q[..., QK_NOPE:], cos[:, :, None], sin[:, :, None])], axis=-1)
    att = causal_block_attention(q, k_sh, v_sh).reshape(B, S, B_HEADS * V_HEAD)
    mo = memory_attention(mq.reshape(B, S, M_HEADS, M_HEAD_DIM), mem_k, mem_v, mq_g, mk_g)
    return x + jnp.concatenate([att, mo], axis=-1) @ w_out

def swiglu(h, w_gate_up, w_down):
    g, u = jnp.split(h @ w_gate_up, 2, axis=-1)
    return (jax.nn.silu(g) * u) @ w_down

def moe_ffn(h, router, w_gate_up, w_down):
    B, S, D = h.shape
    t = h.reshape(B * S, D)
    logits = (t @ router).astype(jnp.float32)
    top_v, top_i = lax.top_k(logits, TOP_K)
    gates = jax.nn.softmax(top_v, axis=-1)
    combine = jnp.sum(jax.nn.one_hot(top_i, N_EXPERTS, dtype=jnp.float32) * gates[..., None], axis=1)
    out = jnp.zeros_like(t)
    for e in range(N_EXPERTS):
        out = out + combine[:, e:e + 1].astype(t.dtype) * swiglu(t, w_gate_up[e], w_down[e])
    return out.reshape(B, S, D)

def setup_inputs(seed: int = 0) -> dict:
    key = jax.random.key(seed)
    ks = iter(jax.random.split(key, 40))
    f32 = jnp.float32

    def w(shape, fan_in):
        return jax.random.normal(next(ks), shape, f32) * (fan_in ** -0.5)

    def gain(shape):
        return 1.0 + 0.02 * jax.random.normal(next(ks), shape, f32)

    x = jax.random.normal(next(ks), (BATCH, SEQ, D_MODEL), f32)
    mem = jax.random.normal(next(ks), (BATCH, N_MEM, D_MODEL), f32)
    offset = jax.random.randint(next(ks), (BATCH, 1), 0, 4096, dtype=jnp.int32)
    positions = jnp.arange(SEQ, dtype=jnp.int32)[None, :] + offset

    i_bias = 0.1 * jax.random.normal(next(ks), (N_A, A_HEADS), f32)
    f_bias = 3.0 + 0.1 * jax.random.normal(next(ks), (N_A, A_HEADS), f32)

    return {
        "x": x, "mem": mem, "positions": positions,
        "a_norm": gain((N_A, D_MODEL)),
        "a_w_in": w((N_A, D_MODEL, A_IN), D_MODEL),
        "a_gate_bias": jnp.concatenate([i_bias, f_bias], axis=-1),
        "a_head_norm": gain((N_A, A_V_W)),
        "a_w_out": w((N_A, MIX_A, D_MODEL), MIX_A),
        "b_norm": gain((N_B, D_MODEL)),
        "b_w_in": w((N_B, D_MODEL, B_IN), D_MODEL),
        "b_q_a_norm": gain((N_B, Q_LORA)),
        "b_w_uq": w((N_B, Q_LORA, B_HEADS * B_QK_HEAD), Q_LORA),
        "b_q_head_norm": gain((N_B, B_QK_HEAD)),
        "b_w_out": w((N_B, MIX_B, D_MODEL), MIX_B),
        "kv_norm": gain((D_MODEL,)),
        "w_dkv": w((D_MODEL, KV_LORA + QK_ROPE), D_MODEL),
        "kv_a_norm": gain((KV_LORA,)),
        "w_ukv": w((KV_LORA, B_HEADS * (QK_NOPE + V_HEAD)), KV_LORA),
        "k_head_norm": gain((B_QK_HEAD,)),
        "mem_norm": gain((DEPTH, D_MODEL)),
        "mem_w_kv": w((DEPTH, D_MODEL, 2 * M_W), D_MODEL),
        "mem_q_norm": gain((DEPTH, M_HEAD_DIM)),
        "mem_k_norm": gain((DEPTH, M_HEAD_DIM)),
        "ffn_norm": gain((DEPTH, D_MODEL)),
        "dense_w_gate_up": w((N_DENSE, D_MODEL, 2 * D_FF), D_MODEL),
        "dense_w_down": w((N_DENSE, D_FF, D_MODEL), D_FF),
        "moe_router": w((N_MOE, D_MODEL, N_EXPERTS), D_MODEL),
        "moe_w_gate_up": w((N_MOE, N_EXPERTS, D_MODEL, 2 * D_FF), D_MODEL),
        "moe_w_down": w((N_MOE, N_EXPERTS, D_FF, D_MODEL), D_FF),
    }

def reference(x, mem, positions,
              a_norm, a_w_in, a_gate_bias, a_head_norm, a_w_out,
              b_norm, b_w_in, b_q_a_norm, b_w_uq, b_q_head_norm, b_w_out,
              kv_norm, w_dkv, kv_a_norm, w_ukv, k_head_norm,
              mem_norm, mem_w_kv, mem_q_norm, mem_k_norm,
              ffn_norm, dense_w_gate_up, dense_w_down,
              moe_router, moe_w_gate_up, moe_w_down):
    cos, sin = rope_angles(positions)
    k_sh = v_sh = None
    if N_A == 0:
        k_sh, v_sh = shared_latent_kv(x, kv_norm, w_dkv, kv_a_norm, w_ukv, k_head_norm, cos, sin)
    for l in range(DEPTH):
        mem_k, mem_v = memory_kv(mem, mem_norm[l], mem_w_kv[l])
        if l < N_A:
            x = mlstm_layer(x, a_norm[l], a_w_in[l], a_gate_bias[l], a_head_norm[l], a_w_out[l],
                            mem_k, mem_v, mem_q_norm[l], mem_k_norm[l])
        else:
            j = l - N_A
            x = mla_layer(x, b_norm[j], b_w_in[j], b_q_a_norm[j], b_w_uq[j], b_q_head_norm[j], b_w_out[j],
                          k_sh, v_sh, cos, sin, mem_k, mem_v, mem_q_norm[l], mem_k_norm[l])
        hf = rms_norm(x, ffn_norm[l])
        if l % 2 == 0:
            x = x + swiglu(hf, dense_w_gate_up[l // 2], dense_w_down[l // 2])
        else:
            x = x + moe_ffn(hf, moe_router[l // 2], moe_w_gate_up[l // 2], moe_w_down[l // 2])
        if l == N_A - 1:
            k_sh, v_sh = shared_latent_kv(x, kv_norm, w_dkv, kv_a_norm, w_ukv, k_head_norm, cos, sin)
    return x


_drawn_inputs = setup_inputs


def setup_inputs(seed=0):
    import zlib

    import numpy as np

    out = dict(_drawn_inputs(seed))
    spreads = {}
    factors = {'b_norm': 4.135,
     'b_q_a_norm': 4.108,
     'b_q_head_norm': 5.347,
     'kv_norm': 8.0,
     'kv_a_norm': 4.057,
     'k_head_norm': 4.126,
     'mem_norm': 4.159,
     'mem_q_norm': 8.0,
     'mem_k_norm': 5.479}
    for name, (base, spread) in spreads.items():
        noise = np.random.default_rng([zlib.crc32(name.encode()), seed]).standard_normal(out[name].shape)
        drawn = base * np.exp(spread * noise) if base else spread * noise
        out[name] = __import__('jax').numpy.asarray(drawn.astype(out[name].dtype))
    for name, factor in factors.items():
        out[name] = (out[name] * factor).astype(out[name].dtype)
    return out
```

```python
from contextlib import ExitStack

import numpy as np

import concourse.bass as bass
from concourse import mybir

ALU = mybir.AluOpType
ACT = mybir.ActivationFunctionType
AX = mybir.AxisListType
F32 = mybir.dt.float32
I32 = mybir.dt.int32
U32 = mybir.dt.uint32

P = 128
EPS = 1e-6
SLOTS = 7
SLOT = 4096
CAP = 96
NEG = -float(2.0 ** 100)
ROPE_THETA = 10000.0
STAGE = 99


def build(nc, T, out):
    SEQ, D = T["x"].shape[1:]
    NT = SEQ // P
    KD = D // P
    NMEM = T["mem"].shape[1]
    AH = T["a_gate_bias"].shape[1] // 2
    AV = T["a_head_norm"].shape[1] // AH
    MH, MD = 4, T["mem_q_norm"].shape[1]
    MW = MH * MD
    AIN = T["a_w_in"].shape[2]
    AQ = (AIN - 2 * AH * AV - 2 * AH - MW) // (2 * AH)
    QL = T["b_q_a_norm"].shape[1]
    KVL = T["kv_a_norm"].shape[0]
    QKH = T["b_q_head_norm"].shape[1]
    BH = T["b_w_uq"].shape[2] // QKH
    ROPE = T["w_dkv"].shape[1] - KVL
    NOPE = QKH - ROPE
    VH = T["w_ukv"].shape[1] // BH - NOPE
    FF = T["dense_w_down"].shape[1]
    NE = T["moe_router"].shape[2]
    KF = FF // P
    HR = ROPE // 2
    assert NT == 2 and KD == 8 and NMEM == SEQ and MW == 256 and AH == 4 and BH == 6 and NOPE == P and VH == P
    PASSES = -(-SEQ // CAP)

    x_d, mem_d = T["x"][0], T["mem"][0]

    def rows(w):
        return w.rearrange("(k p) n -> p k n", p=P)

    def cols(w, a, b):
        return rows(w)[:, :, a:b]

    aw, bw = T["a_w_in"][0], T["b_w_in"][0]
    aqw, avw = AH * AQ, AH * AV
    o_k, o_v, o_o, o_g = aqw, 2 * aqw, 2 * aqw + avw, 2 * aqw + 2 * avw
    hv = avw // 2
    HD = D // 2
    stream = [
        ("memkv0", cols(T["mem_w_kv"][0], 0, 2 * MW)), ("memkv1", cols(T["mem_w_kv"][1], 0, 2 * MW)),
        ("gmq", cols(aw, o_g, AIN)), ("q", cols(aw, 0, aqw)), ("k", cols(aw, o_k, o_v)),
        ("v0", cols(aw, o_v, o_v + hv)), ("v1", cols(aw, o_v + hv, o_o)),
        ("o0", cols(aw, o_o, o_o + hv)), ("o1", cols(aw, o_o + hv, o_g)),
        ("aout0", cols(T["a_w_out"][0], 0, HD)), ("aout1", cols(T["a_w_out"][0], HD, D)),
    ]
    FC = 2 * P
    NGU = FF // FC
    KDN = 4
    NDN = KF // KDN
    PER = NGU + NDN
    assert NGU == 2 * SLOTS and NDN == SLOTS

    def gu_item(w, c):
        return cols(w, c * FC, (c + 1) * FC), cols(w, FF + c * FC, FF + (c + 1) * FC)

    def dn_item(w, c):
        return rows(w)[:, c * KDN:(c + 1) * KDN, :]

    stream += [(f"gu{c}", gu_item(T["dense_w_gate_up"][0], c)) for c in range(NGU)]
    stream += [(f"dn{c}", dn_item(T["dense_w_down"][0], c)) for c in range(NDN)]
    stream += [
        ("dkv", rows(T["w_dkv"])), ("cq", cols(bw, 0, QL)), ("mq", cols(bw, QL, QL + MW)),
        ("ukv", rows(T["w_ukv"])), ("uq", rows(T["b_w_uq"][0])),
        ("bout0", cols(T["b_w_out"][0], 0, HD)), ("bout1", cols(T["b_w_out"][0], HD, D)),
    ]
    NS = len(stream)
    OFF = -NS % SLOTS
    item = {name: n for n, (name, _) in enumerate(stream)}

    def slot_of(n):
        return (OFF + n) % SLOTS

    def filled(n):
        return sum(16 * len(stream[m][1]) if isinstance(stream[m][1], tuple) else 16 for m in range(n % SLOTS, n + 1, SLOTS))

    BASE_FILLS = [sum(filled(n) - (filled(n - SLOTS) if n >= SLOTS else 0) for n in range(NS) if slot_of(n) == j)
                  for j in range(SLOTS)]
    EXPERT_FILLS = 16 * (2 * 2 + 1)

    with ExitStack() as ctx:
        def sb(name, shape, dt=F32):
            return ctx.enter_context(nc.sbuf_tensor(name, shape, dt))

        sems = {}

        def S(name):
            if name not in sems:
                sems[name] = ctx.enter_context(nc.semaphore(name))
            return sems[name]

        PS = ctx.enter_context(nc.psum_tensor("PS", [P, 8, 512], F32))
        ring = sb("ring", [P, SLOTS, SLOT])
        xres = sb("xres", [P, NT, D])
        xn = sb("xn", [P, NT, D])
        xT = sb("xT", [P, KD, SEQ])
        mix = sb("mix", [P, NT, D])
        memkT = sb("memkT", [P, 2, 2, NMEM])
        memv = sb("memv", [P, 2, NT, MW])
        ident = sb("ident", [P, P])
        ones = sb("ones", [P, P])
        mask_kq = sb("mask_kq", [P, P])
        mask_qk = sb("mask_qk", [P, P])
        before = sb("before", [P, P])
        sel = sb("sel", [AH, AH, P])
        NG = 7 * KD + avw // P + QL // P + KVL // P + 4
        gains = sb("gains", [P, NG])
        hg = sb("hg", [P, 2 * QKH])
        bias_i = sb("bias_i", [AH, 1])
        bias_f = sb("bias_f", [AH, 1])
        nhalf = sb("nhalf", [P, 16])
        sumsq = sb("sumsq", [P, 16])
        meansq = sb("meansq", [P, 16])
        rstd = sb("rstd", [P, 16])
        posi = sb("posi", [P, NT], I32)
        posf = sb("posf", [P, NT])
        invf = sb("invf", [P, HR])
        rot = sb("rot", [P, 6, NT, HR])
        roti = sb("roti", [P, NT, HR], I32)
        smax = sb("smax", [P, 16])
        ssum = sb("ssum", [P, 16])
        srec = sb("srec", [P, 16])
        sbias = sb("sbias", [P, 16])
        router = sb("router", [P, KD, NE])
        arena = sb("arena", [P, 11776])

        def carve(at, *shape):
            n = int(np.prod(shape))
            v = arena[:, at:at + n]
            if len(shape) == 1:
                return v
            names = "abcd"[:len(shape)]
            return v.rearrange(f"p ({' '.join(names)}) -> p {' '.join(names)}",
                               **{c: s for c, s in zip(names, shape)})

        sq = carve(9728, NT * D)
        memS = carve(0, NT, D)
        memT = carve(2048, 2, KD, NMEM)
        kS = carve(0, 2, NT, MW)
        mqS = carve(1024, NT, MW)
        mqT = carve(1536, 2, SEQ)
        qT = carve(2048, AH, SEQ)
        kT = carve(3072, AH, SEQ)
        VW = AV + 1
        A0 = 6144
        v1 = carve(A0, NT, AH, VW)
        og = carve(A0 + NT * AH * VW, NT, avw)
        assert A0 + NT * AH * VW + NT * avw <= 9728
        grow = arena[0:NG, A0:A0 + P]
        hrow = arena[0:1, A0 + P:A0 + P + 2 * QKH]
        gat = arena[0:AH, 4096:4096 + 8 * SEQ].rearrange("p (a b) -> p a b", a=8)
        gi, gf, gt, glf, gG, ga, gM, gone = (gat[:, r] for r in range(8))
        gm, gem, gneg = gf, gt, glf
        gN = sb("gN", [P, 2, NT, AH])
        den = sb("den", [P, NT * AH])
        xflat = xn[:, :, :].rearrange("p a b -> p (a b)")
        Dm = mix[:, :, :].rearrange("p a b -> p (a b)")[:, 0:AH * 384].rearrange("p (a b) -> p a b", a=AH)
        PmT = xflat[:, 0:AH * 384].rearrange("p (a b) -> p a b", a=AH)
        mP = xn[:, :, :].rearrange("p a (h m) -> p a h m", h=MH)
        mPT = xT[:, :, :].rearrange("p a b -> p (a b)").rearrange("p (t h m q) -> p t h m q", t=NT, h=MH, m=2)
        hT = carve(0, KF, SEQ)
        silu = carve(KF * SEQ, 4, SEQ)
        xTk = carve(0, KD, SEQ)
        qF = carve(0, NT * BH, QKH)
        cqS = carve(2688, NT, QL)
        mqS1 = carve(3456, NT, MW)
        ckvT = carve(3968, 2, SEQ)
        cqT = carve(4480, 3, SEQ)
        kTn = carve(2304, BH, SEQ)
        kTr = arena[0:ROPE, 3840:3840 + BH * SEQ].rearrange("p (h s) -> p h s", h=BH)
        kF = carve(5760, NT * BH, QKH)
        zS = carve(8064, NT, KVL + ROPE)
        mqT1 = carve(8704, 2, SEQ)
        sqbig = carve(9472, NT * BH * QKH)
        qTn = xT[:, 0:BH, :]
        qTr = xflat[0:ROPE, 0:BH * SEQ].rearrange("p (h s) -> p h s", h=BH)
        vF = mix[:, :, :].rearrange("p a b -> p (a b)")[:, 0:NT * BH * VH].rearrange("p (t h b) -> p t h b", t=NT, b=VH)
        Pb = carve(5760, BH, 384)
        PT = carve(0, BH, 384)
        o = 0
        xe = carve(o, KD, CAP); o += KD * CAP
        Sx = carve(o, NT, CAP); o += NT * CAP
        Sw = carve(o, NT, CAP); o += NT * CAP
        eT = carve(o, KF, CAP); o += KF * CAP
        esilu = carve(o, 2, 2, CAP); o += 4 * CAP
        yT = carve(o, KD, CAP); o += KD * CAP
        y = arena[0:CAP, o:o + D]; o += D
        G = arena[0:CAP, o:o + SEQ].rearrange("p (t s) -> p t s", t=NT); o += SEQ
        NC = (PASSES + 1) * NE
        iota = carve(o, CAP); o += CAP
        iotai = arena[:, o:o + CAP].bitcast(I32); o += CAP
        lg = carve(o, NT, NE); o += NT * NE
        m8 = carve(o, NT, 8); o += NT * 8
        idxf = carve(o, NT, 8); o += NT * 8
        idx8 = arena[:, o:o + NT * 8].bitcast(U32).rearrange("p (a b) -> p a b", a=NT); o += NT * 8
        oh1 = carve(o, NT, NE); o += NT * NE
        oh2 = carve(o, NT, NE); o += NT * NE
        chosen = carve(o, NT, NE); o += NT * NE
        keys = carve(o, NT, NC); o += NT * NC
        combs = carve(o, NT, NC); o += NT * NC
        gt2 = carve(o, 16); o += 16
        assert o <= 9728
        cnt_i = sb("cnt_i", [P, 1], I32)

        NORMS = ["mem", "x0", "mk0", "mk1", "mq0", "hm", "x1", "x2", "ckv", "cq", "mq1", "kh", "qh", "x3"]
        nidx = {n: i for i, n in enumerate(NORMS)}

        def nat(v, W):
            return v.rearrange("p a (h w) -> p a h w", w=W)

        nview = {
            "mem": (memS, memS, D), "x0": (xres[:, :, :], xn[:, :, :], D),
            "mk0": (nat(kS[:, 0], MD), None, MD), "mk1": (nat(kS[:, 1], MD), None, MD),
            "mq0": (nat(mqS, MD), None, MD), "hm": (nat(mix[:, :, 0:avw], AV), None, AV),
            "x1": (xres[:, :, :], xn[:, :, :], D), "x2": (xres[:, :, :], xn[:, :, :], D),
            "ckv": (zS[:, :, 0:KVL], None, KVL), "cq": (cqS, None, QL), "mq1": (nat(mqS1, MD), None, MD),
            "kh": (kF, None, QKH), "qh": (qF, None, QKH), "x3": (xres[:, :, :], xn[:, :, :], D),
        }

        def groups(name):
            v = nview[name][0]
            return int(np.prod(v.shape[1:-1]))

        def shaped(tile, name):
            v = nview[name][0]
            t = tile[:, 0:groups(name)]
            if len(v.shape) == 4:
                t = t.rearrange("p (a b) -> p a b", a=v.shape[1])
            return t

        def sq_of(name):
            v = nview[name][0]
            n = int(np.prod(v.shape[1:]))
            if name in ("kh", "qh"):
                base = sqbig[:, 0:n]
            else:
                base = sq[:, 0:n]
            if len(v.shape) == 4:
                return base.rearrange("p (a b c) -> p a b c", a=v.shape[1], b=v.shape[2])
            return base.rearrange("p (a b) -> p a b", a=v.shape[1])

        def bcast(ap, n):
            return bass.AP(ap.tensor, ap.offset, [list(d) for d in ap.ap] + [[0, n]])

        gcol = {}
        at = 0
        for name, n in (("a_norm", KD), ("b_norm", KD), ("kv_norm", KD), ("mem0", KD), ("mem1", KD), ("ffn0", KD),
                        ("ffn1", KD), ("head", avw // P), ("q_a", QL // P), ("kv_a", KVL // P),
                        ("memq0", 1), ("memk0", 1), ("memq1", 1), ("memk1", 1)):
            gcol[name] = at
            at += n
        assert at == NG

        TR = [
            ("mem", memS, 0, [(memT[:, 0], "mem0"), (memT[:, 1], "mem1")]),
            ("x0", xn, 4, [(xT, "a_norm")]),
            ("mix0", mix, 0, [(xT, "head")]),
            ("x1", xn, 0, [(xT, "ffn0")]),
            ("x2", xn, 0, [(xTk, "kv_norm"), (xT, "b_norm")]),
            ("mix1", mix, 0, [(xT, None)]),
            ("x3", xn, 0, [(xT, "ffn1")]),
        ]
        tidx = {t[0]: i for i, t in enumerate(TR)}

        def trans_gain(name, g, k):
            if g is None or (g == "head" and k >= avw // P):
                return None
            return gains[:, gcol[g] + k:gcol[g] + k + 1]

        block = ctx.enter_context(nc.Block())

        UNITS = [(kind, t, g) for kind in ("kv", "q") for t in range(NT) for g in range(BH // 2)]
        UNITS = [(kind, t, g, u % 8) for u, (kind, t, g) in enumerate(UNITS)]
        KQT = [(full[:, 2 * g:2 * g + 2, :], n, 0) for a, b in ((kTn, kTr), (qTn, qTr))
               for full, n in ((a, P), (b, ROPE)) for g in range(BH // 2)]
        KQT = [(dst, n, u % 8) for u, (dst, n, _) in enumerate(KQT)]
        PTB = [6, 7, 0, 1, 2]
        TURN_AT, COMBINE_AT = 1, 3

        def k_gain(name, g, k):
            if g is None or (g == "head" and k >= avw // P):
                return None
            return gains[:, gcol[g] + k:gcol[g] + k + 1]

        def through(name):
            return item[name] + 1

        @block.sync
        def _(sp):
            def fill(j, views):
                at = 0
                for view in views if isinstance(views, tuple) else (views,):
                    k, n = view.shape[1:]
                    sp.dma_start(ring[:, j, at:at + k * n].rearrange("p (k n) -> p k n", k=k), view).then_inc(S(f"slot_full{j}"), 16)
                    at += k * n

            sp.dma_start(memS, mem_d.rearrange("(t p) d -> p t d", p=P)).then_inc(S("mem_in"), 16)
            for n, (name, view) in enumerate(stream if STAGE >= 3 else stream[:item["dkv"]]):
                if n >= SLOTS:
                    sp.wait_ge(S("through"), n - SLOTS + 1)
                fill(slot_of(n), view)
            if STAGE >= 4:
                sp.wait_ge(S("routed"), 1)
                passes = sp.value_load(cnt_i[0:1, 0:1], min_val=1, max_val=PASSES)
                with sp.Fori(0, passes) as p:
                    with sp.Fori(0, NE) as e:
                        gu = T["moe_w_gate_up"][0][bass.ds(e, 1), :, :].rearrange("e d n -> (e d) n")
                        dn = T["moe_w_down"][0][bass.ds(e, 1), :, :].rearrange("e d n -> (e d) n")
                        for j in range(PER):
                            sp.wait_ge(S("through"), (p * NE + e) * PER + (NS + j - SLOTS + 1))
                            fill(j % SLOTS, gu_item(gu, j) if j < NGU else dn_item(dn, j - NGU))
            for t in range(NT):
                sp.wait_ge(S("x_final"), t + 1)
                sp.dma_start(out[0].rearrange("(t p) d -> p t d", p=P)[:, t], xres[:, t]).then_inc(S("stored"), 16)
            sp.wait_ge(S("stored"), 16 * NT)

        @block.gpsimd
        def _(pool):
            c = S("consts")
            pool.memset(ident[:, :], 0.0).then_inc(c, 1)
            pool.memset(ones[:, :], 1.0).then_inc(c, 1)
            pool.memset(nhalf[:, :], -0.5).then_inc(c, 1)
            pool.wait_ge(c, 3)
            pool.affine_select(out=ident[:, :], in_=ident[:, :], compare_op=ALU.not_equal, fill=1.0, base=0,
                               pattern=[[-1, P]], channel_multiplier=1).then_inc(S("ident"), 1)
            n = [0]

            def rstd_of(name):
                e, g = nidx[name], groups(name)
                pool.wait_ge(S("sums"), e + 1)
                pool.tensor_scalar(meansq[:, 0:g], sumsq[:, 0:g], EPS, None, ALU.add).then_inc(S("mean_eps"), 1)
                pool.wait_ge(S("mean_eps"), e + 1)
                pool.tensor_tensor(rstd[:, 0:g], meansq[:, 0:g], nhalf[:, 0:g], ALU.pow).then_inc(S("rstds"), 1)

            rstd_of("mem")
            rstd_of("x0")
            pool.memset(mask_kq[:, :], 0.0).then_inc(c, 1)
            pool.memset(mask_qk[:, :], 0.0).then_inc(c, 1)
            pool.memset(sel[:, :, :], 0.0).then_inc(c, 1)
            pool.wait_ge(c, 6)
            pool.affine_select(out=mask_kq[:, :], in_=mask_kq[:, :], compare_op=ALU.is_ge, fill=NEG, base=0,
                               pattern=[[1, P]], channel_multiplier=-1).then_inc(c, 1)
            pool.affine_select(out=mask_qk[:, :], in_=mask_qk[:, :], compare_op=ALU.is_ge, fill=NEG, base=0,
                               pattern=[[-1, P]], channel_multiplier=1).then_inc(c, 1)
            pool.affine_select(out=before[:, :], in_=ones[:, :], compare_op=ALU.is_gt, fill=0.0, base=0,
                               pattern=[[1, P]], channel_multiplier=-1).then_inc(c, 1)
            pool.affine_select(out=sel[:, :, :], in_=sel[:, :, :], compare_op=ALU.not_equal, fill=1.0, base=0,
                               pattern=[[-1, AH], [0, P]], channel_multiplier=1).then_inc(c, 1)
            rstd_of("mk0")
            rstd_of("mk1")
            rstd_of("mq0")
            inv = (1.0 / np.float32(ROPE_THETA) ** (np.arange(0, ROPE, 2, dtype=np.float32) / np.float32(ROPE))
                   ).astype(np.float32)
            for j in range(HR):
                last = pool.memset(invf[:, j:j + 1], float(inv[j]))
            last.then_inc(S("freqs"), 1)
            rstd_of("hm")
            rstd_of("x1")
            if STAGE < 3:
                return
            for name in ("x2", "ckv", "cq", "mq1", "kh", "qh"):
                rstd_of(name)
            if STAGE < 4:
                return
            rstd_of("x3")
            pool.iota(iotai, pattern=[[1, CAP]], base=0, channel_multiplier=0).then_inc(S("iota_i"), 1)
            pool.wait_ge(S("iota_i"), 1)
            pool.tensor_copy(iota, iotai).then_inc(S("iota"), 1)
            pool.memset(yT, 0.0).then_inc(S("yT_ready"), 1)
            pool.memset(G, 0.0).then_inc(S("G_ready"), 1)

        @block.scalar
        def _(act):
            G0 = gcol
            vec = [("a_norm", T["a_norm"][0]), ("b_norm", T["b_norm"][0]), ("kv_norm", T["kv_norm"]),
                   ("mem0", T["mem_norm"][0]), ("mem1", T["mem_norm"][1]), ("ffn0", T["ffn_norm"][0]),
                   ("ffn1", T["ffn_norm"][1]), ("head", T["a_head_norm"][0]), ("q_a", T["b_q_a_norm"][0]),
                   ("kv_a", T["kv_a_norm"])]
            act.dma_start(xres[:, :, :], x_d.rearrange("(t p) d -> p t d", p=P)).then_inc(S("x_in"), 16)
            for name, v in vec:
                k = v.shape[0] // P
                act.dma_start(grow[G0[name]:G0[name] + k, :], v.rearrange("(k p) -> k p", p=P)).then_inc(S("gain_in"), 16)
            for name, v in (("memq0", T["mem_q_norm"][0]), ("memk0", T["mem_k_norm"][0]),
                            ("memq1", T["mem_q_norm"][1]), ("memk1", T["mem_k_norm"][1])):
                for h in range(2):
                    act.dma_start(grow[G0[name]:G0[name] + 1, h * MD:(h + 1) * MD],
                                  v.rearrange("(a n) -> a n", a=1)).then_inc(S("gain_in"), 16)
            act.dma_start(hrow[:, 0:QKH], T["k_head_norm"].rearrange("(a n) -> a n", a=1)).then_inc(S("gain_in"), 16)
            act.dma_start(hrow[:, QKH:2 * QKH], T["b_q_head_norm"]).then_inc(S("gain_in"), 16)
            gb = T["a_gate_bias"].rearrange("a n -> n a")
            act.dma_start(bias_i[:, :], gb[0:AH]).then_inc(S("bias_in"), 16)
            act.dma_start(bias_f[:, :], gb[AH:2 * AH]).then_inc(S("bias_in"), 16)
            act.dma_start(posi[:, :], T["positions"][0].rearrange("(t p) -> p t", p=P),
                          allow_slow_non_contiguous=True).then_inc(S("pos_in"), 16)
            act.dma_start(router[:, :, :], rows(T["moe_router"][0])).then_inc(S("router_in"), 16)

            def square(name):
                e, (v, _, w) = nidx[name], nview[name]
                if e > 0:
                    act.wait_ge(S("sums"), e)
                nc.scalar.activation(sq_of(name), v, ACT.Square, scale=float(w) ** -0.5).then_inc(S("squares"), 1)

            def evict(name):
                i, (_, _, bank, dsts) = tidx[name], TR[tidx[name]]
                for b in (0, 2):
                    act.wait_ge(S("transposed"), 4 * i + b + 1)
                    for dst, g in dsts:
                        for k in (2 * b, 2 * b + 1):
                            s = k_gain(name, g, k)
                            last = nc.scalar.activation(dst[:, k, :], PS[:, bank + b, (k % 2) * SEQ:(k % 2 + 1) * SEQ], ACT.Copy,
                                                        scale=1.0 if s is None else s)
                    last.then_inc(S("evicted_even"), 1)

            def mem_softmax(l, bank):
                for t in range(NT):
                    for h in range(MH):
                        if t == 0 and h == 0:
                            act.wait_ge(S("mem_max"), l + 1)
                        c = t * MH + h
                        last = nc.scalar.activation(mP[:, t, h], PS[:, bank + 2 * t + h % 2, (h // 2) * 256:(h // 2 + 1) * 256],
                                                    ACT.Exp, bias=sbias[:, c:c + 1], scale=float(MD) ** -0.5,
                                                    accum_out=ssum[:, c:c + 1])
                last.then_inc(S("mem_exp"), 1)
                for b in range(2):
                    act.wait_ge(S("mem_pt"), 4 * l + 2 * b + 1)
                    nc.scalar.activation(mPT[:, b, 0:2].rearrange("p h m q -> p (h m q)"), PS[:, 2 * b, :],
                                         ACT.Copy).then_inc(S("mem_pt_even"), 1)

            act.wait_ge(S("mem_in"), 16)
            square("mem")
            act.wait_ge(S("x_in"), 16)
            square("x0")
            act.wait_ge(S("gains"), 2)
            evict("mem")
            evict("x0")
            for l in range(2):
                act.wait_ge(S("through"), through(f"memkv{l}"))
                act.wait_ge(S("transposed"), 4)
                nc.scalar.activation(kS[:, l], PS[:, 2 * l:2 * l + 2, 0:MW], ACT.Copy).then_inc(S("kS"), 1)
                nc.scalar.activation(memv[:, l], PS[:, 2 * l:2 * l + 2, MW:2 * MW], ACT.Copy).then_inc(S("memv"), 1)
            act.wait_ge(S("kS"), 2)
            square("mk0")
            square("mk1")
            act.wait_ge(S("through"), through("gmq"))
            act.wait_ge(S("bias_in"), 32)
            nc.scalar.activation(gi, PS[0:AH, 4, 0:SEQ], ACT.Identity, bias=bias_i[:, :]).then_inc(S("gate_in"), 1)
            nc.scalar.activation(gf, PS[0:AH, 4, SEQ:2 * SEQ], ACT.Identity, bias=bias_f[:, :]).then_inc(S("gate_in"), 1)
            nc.scalar.activation(mqS, PS[:, 5, :].rearrange("p (t n) -> p t n", t=NT), ACT.Copy).then_inc(S("mqS"), 1)
            act.wait_ge(S("gate_abs"), 1)
            nc.scalar.activation(gt, gt, ACT.Exp, scale=-1.0).then_inc(S("gate_exp"), 1)
            act.wait_ge(S("gate_exp"), 1)
            nc.scalar.activation(gt, gt, ACT.Ln, bias=1.0).then_inc(S("gate_exp"), 1)
            act.wait_ge(S("mqS"), 1)
            square("mq0")
            act.wait_ge(S("through"), through("q"))
            for b in range(2):
                last = nc.scalar.activation(qT[0:AQ, 2 * b:2 * b + 2, :], PS[0:AQ, 6 + b, :].rearrange("p (h s) -> p h s", h=2), ACT.Copy)
            last.then_inc(S("qT"), 1)
            for half in range(2):
                act.wait_ge(S("through"), through(f"o{half}"))
                for t in range(NT):
                    last = nc.scalar.activation(og[:, t, half * hv:(half + 1) * hv], PS[:, (6, 0)[half] + t, 0:hv], ACT.Sigmoid)
                last.then_inc(S("og"), 1)
            act.wait_ge(S("gate_m"), 1)
            nc.scalar.activation(gem, gm, ACT.Exp, scale=-1.0).then_inc(S("gate_em"), 1)
            act.wait_ge(S("gN"), 1)
            for h in range(AH):
                act.wait_ge(S("decay_arg"), h + 1)
                for s0, c0, c1 in ((0, 0, SEQ), (1, SEQ, SEQ + P)):
                    last = nc.scalar.activation(Dm[:, h, c0:c1], PS[:, h, c0:c1], ACT.Exp, bias=gN[:, 0, s0, h:h + 1])
                last.then_inc(S("decay"), 1)
            mem_softmax(0, 4)
            act.wait_ge(S("h_out"), 1)
            square("hm")
            evict("mix0")
            act.wait_ge(S("x_sum"), 1)
            square("x1")
            evict("x1")

            def dense_silu(rev, j, base):
                act.wait_ge(S("through"), base)
                for a in range(2):
                    last = nc.scalar.activation(silu[:, 2 * (j % 2) + a], PS[:, 2 * (j % 4) + a, 0:SEQ], ACT.Silu)
                last.then_inc(S("silu"), 1)

            with act.Fori(0, 2) as rev:
                for j in range(SLOTS):
                    act.wait_ge(S("h_ready"), rev * SLOTS + (j + (4 if j == 0 else 3)))
                    dense_silu(rev, j, rev * SLOTS + (item["gu0"] + j + 1))
            if STAGE < 3:
                return
            act.wait_ge(S("x_sum"), 2)
            square("x2")
            act.wait_ge(S("angles"), 1)
            nc.scalar.activation(rot[:, 4], rot[:, 2], ACT.Sin).then_inc(S("sincos"), 1)
            nc.scalar.activation(rot[:, 5], rot[:, 3], ACT.Sin).then_inc(S("sincos"), 1)
            evict("x2")
            act.wait_ge(S("through"), through("dkv"))
            nc.scalar.activation(zS, PS[:, 4:6, 0:KVL + ROPE], ACT.Copy).then_inc(S("zS"), 1)
            act.wait_ge(S("through"), through("cq"))
            nc.scalar.activation(cqS, PS[:, 6:8, 0:QL], ACT.Copy).then_inc(S("cqS"), 1)
            act.wait_ge(S("through"), through("mq"))
            nc.scalar.activation(mqS1, PS[:, 0, :].rearrange("p (t n) -> p t n", t=NT), ACT.Copy).then_inc(S("mqS"), 1)
            act.wait_ge(S("zS"), 1)
            square("ckv")
            act.wait_ge(S("cqS"), 1)
            square("cq")
            act.wait_ge(S("mqS"), 2)
            square("mq1")
            for u, (kind, t, g, bank) in enumerate(UNITS):
                if u % 6 == 5:
                    act.wait_ge(S("through"), through("ukv" if u == 5 else "uq"))
                else:
                    act.wait_ge(S("unit"), u + 1 - u // 6)
                if kind == "kv":
                    src = PS[:, bank, :].rearrange("p (h a n) -> p h a n", h=2, a=2)
                    kdst = kF.rearrange("p (t h) n -> p t h n", t=NT)[:, t, 2 * g:2 * g + 2, 0:NOPE]
                    nc.scalar.activation(kdst, src[:, :, 0], ACT.Copy)
                    last = nc.scalar.activation(vF[:, t, 2 * g:2 * g + 2], src[:, :, 1], ACT.Copy)
                else:
                    dst = qF.rearrange("p (t h) n -> p t h n", t=NT)[:, t, 2 * g:2 * g + 2]
                    last = nc.scalar.activation(dst, PS[:, bank, 0:2 * QKH].rearrange("p (h n) -> p h n", h=2), ACT.Copy)
                last.then_inc(S("unit_out"), 1)
                if u == 5:
                    act.wait_ge(S("unit_out"), 6)
                    act.wait_ge(S("k_rope_in"), 1)
                    square("kh")
            act.wait_ge(S("unit_out"), 12)
            square("qh")
            for u, (dst, rws, bank) in enumerate(KQT):
                if u % 2 == 0:
                    act.wait_ge(S("kq_t"), u + 1)
                    nc.scalar.activation(dst, PS[0:rws, bank, :].rearrange("p (h s) -> p h s", h=2), ACT.Copy).then_inc(S("kq_even"), 1)
            act.wait_ge(S("att_max"), 1)
            for h in range(BH):
                for t, (c0, c1) in enumerate(((0, P), (P, 3 * P))):
                    last = nc.scalar.activation(Pb[:, h, c0:c1], PS[:, h, c0:c1], ACT.Exp, bias=sbias[:, t * BH + h:t * BH + h + 1],
                                                scale=float(QKH) ** -0.5, accum_out=ssum[:, t * BH + h:t * BH + h + 1])
                last.then_inc(S("att_exp"), 1)
            for u, bank in enumerate(PTB):
                if u % 2 == 0:
                    act.wait_ge(S("att_pt"), u + 1)
                    n = min(512, BH * 384 - 512 * u)
                    nc.scalar.activation(PT.rearrange("p a b -> p (a b)")[:, 512 * u:512 * u + n], PS[:, bank, 0:n],
                                         ACT.Copy).then_inc(S("att_pt_even"), 1)
            mem_softmax(1, 4)
            evict("mix1")
            if STAGE < 4:
                return
            act.wait_ge(S("x_sum"), 3)
            square("x3")
            evict("x3")
            act.wait_ge(S("top2"), 1)
            nc.scalar.activation(gt2[:, 2:4], gt2[:, 0:2], ACT.Exp).then_inc(S("gate2_exp"), 1)
            act.wait_ge(S("routed"), 1)
            passes = act.value_load(cnt_i[0:1, 0:1], min_val=1, max_val=PASSES)

            def y_out(i):
                act.wait_ge(S("y_turned"), i + 1)
                nc.scalar.activation(y.rearrange("p (a b) -> p a b", a=2), PS[0:CAP, 4:6, :], ACT.Copy).then_inc(S("y_ready"), 1)

            with act.Fori(0, passes) as p:
                with act.Fori(0, NE) as e:
                    i = p * NE + e
                    for c in range(NGU):
                        act.wait_ge(S("through"), i * PER + (NS + c + 1))
                        if c >= 2:
                            act.wait_ge(S("e_ready"), i * NGU + (c - 1))
                        src = PS[:, c % 2, 0:4 * CAP].rearrange("p (a g n) -> p a g n", a=2, g=2)
                        nc.scalar.activation(esilu[:, c % 2], src[:, :, 0], ACT.Silu).then_inc(S("esilu"), 1)
                        if c == TURN_AT:
                            y_out(i)
                    act.wait_ge(S("through"), i * PER + (NS + PER))
                    nc.scalar.activation(yT.rearrange("p (a k) n -> p a (k n)", a=2), PS[:, 2:4, 0:4 * CAP],
                                         ACT.Copy).then_inc(S("yT_ready"), 1)
            y_out(passes * NE)

        @block.tensor
        def _(pe):
            mm = nc.tensor.matmul

            def tr(dst, src):
                return nc.tensor.transpose(dst, src, ident[0:src.shape[0], 0:src.shape[0]])

            def slot(name, *shape):
                n = item[name]
                pe.wait_ge(S(f"slot_full{slot_of(n)}"), filled(n))
                return view_of(slot_of(n), *shape)

            def view_of(j, *shape):
                v = ring[:, j, 0:int(np.prod(shape))]
                if len(shape) == 2:
                    return v.rearrange("p (k n) -> p k n", k=shape[0])
                return v.rearrange("p (g k n) -> p g k n", g=shape[0], k=shape[1])

            def transposes(name):
                _, src, bank, _ = TR[tidx[name]]
                for b in range(4):
                    for k in (2 * b, 2 * b + 1):
                        for t in range(NT):
                            last = tr(PS[:, bank + b, (k % 2) * SEQ + t * P:(k % 2) * SEQ + (t + 1) * P], src[:, t, k * P:(k + 1) * P])
                    last.then_inc(S("transposed"), 1)

            def evicted(name):
                i = tidx[name]
                pe.wait_ge(S("evicted_even"), 2 * (i + 1))
                pe.wait_ge(S("evicted_odd"), 2 * (i + 1))

            def natural(banks, src, w, n, nk=KD, c0=0):
                for t in range(NT):
                    bank, at = banks[t]
                    for k in range(nk):
                        last = mm(PS[:, bank, at:at + n], lhsT=src[:, k, t * P:(t + 1) * P], rhs=w[:, k, c0:c0 + n],
                                  start=(k == 0), stop=(k == nk - 1))
                return last

            def mem_attention(l, kT_, qT_, q_sem, q_val):
                pe.wait_ge(S(q_sem), q_val)
                pe.wait_ge(S("memkT"), 2)
                for par in range(2):
                    for t in range(NT):
                        for pair in range(2):
                            last = mm(PS[:, 4 + 2 * t + par, pair * 256:(pair + 1) * 256],
                                      lhsT=qT_[par * MD:(par + 1) * MD, pair, t * P:(t + 1) * P],
                                      rhs=kT_[par * MD:(par + 1) * MD, pair, :], start=True, stop=True)
                last.then_inc(S("mem_scores"), 1)

            def mem_attention_out(l):
                pe.wait_ge(S("mem_exp"), l + 1)
                for t in range(NT):
                    for hh in range(2):
                        for h in (2 * hh, 2 * hh + 1):
                            for m in range(2):
                                last = tr(PS[:, 2 * t + hh, ((h % 2) * 2 + m) * P:((h % 2) * 2 + m + 1) * P], mP[:, t, h, m * P:(m + 1) * P])
                        last.then_inc(S("mem_pt"), 1)
                pe.wait_ge(S("mem_pt_even"), 2 * (l + 1))
                pe.wait_ge(S("mem_pt_odd"), 2 * (l + 1))
                for t in range(NT):
                    for h in range(MH):
                        for m in range(2):
                            last = mm(PS[:, 4, (t * MH + h) * MD:(t * MH + h + 1) * MD], lhsT=mPT[:, t, h, m, :],
                                      rhs=memv[:, l, m, h * MD:(h + 1) * MD], start=(m == 0), stop=(m == 1))
                last.then_inc(S("mem_out"), 1)

            def project_out(names):
                for hh, name in enumerate(names):
                    w = slot(name, KD, HD)
                    natural([(4 + hh, 0), (6 + hh, 0)], xT, w, HD).then_inc(S("through"), 1)

            pe.wait_ge(S("ident"), 1)
            pe.wait_ge(S("gain_in"), 16 * 20)
            tr(PS[:, 7, 0:NG], grow)
            mm(PS[:, 6, 0:2 * QKH], lhsT=ones[0:1, :], rhs=hrow, start=True, stop=True).then_inc(S("gains_t"), 1)
            pe.wait_ge(S("scaled"), nidx["mem"] + 1)
            transposes("mem")
            pe.wait_ge(S("scaled"), nidx["x0"] + 1)
            pe.wait_ge(S("gains"), 2)
            transposes("x0")
            evicted("mem")
            for l in range(2):
                w = slot(f"memkv{l}", KD, 2 * MW)
                natural([(2 * l, 0), (2 * l + 1, 0)], memT[:, l], w, 2 * MW).then_inc(S("through"), 1)
            evicted("x0")
            w = slot("gmq", KD, 2 * AH + MW)
            for half in range(2):
                for k in range(KD):
                    mm(PS[0:AH, 4, half * SEQ:(half + 1) * SEQ], lhsT=w[:, k, half * AH:(half + 1) * AH], rhs=xT[:, k, :],
                       start=(k == 0), stop=(k == KD - 1))
            natural([(5, 0), (5, MW)], xT, w, MW, c0=2 * AH).then_inc(S("through"), 1)
            for name, bank in (("q", 6), ("k", 0)):
                if name == "k":
                    pe.wait_ge(S("memv"), 2)
                w = slot(name, KD, aqw)
                for h in range(AH):
                    for k in range(KD):
                        last = mm(PS[0:AQ, bank + h // 2, (h % 2) * SEQ:(h % 2 + 1) * SEQ], lhsT=w[:, k, h * AQ:(h + 1) * AQ],
                                  rhs=xT[:, k, :], start=(k == 0), stop=(k == KD - 1))
                last.then_inc(S("through"), 1)
            for name, banks in (("v0", (2, 3)), ("v1", (4, 5)), ("o0", (6, 7)), ("o1", (0, 1))):
                if name == "v1":
                    pe.wait_ge(S("mqS"), 1)
                if name == "o0":
                    pe.wait_ge(S("qT"), 1)
                if name == "o1":
                    pe.wait_ge(S("kT"), 1)
                w = slot(name, KD, hv)
                natural([(b, 0) for b in banks], xT, w, hv).then_inc(S("through"), 1)
            pe.wait_ge(S("v_out"), 2)
            for l in range(2):
                pe.wait_ge(S("scaled"), nidx[f"mk{l}"] + 1)
                for pair in range(2):
                    for t in range(NT):
                        last = tr(PS[:, 2 + l, pair * SEQ + t * P:pair * SEQ + (t + 1) * P], kS[:, l, t, pair * P:(pair + 1) * P])
                last.then_inc(S("memk_t"), 1)
            pe.wait_ge(S("scaled"), nidx["mq0"] + 1)
            for pair in range(2):
                for t in range(NT):
                    last = tr(PS[:, 4, pair * SEQ + t * P:pair * SEQ + (t + 1) * P], mqS[:, t, pair * P:(pair + 1) * P])
            last.then_inc(S("mq_t"), 1)
            pe.wait_ge(S("gate_em"), 1)
            for r, src in enumerate((ga, gem)):
                for t in range(NT):
                    c = (r * NT + t) * AH
                    last = tr(PS[:, 5, c:c + AH], src[:, t * P:(t + 1) * P])
            last.then_inc(S("gate_t"), 1)
            pe.wait_ge(S("og"), 2)
            pe.wait_ge(S("memkT"), 2)
            pe.wait_ge(S("gate_neg"), 1)
            pe.wait_ge(S("consts"), 10)
            for h in range(AH):
                mm(PS[:, h, 0:SEQ], lhsT=sel[:, h, :], rhs=gneg, start=True, stop=False, skip_group_check=True)
                mm(PS[:, h, SEQ:SEQ + P], lhsT=sel[:, h, :], rhs=gneg[:, P:SEQ], start=False, stop=False, skip_group_check=True)
                mm(PS[:, h, 0:P], lhsT=ident[:, :], rhs=mask_kq[:, :], start=False, stop=False, skip_group_check=True)
                mm(PS[:, h, SEQ:SEQ + P], lhsT=ident[:, :], rhs=mask_kq[:, :], start=False, stop=True,
                   skip_group_check=True).then_inc(S("decay_arg"), 1)
            pe.wait_ge(S("mqT"), 1)
            pe.wait_ge(S("gN"), 1)
            for h in range(AH):
                mm(PS[:, 4 + h, 0:SEQ], lhsT=kT[0:AQ, h, 0:P], rhs=qT[0:AQ, h, :], start=True, stop=True)
                mm(PS[:, 4 + h, SEQ:SEQ + P], lhsT=kT[0:AQ, h, P:SEQ], rhs=qT[0:AQ, h, P:SEQ], start=True,
                   stop=True).then_inc(S("kq"), 1)
            for h in range(AH):
                pe.wait_ge(S("weights"), h + 1)
                if h == 0:
                    pe.wait_ge(S("decay"), AH)
                mm(PS[:, h, 0:VW], lhsT=PmT[:, h, 0:P], rhs=v1[:, 0, h, :], start=True, stop=True)
                mm(PS[:, h, 256:256 + VW], lhsT=PmT[:, h, P:SEQ], rhs=v1[:, 0, h, :], start=True, stop=False)
                mm(PS[:, h, 256:256 + VW], lhsT=PmT[:, h, SEQ:SEQ + P], rhs=v1[:, 1, h, :], start=False,
                   stop=True).then_inc(S("num"), 1)
            mem_attention(0, memkT[:, 0], mqT, "mqT", 1)
            pe.wait_ge(S("h_out"), 1)
            mem_attention_out(0)
            pe.wait_ge(S("mixed"), 1)
            transposes("mix0")
            evicted("mix0")
            project_out(("aout0", "aout1"))
            pe.wait_ge(S("scaled"), nidx["x1"] + 1)
            transposes("x1")
            evicted("x1")
            with pe.Fori(0, 2) as rev:
                for j in range(SLOTS):
                    n = item["gu0"] + j
                    pe.wait_ge(S(f"slot_full{slot_of(n)}"), rev * 32 + filled(n))
                    pe.wait_ge(S("h_ready"), rev * SLOTS + (j + 2))
                    w = view_of(slot_of(n), 2, KD, FC)
                    for a in range(2):
                        for g in range(2):
                            for k in range(KD):
                                last = mm(PS[:, 2 * (j % 4) + a, g * SEQ:(g + 1) * SEQ], lhsT=w[:, g, k, a * P:(a + 1) * P],
                                          rhs=xT[:, k, :], start=(k == 0), stop=(k == KD - 1))
                    last.then_inc(S("through"), 1)
            pe.wait_ge(S("h_ready"), NGU + 4)
            for c in range(NDN):
                w = slot(f"dn{c}", KDN, D)
                for kk in range(KDN):
                    kf = c * KDN + kk
                    for t in range(NT):
                        for hh in range(2):
                            last = mm(PS[:, 4 + 2 * t + hh, :], lhsT=hT[:, kf, t * P:(t + 1) * P], rhs=w[:, kk, hh * HD:(hh + 1) * HD],
                                      start=(kf == 0), stop=(kf == KF - 1))
                last.then_inc(S("through"), 1)
            if STAGE < 3:
                return
            pe.wait_ge(S("scaled"), nidx["x2"] + 1)
            transposes("x2")
            evicted("x2")
            w = slot("dkv", KD, KVL + ROPE)
            natural([(4, 0), (5, 0)], xTk, w, KVL + ROPE).then_inc(S("through"), 1)
            w = slot("cq", KD, QL)
            natural([(6, 0), (7, 0)], xT, w, QL).then_inc(S("through"), 1)
            w = slot("mq", KD, MW)
            natural([(0, 0), (0, MW)], xT, w, MW).then_inc(S("through"), 1)
            pe.wait_ge(S("scaled"), nidx["ckv"] + 1)
            for k in range(2):
                for t in range(NT):
                    last = tr(PS[:, 1, k * SEQ + t * P:k * SEQ + (t + 1) * P], zS[:, t, k * P:(k + 1) * P])
            last.then_inc(S("lat_t"), 1)
            pe.wait_ge(S("scaled"), nidx["cq"] + 1)
            for k in range(3):
                for t in range(NT):
                    last = tr(PS[:, 2 + k // 2, (k % 2) * SEQ + t * P:(k % 2) * SEQ + (t + 1) * P], cqS[:, t, k * P:(k + 1) * P])
            last.then_inc(S("lat_t"), 1)
            pe.wait_ge(S("scaled"), nidx["mq1"] + 1)
            for pair in range(2):
                for t in range(NT):
                    last = tr(PS[:, 4, pair * SEQ + t * P:pair * SEQ + (t + 1) * P], mqS1[:, t, pair * P:(pair + 1) * P])
            last.then_inc(S("lat_t"), 1)
            pe.wait_ge(S("lat_out"), 3)
            for u, (kind, t, g, bank) in enumerate(UNITS):
                if u == 0:
                    w = slot("ukv", 2, BH * (NOPE + VH))
                if u == 6:
                    w = slot("uq", 3, BH * QKH)
                if u >= 8:
                    pe.wait_ge(S("unit_out"), u - 8 + 1)
                src, nk, n = (ckvT, 2, 2 * (NOPE + VH)) if kind == "kv" else (cqT, 3, 2 * QKH)
                for k in range(nk):
                    last = mm(PS[:, bank, 0:n], lhsT=src[:, k, t * P:(t + 1) * P], rhs=w[:, k, g * n:(g + 1) * n],
                              start=(k == 0), stop=(k == nk - 1))
                last.then_inc(S("through") if u % 6 == 5 else S("unit"), 1)
            for u, (dst, rws, bank) in enumerate(KQT):
                who, part = ("k", u) if u < 6 else ("q", u - 6)
                if part == 0:
                    pe.wait_ge(S("roped"), 1 if who == "k" else 2)
                if u == 0:
                    pe.wait_ge(S("unit_out"), 12)
                if u >= 8:
                    pe.wait_ge(S("kq_even" if u % 2 == 0 else "kq_odd"), (u - 8) // 2 + 1)
                src = (kF if who == "k" else qF).rearrange("p (t h) n -> p t h n", t=NT)
                for h in (2 * (part % 3), 2 * (part % 3) + 1):
                    for t in range(NT):
                        v = src[:, t, h, 0:NOPE] if part < 3 else src[:, t, h, NOPE:QKH]
                        last = tr(PS[0:rws, bank, (h % 2) * SEQ + t * P:(h % 2) * SEQ + (t + 1) * P], v)
                last.then_inc(S("kq_t"), 1)
            pe.wait_ge(S("kq_even"), 6)
            pe.wait_ge(S("kq_odd"), 6)
            for h in range(BH):
                for t, (c0, c1) in enumerate(((0, P), (P, 3 * P))):
                    nk = (t + 1) * P
                    mm(PS[:, h, c0:c1], lhsT=qTn[:, h, t * P:(t + 1) * P], rhs=kTn[:, h, 0:nk], start=True, stop=False)
                    mm(PS[:, h, c1 - P:c1], lhsT=ident[:, :], rhs=mask_qk[:, :], start=False, stop=False)
                    last = mm(PS[:, h, c0:c1], lhsT=qTr[:, h, t * P:(t + 1) * P], rhs=kTr[:, h, 0:nk], start=False, stop=True)
                last.then_inc(S("att_scores"), 1)
            for u, bank in enumerate(PTB):
                for f in range(4 * u, min(4 * u + 4, 3 * BH)):
                    h, b = f // 3, f % 3
                    if b == 0 or f == 4 * u:
                        pe.wait_ge(S("att_exp"), BH if u >= 2 else h + 1)
                    last = tr(PS[:, bank, (f % 4) * P:(f % 4 + 1) * P], Pb[:, h, b * P:(b + 1) * P])
                last.then_inc(S("att_pt"), 1)
            pe.wait_ge(S("att_pt_even"), 3)
            pe.wait_ge(S("att_pt_odd"), 2)
            for t in range(NT):
                for h in range(BH):
                    c = t * BH + h
                    for m in range(t + 1):
                        last = mm(PS[:, 3 + c // 4, (c % 4) * VH:(c % 4 + 1) * VH], lhsT=PT[:, h, (t + m) * P:(t + m + 1) * P],
                                  rhs=vF[:, m, h, :], start=(m == 0), stop=(m == t))
            last.then_inc(S("att_out"), 1)
            pe.wait_ge(S("att_mixed"), 1)
            mem_attention(1, memkT[:, 1], mqT1, "lat_out", 3)
            mem_attention_out(1)
            pe.wait_ge(S("mixed"), 2)
            transposes("mix1")
            evicted("mix1")
            project_out(("bout0", "bout1"))
            if STAGE < 4:
                return
            pe.wait_ge(S("scaled"), nidx["x3"] + 1)
            transposes("x3")
            evicted("x3")
            pe.wait_ge(S("router_in"), 16)
            natural([(4, 0), (4, NE)], xT, router, NE).then_inc(S("logits"), 1)
            pe.wait_ge(S("chosen"), 1)
            mm(PS[:, 5, 0:NE], lhsT=before[:, :], rhs=chosen[:, 0], start=True, stop=True)
            mm(PS[:, 5, NE:2 * NE], lhsT=ones[:, :], rhs=chosen[:, 0], start=True, stop=False)
            mm(PS[:, 5, NE:2 * NE], lhsT=before[:, :], rhs=chosen[:, 1], start=False, stop=True)
            mm(PS[:, 5, 2 * NE:3 * NE], lhsT=ones[:, :], rhs=chosen[:, 0], start=True, stop=False)
            mm(PS[:, 5, 2 * NE:3 * NE], lhsT=ones[:, :], rhs=chosen[:, 1], start=False, stop=True).then_inc(S("ranks"), 1)

            def gather(last_sem="gathered"):
                for k in range(KD):
                    for t in range(NT):
                        last = mm(PS[:, 6 + k // 4, (k % 4) * CAP:(k % 4 + 1) * CAP], lhsT=xn[:, t, k * P:(k + 1) * P],
                                  rhs=Sx[:, t, :], start=(t == 0), stop=(t == NT - 1))
                last.then_inc(S("gathered"), 1)

            def turn(i):
                pe.wait_ge(S("yT_ready"), i + 1)
                pe.wait_ge(S("G_ready"), i + 1)
                for m in range(KD):
                    last = tr(PS[0:CAP, 4 + m // 4, (m % 4) * P:(m % 4 + 1) * P], yT[:, m, :])
                last.then_inc(S("y_turned"), 1)

            def combine(i):
                pe.wait_ge(S("y_ready"), i + 1)
                for t in range(NT):
                    for hh in range(2):
                        last = mm(PS[:, (6, 4)[t] + hh, :], lhsT=G[:, t, :], rhs=y[:, hh * HD:(hh + 1) * HD], start=True, stop=True)
                    last.then_inc(S("combined"), 1)

            pe.wait_ge(S("routed"), 1)
            passes = pe.value_load(cnt_i[0:1, 0:1], min_val=1, max_val=PASSES)
            pe.wait_ge(S("dispatch"), 1)
            gather()
            with pe.Fori(0, passes) as p:
                with pe.Fori(0, NE) as e:
                    i = p * NE + e
                    pe.wait_ge(S("xe_ready"), i + 1)
                    for c in range(NGU):
                        j = c % SLOTS
                        pe.wait_ge(S(f"slot_full{j}"), i * EXPERT_FILLS + (BASE_FILLS[j] + 32 * (c // SLOTS + 1)))
                        if c >= 2:
                            pe.wait_ge(S("e_ready"), i * NGU + (c - 1))
                        w = view_of(j, 2, KD, FC)
                        for a in range(2):
                            for g in range(2):
                                at = (2 * a + g) * CAP
                                for k in range(KD):
                                    last = mm(PS[:, c % 2, at:at + CAP], lhsT=w[:, g, k, a * P:(a + 1) * P], rhs=xe[:, k, :],
                                              start=(k == 0), stop=(k == KD - 1))
                        last.then_inc(S("through"), 1)
                        if c == TURN_AT:
                            turn(i)
                        if c == COMBINE_AT:
                            combine(i)
                    pe.wait_ge(S("dispatch"), i + 2)
                    pe.wait_ge(S("added"), i * NT + NT)
                    gather()
                    for t in range(NT):
                        last = tr(PS[0:CAP, 4, t * P:(t + 1) * P], Sw[:, t, :])
                    last.then_inc(S("G_turned"), 1)
                    for c in range(NDN):
                        pe.wait_ge(S(f"slot_full{c}"), (i + 1) * EXPERT_FILLS + BASE_FILLS[c])
                        if c == 0:
                            pe.wait_ge(S("e_ready"), i * NGU + NGU)
                        w = view_of(c, KDN, D)
                        for m in range(KD):
                            for kk in range(KDN):
                                last = mm(PS[:, 2 + m // 4, (m % 4) * CAP:(m % 4 + 1) * CAP], lhsT=w[:, kk, m * P:(m + 1) * P],
                                          rhs=eT[:, c * KDN + kk, :], start=(c == 0 and kk == 0 and m % 4 == 0),
                                          stop=(c == NDN - 1 and kk == KDN - 1), skip_group_check=True)
                        last.then_inc(S("through"), 1)
            pe.wait_ge(S("xe_ready"), passes * NE + 1)
            turn(passes * NE)
            combine(passes * NE)

        @block.vector
        def _(dve):
            v = nc.vector
            chain = [0]

            def then(ins):
                chain[0] += 1
                ins.then_inc(S("dve_step"), 1)
                dve.wait_ge(S("dve_step"), chain[0])

            def norm(name, gain=None):
                e, (src, dst, w), g = nidx[name], nview[name], groups(name)
                dst = src if dst is None else dst
                dve.wait_ge(S("squares"), e + 1)
                v.tensor_reduce(shaped(sumsq, name), sq_of(name), AX.X, ALU.add).then_inc(S("sums"), 1)
                dve.wait_ge(S("rstds"), e + 1)
                if gain is not None:
                    for k in range(g):
                        last = v.scalar_tensor_tensor(out=dst[:, k], in0=src[:, k], scalar=rstd[:, k:k + 1], in1=gain,
                                                      op0=ALU.mult, op1=ALU.mult)
                elif w == D:
                    for t in range(NT):
                        last = v.tensor_scalar(dst[:, t], src[:, t], rstd[:, t:t + 1], None, ALU.mult)
                else:
                    last = v.tensor_tensor(dst, src, bcast(shaped(rstd, name), w), ALU.mult)
                last.then_inc(S("scaled"), 1)

            def evict(name):
                i, (_, _, bank, dsts) = tidx[name], TR[tidx[name]]
                for b in (1, 3):
                    dve.wait_ge(S("transposed"), 4 * i + b + 1)
                    for dst, g in dsts:
                        for k in (2 * b, 2 * b + 1):
                            s, src = k_gain(name, g, k), PS[:, bank + b, (k % 2) * SEQ:(k % 2 + 1) * SEQ]
                            if s is None:
                                last = v.tensor_copy(dst[:, k, :], src)
                            else:
                                last = v.tensor_scalar(dst[:, k, :], src, s, None, ALU.mult)
                    last.then_inc(S("evicted_odd"), 1)

            def mem_max(l, bank):
                dve.wait_ge(S("mem_scores"), l + 1)
                for t in range(NT):
                    src = PS[:, bank + 2 * t:bank + 2 * t + 2, :].rearrange("p par (pair m) -> p pair par m", pair=2)
                    last = v.tensor_reduce(smax[:, t * MH:(t + 1) * MH].rearrange("p (a b) -> p a b", a=2), src, AX.X, ALU.max)
                then(last)
                v.tensor_scalar(sbias[:, 0:8], smax[:, 0:8], -float(MD) ** -0.5, None, ALU.mult).then_inc(S("mem_max"), 1)

            def mem_turned(l):
                for b in range(2):
                    dve.wait_ge(S("mem_pt"), 4 * l + 2 * b + 2)
                    v.tensor_copy(mPT[:, b, 2:4].rearrange("p h m q -> p (h m q)"), PS[:, 2 * b + 1, :]).then_inc(S("mem_pt_odd"), 1)

            def mem_out(l):
                dve.wait_ge(S("mem_exp"), l + 1)
                then(v.reciprocal(srec[:, 0:8], ssum[:, 0:8]))
                dve.wait_ge(S("mem_out"), l + 1)
                v.tensor_tensor(nat(mix[:, :, D - MW:D], MD), PS[:, 4, :].rearrange("p (t h n) -> p t h n", t=NT, h=MH),
                                bcast(srec[:, 0:8].rearrange("p (a b) -> p a b", a=NT), MD), ALU.mult).then_inc(S("mixed"), 1)

            def add_out(n):
                dve.wait_ge(S("through"), n)
                last = v.tensor_tensor(xres[:, :, :].rearrange("p t (a b) -> p (t a) b", a=2), PS[:, 4:8, :],
                                       xres[:, :, :].rearrange("p t (a b) -> p (t a) b", a=2), ALU.add)
                last.then_inc(S("x_sum"), 1)

            norm("mem")
            norm("x0")
            dve.wait_ge(S("gains_t"), 1)
            v.tensor_copy(gains[:, :], PS[:, 7, 0:NG]).then_inc(S("gains"), 1)
            v.tensor_copy(hg[:, :], PS[:, 6, 0:2 * QKH]).then_inc(S("gains"), 1)
            dve.wait_ge(S("gains"), 2)
            evict("mem")
            evict("x0")
            dve.wait_ge(S("kS"), 2)
            norm("mk0")
            norm("mk1")
            dve.wait_ge(S("gate_in"), 2)
            v.scalar_tensor_tensor(out=gt, in0=gf, scalar=-1.0, in1=gf, op0=ALU.mult, op1=ALU.max).then_inc(S("gate_abs"), 1)
            v.memset(gone, 1.0)
            then(v.tensor_scalar(gf, gf, 0.0, None, ALU.min))
            dve.wait_ge(S("gate_exp"), 2)
            then(v.tensor_tensor(glf, gf, gt, ALU.subtract))
            then(v.tensor_tensor_scan(gG, gone, glf, 0.0, ALU.mult, ALU.add))
            then(v.tensor_tensor(ga, gi, gG, ALU.subtract))
            then(v.tensor_tensor_scan(gM, ga, ga, 0.0, ALU.max, ALU.max))
            v.tensor_tensor(gm, gG, gM, ALU.add).then_inc(S("gate_m"), 1)
            v.tensor_scalar(gneg, gM, -1.0, None, ALU.mult).then_inc(S("gate_neg"), 1)
            norm("mq0")
            dve.wait_ge(S("through"), through("k"))
            for b in range(2):
                last = v.tensor_scalar(kT[0:AQ, 2 * b:2 * b + 2, :], PS[0:AQ, b, :].rearrange("p (h s) -> p h s", h=2),
                                       float(AQ) ** -0.5, None, ALU.mult)
            last.then_inc(S("kT"), 1)
            v.memset(v1[:, :, :, AV:VW], 1.0)
            for half in range(2):
                dve.wait_ge(S("through"), through(f"v{half}"))
                for t in range(NT):
                    last = v.tensor_copy(v1[:, t, 2 * half:2 * half + 2, 0:AV],
                                         PS[:, 2 + 2 * half + t, 0:hv].rearrange("p (h n) -> p h n", h=2))
                last.then_inc(S("v_out"), 1)
            for l in range(2):
                dve.wait_ge(S("memk_t"), l + 1)
                g = gcol[f"memk{l}"]
                v.tensor_scalar(memkT[:, l], PS[:, 2 + l, :].rearrange("p (a s) -> p a s", a=2), gains[:, g:g + 1], None,
                                ALU.mult).then_inc(S("memkT"), 1)
            dve.wait_ge(S("mq_t"), 1)
            g = gcol["memq0"]
            v.tensor_scalar(mqT, PS[:, 4, :].rearrange("p (a s) -> p a s", a=2), gains[:, g:g + 1], None,
                            ALU.mult).then_inc(S("mqT"), 1)
            dve.wait_ge(S("gate_t"), 1)
            v.tensor_copy(gN[:, :, :, :].rearrange("p a b c -> p (a b c)"), PS[:, 5, 0:2 * NT * AH]).then_inc(S("gN"), 1)
            dve.wait_ge(S("scaled"), nidx["mq0"] + 1)
            for h in range(AH):
                dve.wait_ge(S("decay"), h + 1)
                dve.wait_ge(S("kq"), h + 1)
                v.tensor_tensor(PmT[:, h, :], PS[:, 4 + h, 0:384], Dm[:, h, :], ALU.mult).then_inc(S("weights"), 1)
            dve.wait_ge(S("num"), AH)
            dv = den[:, :].rearrange("p (t h) -> p t h", t=NT)
            src = PS[:, 0:AH, :].rearrange("p h (t n) -> p t h n", t=NT)
            then(v.tensor_copy(dv, src[:, :, :, AV]))
            then(v.scalar_tensor_tensor(out=dv, in0=dv, scalar=-1.0, in1=dv, op0=ALU.mult, op1=ALU.max))
            then(v.tensor_tensor(dv, dv, gN[:, 1], ALU.max))
            then(v.reciprocal(den[:, :], den[:, :]))
            hview = nat(mix[:, :, 0:avw], AV)
            for t in range(NT):
                last = v.tensor_tensor(hview[:, t], src[:, t, :, 0:AV], bcast(dv[:, t], AV), ALU.mult)
            last.then_inc(S("h_out"), 1)
            mem_max(0, 4)
            mem_turned(0)
            norm("hm")
            dve.wait_ge(S("scaled"), nidx["hm"] + 1)
            dve.wait_ge(S("og"), 2)
            v.tensor_tensor(mix[:, :, 0:avw], mix[:, :, 0:avw], og, ALU.mult)
            mem_out(0)
            evict("mix0")
            add_out(through("aout1"))
            dve.wait_ge(S("x_sum"), 1)
            norm("x1")
            evict("x1")
            TWO_PI = 2.0 * np.pi
            part, left = [], TWO_PI
            for n in range(3):
                step = 2.0 ** (np.floor(np.log2(left)) - 7)
                part.append(float(np.floor(left / step) * step))
                left -= part[-1]
            part.append(float(np.float32(left)))
            HALF_TURN = 3.1415925
            dve.wait_ge(S("pos_in"), 16)
            dve.wait_ge(S("freqs"), 1)
            then(v.tensor_copy(posf[:, :], posi[:, :]))
            for t in range(NT):
                last = v.tensor_scalar(rot[:, 0, t], invf[:, :], posf[:, t:t + 1], None, ALU.mult)
            then(last)
            then(v.tensor_scalar(roti[:, :, :], rot[:, 0], float(1.0 / TWO_PI), None, ALU.mult))
            then(v.tensor_copy(rot[:, 1], roti[:, :, :]))
            for c in part:
                then(v.scalar_tensor_tensor(out=rot[:, 0], in0=rot[:, 1], scalar=-c, in1=rot[:, 0], op0=ALU.mult, op1=ALU.add))
            v.tensor_scalar(rot[:, 2], rot[:, 0], HALF_TURN, -HALF_TURN, ALU.min, ALU.max)
            then(v.tensor_scalar(rot[:, 3], rot[:, 0], float(np.pi / 2), None, ALU.add))
            then(v.tensor_scalar(rot[:, 1], rot[:, 3], float(np.pi), -TWO_PI, ALU.is_gt, ALU.mult))
            then(v.tensor_tensor(rot[:, 3], rot[:, 3], rot[:, 1], ALU.add))
            v.tensor_scalar(rot[:, 3], rot[:, 3], HALF_TURN, -HALF_TURN, ALU.min, ALU.max).then_inc(S("angles"), 1)
            v.memset(den[:, 0:1], 0.0).then_inc(S("h_ready"), 4)
            with dve.Fori(0, 2) as rev:
                for j in range(SLOTS):
                    dve.wait_ge(S("silu"), rev * SLOTS + (j + 1))
                    v.tensor_tensor(hT[:, bass.ds(rev * (2 * SLOTS) + 2 * j, 2), :], PS[:, 2 * (j % 4):2 * (j % 4) + 2, SEQ:2 * SEQ],
                                    silu[:, 2 * (j % 2):2 * (j % 2) + 2, :], ALU.mult).then_inc(S("h_ready"), 1)
            add_out(through(f"dn{NDN - 1}"))

            def debug_end():
                dve.wait_ge(S("router_in"), 16)
                for t in range(NT):
                    v.memset(den[:, t:t + 1], 0.0).then_inc(S("x_final"), 1)

            if STAGE < 3:
                debug_end()
                return
            dve.wait_ge(S("x_sum"), 2)
            norm("x2")
            evict("x2")
            dve.wait_ge(S("zS"), 1)
            kF4 = kF.rearrange("p (t h) n -> p t h n", t=NT)
            qF4 = qF.rearrange("p (t h) n -> p t h n", t=NT)

            def per_head(ap, n):
                dims = [list(d) for d in ap.ap]
                return bass.AP(ap.tensor, ap.offset, dims[:-1] + [[0, n]] + dims[-1:])

            for t in range(NT):
                last = v.tensor_copy(kF4[:, t, :, NOPE:QKH], per_head(zS[:, t, KVL:KVL + ROPE], BH))
            last.then_inc(S("k_rope_in"), 1)
            norm("ckv")
            norm("cq")
            norm("mq1")
            for n, (dst, name, view, nk) in enumerate((
                    (ckvT, "kv_a", PS[:, 1:2, :], 2), (cqT, "q_a", PS[:, 2:4, :], 3), (mqT1, "memq1", PS[:, 4:5, :], 2))):
                dve.wait_ge(S("lat_t"), n + 1)
                for k in range(nk):
                    g = gcol[name] + (k if n < 2 else 0)
                    last = v.tensor_scalar(dst[:, k], view[:, k // 2, (k % 2) * SEQ:(k % 2 + 1) * SEQ], gains[:, g:g + 1], None, ALU.mult)
                last.then_inc(S("lat_out"), 1)
            dve.wait_ge(S("sincos"), 2)
            sin, cos = rot[:, 4], rot[:, 5]
            tmp = xT[:, :, :].rearrange("p a b -> p (a b)")[:, 0:4 * NT * BH * HR].rearrange(
                "p (q t h n) -> p q t h n", q=4, t=NT, h=BH)
            for name, full, g0 in (("kh", kF4, 0), ("qh", qF4, QKH)):
                norm(name, hg[:, g0:g0 + QKH])
                dve.wait_ge(S("scaled"), nidx[name] + 1)
                x1, x2 = full[:, :, :, NOPE:NOPE + HR], full[:, :, :, NOPE + HR:QKH]
                for q, (a, b) in enumerate(((x1, cos), (x2, sin), (x2, cos), (x1, sin))):
                    last = v.tensor_tensor(tmp[:, q], a, per_head(b, BH), ALU.mult)
                then(last)
                v.tensor_tensor(x1, tmp[:, 0], tmp[:, 1], ALU.subtract)
                v.tensor_tensor(x2, tmp[:, 2], tmp[:, 3], ALU.add).then_inc(S("roped"), 1)
            for u, (dst, n, bank) in enumerate(KQT):
                if u % 2 == 1:
                    dve.wait_ge(S("kq_t"), u + 1)
                    v.tensor_copy(dst, PS[0:n, bank, :].rearrange("p (h s) -> p h s", h=2)).then_inc(S("kq_odd"), 1)
            dve.wait_ge(S("att_scores"), BH)
            v.tensor_reduce(smax[:, 0:BH], PS[:, 0:BH, 0:P], AX.X, ALU.max)
            then(v.tensor_reduce(smax[:, BH:2 * BH], PS[:, 0:BH, P:3 * P], AX.X, ALU.max))
            v.tensor_scalar(sbias[:, 0:2 * BH], smax[:, 0:2 * BH], -float(QKH) ** -0.5, None, ALU.mult).then_inc(S("att_max"), 1)
            for u, bank in enumerate(PTB):
                if u % 2 == 1:
                    dve.wait_ge(S("att_pt"), u + 1)
                    v.tensor_copy(PT.rearrange("p a b -> p (a b)")[:, 512 * u:512 * u + 512], PS[:, bank, :]).then_inc(S("att_pt_odd"), 1)
            dve.wait_ge(S("att_exp"), BH)
            then(v.reciprocal(srec[:, 0:2 * BH], ssum[:, 0:2 * BH]))
            dve.wait_ge(S("att_out"), 1)
            for t in range(NT):
                blocks = PS[:, 3:6, :].rearrange("p a b -> p (a b)")[:, t * BH * VH:(t + 1) * BH * VH]
                last = v.tensor_tensor(mix[:, t, 0:BH * VH].rearrange("p (h n) -> p h n", h=BH),
                                       blocks.rearrange("p (h n) -> p h n", h=BH), bcast(srec[:, t * BH:(t + 1) * BH], VH), ALU.mult)
            last.then_inc(S("att_mixed"), 1)
            mem_max(1, 4)
            mem_turned(1)
            mem_out(1)
            evict("mix1")
            add_out(through("bout1"))
            if STAGE < 4:
                debug_end()
                return
            dve.wait_ge(S("x_sum"), 3)
            norm("x3")
            evict("x3")
            dve.wait_ge(S("logits"), 1)
            dve.wait_ge(S("iota"), 1)
            then(v.tensor_copy(lg, PS[:, 4, 0:NT * NE].rearrange("p (t n) -> p t n", t=NT)))
            for t in range(NT):
                last = v.max(m8[:, t], lg[:, t])
            then(last)
            for t in range(NT):
                v.tensor_tensor(gt2[:, t:t + 1], m8[:, t, 1:2], m8[:, t, 0:1], ALU.subtract)
                last = v.max_index(idx8[:, t], m8[:, t], lg[:, t])
            last.then_inc(S("top2"), 1)
            dve.wait_ge(S("top2"), 1)
            then(v.tensor_copy(idxf, idx8))
            for t in range(NT):
                v.tensor_scalar(oh1[:, t], iota[:, 0:NE], idxf[:, t, 0:1], None, ALU.is_equal)
                last = v.tensor_scalar(oh2[:, t], iota[:, 0:NE], idxf[:, t, 1:2], None, ALU.is_equal)
            then(last)
            v.tensor_tensor(chosen, oh1, oh2, ALU.add).then_inc(S("chosen"), 1)
            dve.wait_ge(S("gate2_exp"), 1)
            then(v.tensor_scalar(gt2[:, 4:6], gt2[:, 2:4], 1.0, None, ALU.add))
            then(v.reciprocal(gt2[:, 6:8], gt2[:, 4:6]))
            then(v.tensor_tensor(gt2[:, 8:10], gt2[:, 6:8], gt2[:, 2:4], ALU.mult))
            for t in range(NT):
                last = v.tensor_scalar(oh1[:, t], oh1[:, t], gt2[:, 6 + t:7 + t], None, ALU.mult)
            then(last)
            for t in range(NT):
                for q in range(PASSES + 1):
                    last = v.scalar_tensor_tensor(out=combs[:, t, q * NE:(q + 1) * NE], in0=oh2[:, t], scalar=gt2[:, 8 + t:9 + t],
                                                  in1=oh1[:, t], op0=ALU.mult, op1=ALU.add)
            dve.wait_ge(S("chosen"), 1)
            dve.wait_ge(S("ranks"), 1)
            then(v.scalar_tensor_tensor(out=keys[:, :, 0:NE], in0=PS[:, 5, 0:NT * NE].rearrange("p (t n) -> p t n", t=NT),
                                        scalar=4096.0, in1=chosen, op0=ALU.add, op1=ALU.mult))
            then(v.tensor_scalar(keys[:, :, 0:NE], keys[:, :, 0:NE], -4096.0, None, ALU.add))
            for q in range(1, PASSES + 1):
                last = v.tensor_scalar(keys[:, :, q * NE:(q + 1) * NE], keys[:, :, 0:NE], -float(q * CAP), None, ALU.add)
            then(last)
            then(v.tensor_reduce(gt2[:, 10:11], PS[:, 5, 2 * NE:3 * NE], AX.X, ALU.max))
            then(v.tensor_scalar(gt2[:, 11:12], gt2[:, 10:11], float(CAP), 1.0, ALU.is_gt, ALU.add))
            for q in range(2, PASSES):
                then(v.scalar_tensor_tensor(out=gt2[:, 11:12], in0=gt2[:, 10:11], scalar=float(q * CAP), in1=gt2[:, 11:12],
                                            op0=ALU.is_gt, op1=ALU.add))
            v.tensor_copy(cnt_i[:, :], gt2[:, 11:12]).then_inc(S("routed"), 1)
            for t in range(NT):
                last = v.tensor_scalar(Sx[:, t], iota, keys[:, t, 0:1], None, ALU.is_equal)
            last.then_inc(S("dispatch"), 1)
            dve.wait_ge(S("routed"), 1)
            passes = dve.value_load(cnt_i[0:1, 0:1], min_val=1, max_val=PASSES)

            def gathered(i):
                dve.wait_ge(S("gathered"), i + 1)
                for b in range(2):
                    g = gcol["ffn1"] + 4 * b
                    last = v.tensor_tensor(xe[:, 4 * b:4 * b + 4, :], PS[:, 6 + b, 0:4 * CAP].rearrange("p (k n) -> p k n", k=4),
                                           bcast(gains[:, g:g + 4], CAP), ALU.mult)
                last.then_inc(S("xe_ready"), 1)

            def add(i, sem):
                for t in range(NT):
                    dve.wait_ge(S("combined"), i * NT + (t + 1))
                    xv = xres[:, t].rearrange("p (a b) -> p a b", a=2)
                    v.tensor_tensor(xv, PS[:, (6, 4)[t]:(6, 4)[t] + 2, :], xv, ALU.add).then_inc(S(sem), 1)

            gathered(0)
            with dve.Fori(0, passes) as p:
                with dve.Fori(0, NE) as e:
                    i = p * NE + e
                    for t in range(NT):
                        v.tensor_scalar(Sx[:, t], iota, keys[:, t, bass.ds(i + 1, 1)], None, ALU.is_equal)
                        last = v.tensor_scalar(Sw[:, t], iota, keys[:, t, bass.ds(i, 1)], combs[:, t, bass.ds(i, 1)],
                                               ALU.is_equal, ALU.mult)
                    last.then_inc(S("dispatch"), 1)
                    for c in range(NGU):
                        dve.wait_ge(S("esilu"), i * NGU + (c + 1))
                        src = PS[:, c % 2, 0:4 * CAP].rearrange("p (a g n) -> p a g n", a=2, g=2)
                        v.tensor_tensor(eT[:, 2 * c:2 * c + 2, :], src[:, :, 1], esilu[:, c % 2], ALU.mult).then_inc(S("e_ready"), 1)
                        if c == COMBINE_AT:
                            add(i, "added")
                    gathered(i + 1)
                    dve.wait_ge(S("G_turned"), i + 1)
                    v.tensor_copy(G, PS[0:CAP, 4, 0:SEQ].rearrange("p (t s) -> p t s", t=NT)).then_inc(S("G_ready"), 1)
            add(passes * NE, "x_final")


_NAMES = ["x", "mem", "positions", "a_norm", "a_w_in", "a_gate_bias", "a_head_norm", "a_w_out", "b_norm", "b_w_in",
          "b_q_a_norm", "b_w_uq", "b_q_head_norm", "b_w_out", "kv_norm", "w_dkv", "kv_a_norm", "w_ukv", "k_head_norm",
          "mem_norm", "mem_w_kv", "mem_q_norm", "mem_k_norm", "ffn_norm", "dense_w_gate_up", "dense_w_down",
          "moe_router", "moe_w_gate_up", "moe_w_down"]


def kernel(**inputs):
    import concourse.bacc as bacc
    from concourse.bass_utils import run_bass_kernel_spmd

    nc = bacc.Bacc("TRN2", target_bir_lowering=False, num_devices=1)
    arrays, views = {}, {}
    for name in _NAMES:
        a = np.ascontiguousarray(inputs[name])
        arrays[f"in_{name}"] = a
        views[name] = nc.dram_tensor(f"in_{name}", a.shape, mybir.dt.from_np(a.dtype), kind="ExternalInput").ap()
    shape = arrays["in_x"].shape
    out = nc.dram_tensor("out_x", shape, F32, kind="ExternalOutput").ap()
    build(nc, views, out)
    r = run_bass_kernel_spmd(nc, [arrays], core_ids=[0])
    return r.results[0]["out_x"]
```

```python
from contextlib import ExitStack

import numpy as np

import concourse.bass as bass
from concourse import mybir

ALU = mybir.AluOpType
ACT = mybir.ActivationFunctionType
AX = mybir.AxisListType
F32 = mybir.dt.float32
FR = mybir.dt.float32r
I32 = mybir.dt.int32
U32 = mybir.dt.uint32

P = 128
EPS = 1e-6
SLOTS = 6
SLOT = 2048
CUTS = 3
CAP = 128
NEG = -float(2.0 ** 100)
ROPE_THETA = 10000.0


def build(nc, T, out):
    SEQ, D = T["x"].shape[1:]
    NT = SEQ // P
    KD = D // P
    NMEM = T["mem"].shape[1]
    AH = T["a_gate_bias"].shape[1] // 2
    AV = T["a_head_norm"].shape[1] // AH
    MH, MD = 4, T["mem_q_norm"].shape[1]
    MW = MH * MD
    AIN = T["a_w_in"].shape[2]
    AQ = (AIN - 2 * AH * AV - 2 * AH - MW) // (2 * AH)
    QL = T["b_q_a_norm"].shape[1]
    KVL = T["kv_a_norm"].shape[0]
    QKH = T["b_q_head_norm"].shape[1]
    BH = T["b_w_uq"].shape[2] // QKH
    ROPE = T["w_dkv"].shape[1] - KVL
    NOPE = QKH - ROPE
    VH = T["w_ukv"].shape[1] // BH - NOPE
    FF = T["dense_w_down"].shape[1]
    NE = T["moe_router"].shape[2]
    KF = FF // P
    HR = ROPE // 2
    assert NT == 2 and KD == 8 and NMEM == SEQ and MW == 256 and AH == 4 and BH == 6 and NOPE == P and VH == P
    PASSES = -(-SEQ // CAP)

    x_d, mem_d = T["x"][0], T["mem"][0]

    def rows(w):
        return w.rearrange("(k p) n -> p k n", p=P)

    def cols(w, a, b):
        return rows(w)[:, :, a:b]

    aw, bw = T["a_w_in"][0], T["b_w_in"][0]
    aqw, avw = AH * AQ, AH * AV
    o_k, o_v, o_o, o_g = aqw, 2 * aqw, 2 * aqw + avw, 2 * aqw + 2 * avw
    hv = avw // 2
    HD = D // 2
    stream = [
        ("memkv0", cols(T["mem_w_kv"][0], 0, 2 * MW)), ("memkv1", cols(T["mem_w_kv"][1], 0, 2 * MW)),
        ("gmq", cols(aw, o_g, AIN)), ("q", cols(aw, 0, aqw)), ("k", cols(aw, o_k, o_v)),
        ("v0", cols(aw, o_v, o_v + hv)), ("v1", cols(aw, o_v + hv, o_o)),
        ("o0", cols(aw, o_o, o_o + hv)), ("o1", cols(aw, o_o + hv, o_g)),
        ("aout0", cols(T["a_w_out"][0], 0, HD)), ("aout1", cols(T["a_w_out"][0], HD, D)),
    ]
    FB = 2 * P
    NB = FF // FB
    PER = 3 * NB
    KH = KD // 2
    W = 2 * FB
    FFN = [("gu", 0, 0), ("gu", 0, 1)]
    for b in range(1, NB):
        FFN += [("gu", b, 0), ("gu", b, 1), ("dn", b - 1, 0)]
    FFN.append(("dn", NB - 1, 0))
    assert NB % 2 == 0 and PER % SLOTS == 0 and PER % CUTS == 0 and len(FFN) == PER

    def gu_item(b):
        return max(3 * b - 1, 0)

    def dn_item(b):
        return min(3 * b + 4, PER - 1)

    def ffn_parts(gu, dn, n):
        kind, b, h = FFN[n]
        if kind == "gu":
            return [(cols(gu, g * FF + b * FB, g * FF + (b + 1) * FB)[:, h * KH:(h + 1) * KH, :],
                     KH, slice(0, KH), slice(g * FB, (g + 1) * FB)) for g in range(2)]
        return [(rows(dn)[:, 2 * b + kk:2 * b + kk + 1, :], 2, slice(kk, kk + 1), slice(0, D)) for kk in range(2)]

    FFN0 = len(stream)
    stream += [(f"ffn{n}", None) for n in range(PER)]
    stream += [
        ("dkv", rows(T["w_dkv"])), ("cq", cols(bw, 0, QL)), ("mq", cols(bw, QL, QL + MW)),
        ("ukv", rows(T["w_ukv"])), ("uq", rows(T["b_w_uq"][0])),
        ("bout0", cols(T["b_w_out"][0], 0, HD)), ("bout1", cols(T["b_w_out"][0], HD, D)),
    ]
    NS = len(stream)
    item = {name: n for n, (name, _) in enumerate(stream)}
    place, before_it, filled_at = [], [], []
    at, occupant, fills = -2 * FFN0 % SLOTS, [None] * SLOTS, [0] * SLOTS
    for n, (name, view) in enumerate(stream):
        halves = [at] if view is None else [at, at + 1]
        place.append(at)
        before_it.append(sorted({occupant[h] for h in halves if occupant[h] is not None}))
        fills[at] += 32 if view is None else 16
        filled_at.append(fills[at])
        for h in halves:
            occupant[h] = n
        at = (at + len(halves)) % SLOTS
    E0 = at
    BASE_FILLS = fills
    EXPERT_FILLS = 32 * PER // SLOTS
    assert place[FFN0] == 0

    with ExitStack() as ctx:
        def sb(name, shape, dt=F32):
            return ctx.enter_context(nc.sbuf_tensor(name, shape, dt))

        sems = {}

        def S(name):
            if name not in sems:
                sems[name] = ctx.enter_context(nc.semaphore(name))
            return sems[name]

        PS = ctx.enter_context(nc.psum_tensor("PS", [P, 8, 512], F32))
        ring = sb("ring", [P, SLOTS * SLOT])
        whi = sb("whi", [P, CUTS, SLOT], FR)
        wlo = sb("wlo", [P, CUTS, SLOT], FR)
        xhi = sb("xhi", [P, KD, SEQ], FR)
        xlo = sb("xlo", [P, KD, SEQ], FR)
        hhi = sb("hhi", [P, 2, SEQ], FR)
        hlo = sb("hlo", [P, 2, SEQ], FR)
        xres = sb("xres", [P, NT, D])
        xn = sb("xn", [P, NT, D])
        xT = sb("xT", [P, KD, SEQ])
        mix = sb("mix", [P, NT, D])
        memkT = sb("memkT", [P, 2, 2, NMEM])
        memv = sb("memv", [P, 2, NT, MW])
        ident = sb("ident", [P, P])
        ones = sb("ones", [P, P])
        mask_kq = sb("mask_kq", [P, P])
        mask_qk = sb("mask_qk", [P, P])
        before = sb("before", [P, P])
        sel = sb("sel", [AH, AH, P])
        NG = 7 * KD + avw // P + QL // P + KVL // P + 4
        gains = sb("gains", [P, NG])
        hg = sb("hg", [P, 2 * QKH])
        bias_i = sb("bias_i", [AH, 1])
        bias_f = sb("bias_f", [AH, 1])
        nhalf = sb("nhalf", [P, 16])
        sumsq = sb("sumsq", [P, 2, 16])
        meansq = sb("meansq", [P, 2, 16])
        rstd = sb("rstd", [P, 2, 16])
        posi = sb("posi", [P, NT], I32)
        posf = sb("posf", [P, NT])
        invf = sb("invf", [P, HR])
        rot = sb("rot", [P, 6, NT, HR])
        roti = sb("roti", [P, NT, HR], I32)
        smax = sb("smax", [P, 16])
        ssum = sb("ssum", [P, 16])
        srec = sb("srec", [P, 16])
        sbias = sb("sbias", [P, 16])
        router = sb("router", [P, KD, NE])
        arena = sb("arena", [P, 10240])

        def carve(at, *shape):
            n = int(np.prod(shape))
            v = arena[:, at:at + n]
            if len(shape) == 1:
                return v
            names = "abcd"[:len(shape)]
            return v.rearrange(f"p ({' '.join(names)}) -> p {' '.join(names)}",
                               **{c: s for c, s in zip(names, shape)})

        memS = carve(0, NT, D)
        memT = carve(2048, 2, KD, NMEM)
        kS = carve(0, 2, NT, MW)
        mqS = carve(1024, NT, MW)
        mqT = carve(1536, 2, SEQ)
        qT = carve(2048, AH, SEQ)
        kT = carve(3072, AH, SEQ)
        VW = AV + 1
        A0 = 6144
        v1 = carve(A0, NT, AH, VW)
        og = carve(A0 + NT * AH * VW, NT, avw)
        assert A0 + NT * AH * VW + NT * avw <= 9728
        grow = arena[0:NG, A0:A0 + P]
        hrow = arena[0:1, A0 + P:A0 + P + 2 * QKH]
        gat = arena[0:AH, 4096:4096 + 8 * SEQ].rearrange("p (a b) -> p a b", a=8)
        gi, gf, gt, glf, gG, ga, gM, gone = (gat[:, r] for r in range(8))
        gm, gem, gneg = gf, gt, glf
        gN = sb("gN", [P, 2, NT, AH])
        den = sb("den", [P, NT * AH])
        xflat = xn[:, :, :].rearrange("p a b -> p (a b)")
        Dm = mix[:, :, :].rearrange("p a b -> p (a b)")[:, 0:AH * 384].rearrange("p (a b) -> p a b", a=AH)
        PmT = xflat[:, 0:AH * 384].rearrange("p (a b) -> p a b", a=AH)
        mP = xn[:, :, :].rearrange("p a (h m) -> p a h m", h=MH)
        mPT = xT[:, :, :].rearrange("p a b -> p (a b)").rearrange("p (t h m q) -> p t h m q", t=NT, h=MH, m=2)
        sil = carve(0, NT, FB)
        hn = carve(NT * FB, NT, FB)
        xTk = carve(0, KD, SEQ)
        qF = carve(0, NT * BH, QKH)
        cqS = carve(2688, NT, QL)
        mqS1 = carve(3456, NT, MW)
        ckvT = carve(3968, 2, SEQ)
        cqT = carve(4480, 3, SEQ)
        kTn = carve(2304, BH, SEQ)
        kTr = arena[0:ROPE, 3840:3840 + BH * SEQ].rearrange("p (h s) -> p h s", h=BH)
        kF = carve(5760, NT * BH, QKH)
        zS = carve(8064, NT, KVL + ROPE)
        mqT1 = carve(8704, 2, SEQ)
        qTn = xT[:, 0:BH, :]
        qTr = xflat[0:ROPE, 0:BH * SEQ].rearrange("p (h s) -> p h s", h=BH)
        vF = mix[:, :, :].rearrange("p a b -> p (a b)")[:, 0:NT * BH * VH].rearrange("p (t h b) -> p t h b", t=NT, b=VH)
        Pb = carve(5760, BH, 384)
        PT = carve(0, BH, 384)
        o = 2 * NT * FB
        xe = carve(o, KD, CAP); o += KD * CAP
        Sx = carve(o, NT, CAP); o += NT * CAP
        Sw = carve(o, NT, CAP); o += NT * CAP
        y = carve(o, D); o += D
        G = carve(o, NT, P); o += NT * P
        NC = (PASSES + 1) * NE
        iota = carve(o, CAP); o += CAP
        iotai = arena[:, o:o + CAP].bitcast(I32); o += CAP
        lg = carve(o, NT, NE); o += NT * NE
        m8 = carve(o, NT, 8); o += NT * 8
        idxf = carve(o, NT, 8); o += NT * 8
        idx8 = arena[:, o:o + NT * 8].bitcast(U32).rearrange("p (a b) -> p a b", a=NT); o += NT * 8
        oh1 = carve(o, NT, NE); o += NT * NE
        oh2 = carve(o, NT, NE); o += NT * NE
        chosen = carve(o, NT, NE); o += NT * NE
        keys = carve(o, NT, NC); o += NT * NC
        combs = carve(o, NT, NC); o += NT * NC
        gt2 = carve(o, 16); o += 16
        assert o <= 9728
        cnt_i = sb("cnt_i", [P, 1], I32)

        NORMS = ["mem", "x0", "mk0", "mk1", "mq0", "hm", "x1", "x2", "ckv", "cq", "mq1", "kh", "qh", "x3"]
        nidx = {n: i for i, n in enumerate(NORMS)}

        def nat(v, W):
            return v.rearrange("p a (h w) -> p a h w", w=W)

        nview = {
            "mem": (memS, memS, D), "x0": (xres[:, :, :], xn[:, :, :], D),
            "mk0": (nat(kS[:, 0], MD), None, MD), "mk1": (nat(kS[:, 1], MD), None, MD),
            "mq0": (nat(mqS, MD), None, MD), "hm": (nat(mix[:, :, 0:avw], AV), None, AV),
            "x1": (xres[:, :, :], xn[:, :, :], D), "x2": (xres[:, :, :], xn[:, :, :], D),
            "ckv": (zS[:, :, 0:KVL], None, KVL), "cq": (cqS, None, QL), "mq1": (nat(mqS1, MD), None, MD),
            "kh": (kF, None, QKH), "qh": (qF, None, QKH), "x3": (xres[:, :, :], xn[:, :, :], D),
        }

        OWN_SUMS = ("mem", "x0", "x1", "x2", "kh", "qh", "x3")
        squares_no, m = {}, 0
        for name in NORMS:
            m += name not in OWN_SUMS
            squares_no[name] = m

        def sums(name):
            return sumsq[:, nidx[name] % 2, :]

        def groups(name):
            v = nview[name][0]
            return int(np.prod(v.shape[1:-1]))

        def shaped(tile, name):
            v = nview[name][0]
            t = tile[:, 0:groups(name)]
            if len(v.shape) == 4:
                t = t.rearrange("p (a b) -> p a b", a=v.shape[1])
            return t

        def sq_of(name):
            v = nview[name][0]
            n = int(np.prod(v.shape[1:]))
            at = {"hm": 2048, "mk0": 9728, "mk1": 9728, "mq0": 9728}.get(name, 9472)
            assert at + n <= arena.shape[1]
            base = arena[:, at:at + n]
            if len(v.shape) == 4:
                return base.rearrange("p (a b c) -> p a b c", a=v.shape[1], b=v.shape[2])
            return base.rearrange("p (a b) -> p a b", a=v.shape[1])

        def bcast(ap, n):
            return bass.AP(ap.tensor, ap.offset, [list(d) for d in ap.ap] + [[0, n]])

        gcol = {}
        at = 0
        for name, n in (("a_norm", KD), ("b_norm", KD), ("kv_norm", KD), ("mem0", KD), ("mem1", KD), ("ffn0", KD),
                        ("ffn1", KD), ("head", avw // P), ("q_a", QL // P), ("kv_a", KVL // P),
                        ("memq0", 1), ("memk0", 1), ("memq1", 1), ("memk1", 1)):
            gcol[name] = at
            at += n
        assert at == NG

        TR = [
            ("mem", memS, 0, [(memT[:, 0], "mem0"), (memT[:, 1], "mem1")]),
            ("x0", xn, 4, [(xT, "a_norm")]),
            ("mix0", mix, 0, [(xT, "head")]),
            ("x1", xn, 0, []),
            ("x2", xn, 0, [(xTk, "kv_norm"), (xT, "b_norm")]),
            ("mix1", mix, 0, [(xT, None)]),
            ("x3", xn, 0, [(xT, "ffn1")]),
        ]
        tidx = {t[0]: i for i, t in enumerate(TR)}

        def trans_gain(name, g, k):
            if g is None or (g == "head" and k >= avw // P):
                return None
            return gains[:, gcol[g] + k:gcol[g] + k + 1]

        block = ctx.enter_context(nc.Block())

        UNITS = [(kind, t, g) for kind in ("kv", "q") for t in range(NT) for g in range(BH // 2)]
        UNITS = [(kind, t, g, u % 8) for u, (kind, t, g) in enumerate(UNITS)]
        KQT = [(full[:, 2 * g:2 * g + 2, :], n, 0) for a, b in ((kTn, kTr), (qTn, qTr))
               for full, n in ((a, P), (b, ROPE)) for g in range(BH // 2)]
        KQT = [(dst, n, u % 8) for u, (dst, n, _) in enumerate(KQT)]
        PTB = [6, 7, 0, 1, 2]
        REST = range(2, NB - 2, 2)

        def count(i, per_ffn, r, per_block, const):
            if r is not None:
                const = r * (2 * per_block) + const
            return const if i is None else i * per_ffn + const

        def cuts_before(i):
            return 0 if i is None else PER

        def blocks_before(i):
            return 0 if i is None else NB

        def items_before(i):
            return FFN0 if i is None else NS

        def cut_item(b):
            return [n for n in (3 * b + 1, 3 * b + 2) if n < PER]

        def k_gain(name, g, k):
            if g is None or (g == "head" and k >= avw // P):
                return None
            return gains[:, gcol[g] + k:gcol[g] + k + 1]

        def through(name):
            return item[name] + 1

        @block.sync
        def _(sp):
            def fill_big(h, view):
                k, n = view.shape[1:]
                sp.dma_start(ring[:, h * SLOT:h * SLOT + k * n].rearrange("p (k n) -> p k n", k=k), view).then_inc(S(f"slot_full{h}"), 16)

            def fill_ffn(h, gu, dn, n):
                for view, k, ks, ns in ffn_parts(gu, dn, n):
                    dst = ring[:, h * SLOT:(h + 1) * SLOT].rearrange("p (k n) -> p k n", k=k)
                    sp.dma_start(dst[:, ks, ns], view).then_inc(S(f"slot_full{h}"), 16)

            sp.dma_start(memS, mem_d.rearrange("(t p) d -> p t d", p=P)).then_inc(S("mem_in"), 16)
            sp.wait_ge(S("mem_in"), 16)
            sp.wait_ge(S("x_in"), 16)
            for n, (name, view) in enumerate(stream):
                for m in before_it[n]:
                    if stream[m][1] is None:
                        sp.wait_ge(S("lows"), m - FFN0 + 1)
                    else:
                        sp.wait_ge(S("through"), m + 1)
                if view is None:
                    fill_ffn(place[n], T["dense_w_gate_up"][0], T["dense_w_down"][0], n - FFN0)
                else:
                    fill_big(place[n], view)

            def load_experts(p):
                with sp.Fori(0, NE) as e:
                    gu = T["moe_w_gate_up"][0][bass.ds(e, 1), :, :].rearrange("e d n -> (e d) n")
                    dn = T["moe_w_down"][0][bass.ds(e, 1), :, :].rearrange("e d n -> (e d) n")
                    i = e if p is None else p * NE + e
                    for n in range(PER):
                        sp.wait_ge(S("lows"), i * PER + (PER + n - SLOTS + 1))
                        fill_ffn((E0 + n) % SLOTS, gu, dn, n)

            sp.wait_ge(S("through"), NS)
            sp.wait_ge(S("routed"), 1)
            passes = sp.value_load(cnt_i[0:1, 0:1], min_val=1, max_val=PASSES)
            with sp.Fori(0, passes) as p:
                load_experts(p)
            for t in range(NT):
                sp.wait_ge(S("x_final"), t + 1)
                sp.dma_start(out[0].rearrange("(t p) d -> p t d", p=P)[:, t], xres[:, t]).then_inc(S("stored"), 16)
            sp.wait_ge(S("stored"), 16 * NT)

        @block.gpsimd
        def _(pool):
            c = S("consts")
            pool.memset(ident[:, :], 0.0).then_inc(c, 1)
            pool.memset(ones[:, :], 1.0).then_inc(c, 1)
            pool.memset(nhalf[:, :], -0.5).then_inc(c, 1)
            pool.wait_ge(c, 3)
            pool.affine_select(out=ident[:, :], in_=ident[:, :], compare_op=ALU.not_equal, fill=1.0, base=0,
                               pattern=[[-1, P]], channel_multiplier=1).then_inc(S("ident"), 1)
            n = [0]

            def rstd_of(name):
                e, g = nidx[name], groups(name)
                if e > 1:
                    pool.wait_ge(S("scaled"), e - 1)
                pool.wait_ge(S("sums"), e + 1)
                pool.tensor_scalar(meansq[:, e % 2, 0:g], sums(name)[:, 0:g], EPS, None, ALU.add).then_inc(S("mean_eps"), 1)
                pool.wait_ge(S("mean_eps"), e + 1)
                pool.tensor_tensor(rstd[:, e % 2, 0:g], meansq[:, e % 2, 0:g], nhalf[:, 0:g], ALU.pow).then_inc(S("rstds"), 1)

            rstd_of("mem")
            rstd_of("x0")
            pool.memset(mask_kq[:, :], 0.0).then_inc(c, 1)
            pool.memset(mask_qk[:, :], 0.0).then_inc(c, 1)
            pool.memset(sel[:, :, :], 0.0).then_inc(c, 1)
            pool.wait_ge(c, 6)
            pool.affine_select(out=mask_kq[:, :], in_=mask_kq[:, :], compare_op=ALU.is_ge, fill=NEG, base=0,
                               pattern=[[1, P]], channel_multiplier=-1).then_inc(c, 1)
            pool.affine_select(out=mask_qk[:, :], in_=mask_qk[:, :], compare_op=ALU.is_ge, fill=NEG, base=0,
                               pattern=[[-1, P]], channel_multiplier=1).then_inc(c, 1)
            pool.affine_select(out=before[:, :], in_=ones[:, :], compare_op=ALU.is_gt, fill=0.0, base=0,
                               pattern=[[1, P]], channel_multiplier=-1).then_inc(c, 1)
            pool.affine_select(out=sel[:, :, :], in_=sel[:, :, :], compare_op=ALU.not_equal, fill=1.0, base=0,
                               pattern=[[-1, AH], [0, P]], channel_multiplier=1).then_inc(c, 1)
            rstd_of("mk0")
            rstd_of("mk1")
            rstd_of("mq0")
            inv = (1.0 / np.float32(ROPE_THETA) ** (np.arange(0, ROPE, 2, dtype=np.float32) / np.float32(ROPE))
                   ).astype(np.float32)
            for j in range(HR):
                last = pool.memset(invf[:, j:j + 1], float(inv[j]))
            last.then_inc(S("freqs"), 1)
            rstd_of("hm")
            rstd_of("x1")
            for name in ("x2", "ckv", "cq", "mq1", "kh", "qh"):
                rstd_of(name)
            rstd_of("x3")
            pool.iota(iotai, pattern=[[1, CAP]], base=0, channel_multiplier=0).then_inc(S("iota_i"), 1)
            pool.wait_ge(S("iota_i"), 1)
            pool.tensor_copy(iota, iotai).then_inc(S("iota"), 1)
            pool.memset(G, 0.0).then_inc(S("G_ready"), 1)

        @block.scalar
        def _(act):
            G0 = gcol
            vec = [("a_norm", T["a_norm"][0]), ("b_norm", T["b_norm"][0]), ("kv_norm", T["kv_norm"]),
                   ("mem0", T["mem_norm"][0]), ("mem1", T["mem_norm"][1]), ("ffn0", T["ffn_norm"][0]),
                   ("ffn1", T["ffn_norm"][1]), ("head", T["a_head_norm"][0]), ("q_a", T["b_q_a_norm"][0]),
                   ("kv_a", T["kv_a_norm"])]
            act.dma_start(xres[:, :, :], x_d.rearrange("(t p) d -> p t d", p=P)).then_inc(S("x_in"), 16)
            for name, v in vec:
                k = v.shape[0] // P
                act.dma_start(grow[G0[name]:G0[name] + k, :], v.rearrange("(k p) -> k p", p=P)).then_inc(S("gain_in"), 16)
            for name, v in (("memq0", T["mem_q_norm"][0]), ("memk0", T["mem_k_norm"][0]),
                            ("memq1", T["mem_q_norm"][1]), ("memk1", T["mem_k_norm"][1])):
                for h in range(2):
                    act.dma_start(grow[G0[name]:G0[name] + 1, h * MD:(h + 1) * MD],
                                  v.rearrange("(a n) -> a n", a=1)).then_inc(S("gain_in"), 16)
            act.dma_start(hrow[:, 0:QKH], T["k_head_norm"].rearrange("(a n) -> a n", a=1)).then_inc(S("gain_in"), 16)
            act.dma_start(hrow[:, QKH:2 * QKH], T["b_q_head_norm"]).then_inc(S("gain_in"), 16)
            gb = T["a_gate_bias"].rearrange("a n -> n a")
            act.dma_start(bias_i[:, :], gb[0:AH]).then_inc(S("bias_in"), 16)
            act.dma_start(bias_f[:, :], gb[AH:2 * AH]).then_inc(S("bias_in"), 16)
            act.dma_start(posi[:, :], T["positions"][0].rearrange("(t p) -> p t", p=P),
                          allow_slow_non_contiguous=True).then_inc(S("pos_in"), 16)
            act.dma_start(router[:, :, :], rows(T["moe_router"][0])).then_inc(S("router_in"), 16)

            def square(name):
                e, (v, dst, w) = nidx[name], nview[name]
                if e > 1:
                    act.wait_ge(S("rstds"), e - 1)
                if name not in OWN_SUMS:
                    if squares_no[name] > 1:
                        act.wait_ge(S("sums"), e)
                    nc.scalar.activation(sq_of(name), v, ACT.Square, scale=float(w) ** -0.5).then_inc(S("squares"), 1)
                    return
                n = groups(name) * w
                junk = {"mem": arena[:, 2048:2048 + n], "kh": whi[:, 0:2, :].rearrange("p a b -> p (a b)")[:, 0:n],
                        "qh": wlo[:, 0:2, :].rearrange("p a b -> p (a b)")[:, 0:n]}.get(name, xflat)
                for g in range(groups(name)):
                    last = nc.scalar.activation(junk[:, g * w:(g + 1) * w], v[:, g], ACT.Square, scale=float(w) ** -0.5, accum_out=sums(name)[:, g:g + 1])
                last.then_inc(S("sums"), 1)

            def hi_of(i, n, r=None):
                const = items_before(i) + n - CUTS + 1
                if i is not None or n >= CUTS or r is not None:
                    act.wait_ge(S("through"), count(i, PER, r, 3, const))
                h = ((E0 if i is not None else 0) + n) % SLOTS
                base = filled_at[FFN0 + n] if i is None else BASE_FILLS[h] + 32 * (n // SLOTS + 1)
                if r is not None:
                    base = r * 32 + base
                act.wait_ge(S(f"slot_full{h}"), base if i is None else i * EXPERT_FILLS + base)
                nc.scalar.activation(whi[:, n % CUTS, :], ring[:, h * SLOT:(h + 1) * SLOT], ACT.Copy).then_inc(S("highs"), 1)

            def block(i, b, nt, r=None):
                for n in cut_item(b):
                    hi_of(i, n, r)
                if b == 0 and i is not None:
                    act.wait_ge(S("through"), count(i, PER, r, 3, NS))
                    nc.scalar.activation(y.rearrange("p (a b) -> p a b", a=2), PS[:, 4:6, :], ACT.Copy).then_inc(S("y_ready"), 1)
                act.wait_ge(S("through"), count(i, PER, r, 3, items_before(i) + gu_item(b) + 2))
                nc.scalar.activation(sil[:, 0:nt], PS[:, 0:nt, 0:FB], ACT.Silu).then_inc(S("silu"), 1)
                if 3 * b + 3 < PER:
                    hi_of(i, 3 * b + 3, r)
                if b == NB - 1 and i is not None:
                    act.wait_ge(S("xe_ready"), i + 2)
                    nc.scalar.activation(xhi[:, :, 0:CAP], xe, ACT.Copy).then_inc(S("xhi_ready"), 1)
                act.wait_ge(S("h_turned"), count(i, NB, r, 1, blocks_before(i) + b + 1))
                src = PS[:, 3, :].rearrange("p (a s) -> p a s", a=2)
                nc.scalar.activation(hhi[:, :, 0:nt * P], src[:, :, 0:nt * P], ACT.Copy).then_inc(S("h_high"), 1)

            def swiglu(i, nt):
                hi_of(i, 0)
                for b in (0, 1):
                    block(i, b, nt)
                with act.Fori(0, len(REST)) as r:
                    for b in (2, 3):
                        block(i, b, nt, r)
                for b in (NB - 2, NB - 1):
                    block(i, b, nt)

            def evict(name):
                i, (_, _, bank, dsts) = tidx[name], TR[tidx[name]]
                for b in (0, 2):
                    act.wait_ge(S("transposed"), 4 * i + b + 1)
                    for dst, g in dsts:
                        for k in (2 * b, 2 * b + 1):
                            s = k_gain(name, g, k)
                            last = nc.scalar.activation(dst[:, k, :], PS[:, bank + b, (k % 2) * SEQ:(k % 2 + 1) * SEQ], ACT.Copy,
                                                        scale=1.0 if s is None else s)
                    last.then_inc(S("evicted_even"), 1)

            def mem_softmax(l, bank):
                for t in range(NT):
                    for h in range(MH):
                        if t == 0 and h == 0:
                            act.wait_ge(S("mem_max"), l + 1)
                        c = t * MH + h
                        last = nc.scalar.activation(mP[:, t, h], PS[:, bank + 2 * t + h % 2, (h // 2) * 256:(h // 2 + 1) * 256],
                                                    ACT.Exp, bias=sbias[:, c:c + 1], scale=float(MD) ** -0.5,
                                                    accum_out=ssum[:, c:c + 1])
                last.then_inc(S("mem_exp"), 1)
                for b in range(2):
                    act.wait_ge(S("mem_pt"), 4 * l + 2 * b + 1)
                    nc.scalar.activation(mPT[:, b, 0:2].rearrange("p h m q -> p (h m q)"), PS[:, 2 * b, :],
                                         ACT.Copy).then_inc(S("mem_pt_even"), 1)

            act.wait_ge(S("mem_in"), 16)
            square("mem")
            act.wait_ge(S("x_in"), 16)
            square("x0")
            act.wait_ge(S("gains"), 2)
            evict("mem")
            evict("x0")
            for l in range(2):
                act.wait_ge(S("through"), through(f"memkv{l}"))
                act.wait_ge(S("transposed"), 4)
                nc.scalar.activation(kS[:, l], PS[:, 2 * l:2 * l + 2, 0:MW], ACT.Copy).then_inc(S("kS"), 1)
                nc.scalar.activation(memv[:, l], PS[:, 2 * l:2 * l + 2, MW:2 * MW], ACT.Copy).then_inc(S("memv"), 1)
            act.wait_ge(S("kS"), 2)
            square("mk0")
            square("mk1")
            act.wait_ge(S("through"), through("gmq"))
            act.wait_ge(S("bias_in"), 32)
            nc.scalar.activation(gi, PS[0:AH, 4, 0:SEQ], ACT.Identity, bias=bias_i[:, :]).then_inc(S("gate_in"), 1)
            nc.scalar.activation(gf, PS[0:AH, 4, SEQ:2 * SEQ], ACT.Identity, bias=bias_f[:, :]).then_inc(S("gate_in"), 1)
            nc.scalar.activation(mqS, PS[:, 5, :].rearrange("p (t n) -> p t n", t=NT), ACT.Copy).then_inc(S("mqS"), 1)
            act.wait_ge(S("gate_abs"), 1)
            nc.scalar.activation(gt, gt, ACT.Exp, scale=-1.0).then_inc(S("gate_exp"), 1)
            act.wait_ge(S("gate_exp"), 1)
            nc.scalar.activation(gt, gt, ACT.Ln, bias=1.0).then_inc(S("gate_exp"), 1)
            act.wait_ge(S("mqS"), 1)
            square("mq0")
            act.wait_ge(S("through"), through("q"))
            for b in range(2):
                last = nc.scalar.activation(qT[0:AQ, 2 * b:2 * b + 2, :], PS[0:AQ, 6 + b, :].rearrange("p (h s) -> p h s", h=2), ACT.Copy)
            last.then_inc(S("qT"), 1)
            for half in range(2):
                act.wait_ge(S("through"), through(f"o{half}"))
                for t in range(NT):
                    last = nc.scalar.activation(og[:, t, half * hv:(half + 1) * hv], PS[:, (6, 0)[half] + t, 0:hv], ACT.Sigmoid)
                last.then_inc(S("og"), 1)
            act.wait_ge(S("gate_m"), 1)
            nc.scalar.activation(gem, gm, ACT.Exp, scale=-1.0).then_inc(S("gate_em"), 1)
            act.wait_ge(S("gN"), 1)
            for h in range(AH):
                act.wait_ge(S("decay_arg"), h + 1)
                for s0, c0, c1 in ((0, 0, SEQ), (1, SEQ, SEQ + P)):
                    last = nc.scalar.activation(Dm[:, h, c0:c1], PS[:, h, c0:c1], ACT.Exp, bias=gN[:, 0, s0, h:h + 1])
                last.then_inc(S("decay"), 1)
            mem_softmax(0, 4)
            act.wait_ge(S("h_out"), 1)
            square("hm")
            evict("mix0")
            act.wait_ge(S("x_sum"), 1)
            square("x1")
            for k in range(KD):
                if k % 2 == 0:
                    act.wait_ge(S("transposed"), 4 * tidx["x1"] + k // 2 + 1)
                last = nc.scalar.activation(xhi[:, k, :], PS[:, k // 2, (k % 2) * SEQ:(k % 2 + 1) * SEQ], ACT.Copy,
                                            scale=k_gain("x1", "ffn0", k))
                if k % 2 == 1:
                    last.then_inc(S("x1_high"), 1)

            swiglu(None, NT)
            act.wait_ge(S("x_sum"), 2)
            square("x2")
            act.wait_ge(S("angles"), 1)
            nc.scalar.activation(rot[:, 4], rot[:, 2], ACT.Sin).then_inc(S("sincos"), 1)
            nc.scalar.activation(rot[:, 5], rot[:, 3], ACT.Sin).then_inc(S("sincos"), 1)
            evict("x2")
            act.wait_ge(S("through"), through("dkv"))
            nc.scalar.activation(zS, PS[:, 4:6, 0:KVL + ROPE], ACT.Copy).then_inc(S("zS"), 1)
            act.wait_ge(S("through"), through("cq"))
            nc.scalar.activation(cqS, PS[:, 6:8, 0:QL], ACT.Copy).then_inc(S("cqS"), 1)
            act.wait_ge(S("through"), through("mq"))
            nc.scalar.activation(mqS1, PS[:, 0, :].rearrange("p (t n) -> p t n", t=NT), ACT.Copy).then_inc(S("mqS"), 1)
            act.wait_ge(S("zS"), 1)
            square("ckv")
            act.wait_ge(S("cqS"), 1)
            square("cq")
            act.wait_ge(S("mqS"), 2)
            square("mq1")
            for u, (kind, t, g, bank) in enumerate(UNITS):
                if u % 6 == 5:
                    act.wait_ge(S("through"), through("ukv" if u == 5 else "uq"))
                else:
                    act.wait_ge(S("unit"), u + 1 - u // 6)
                if kind == "kv":
                    src = PS[:, bank, :].rearrange("p (h a n) -> p h a n", h=2, a=2)
                    kdst = kF.rearrange("p (t h) n -> p t h n", t=NT)[:, t, 2 * g:2 * g + 2, 0:NOPE]
                    nc.scalar.activation(kdst, src[:, :, 0], ACT.Copy)
                    last = nc.scalar.activation(vF[:, t, 2 * g:2 * g + 2], src[:, :, 1], ACT.Copy)
                else:
                    dst = qF.rearrange("p (t h) n -> p t h n", t=NT)[:, t, 2 * g:2 * g + 2]
                    last = nc.scalar.activation(dst, PS[:, bank, 0:2 * QKH].rearrange("p (h n) -> p h n", h=2), ACT.Copy)
                last.then_inc(S("unit_out"), 1)
                if u == 5:
                    act.wait_ge(S("unit_out"), 6)
                    act.wait_ge(S("k_rope_in"), 1)
                    square("kh")
            act.wait_ge(S("unit_out"), 12)
            square("qh")
            for u, (dst, rws, bank) in enumerate(KQT):
                if u % 2 == 0:
                    act.wait_ge(S("kq_t"), u + 1)
                    nc.scalar.activation(dst, PS[0:rws, bank, :].rearrange("p (h s) -> p h s", h=2), ACT.Copy).then_inc(S("kq_even"), 1)
            act.wait_ge(S("att_max"), 1)
            for h in range(BH):
                for t, (c0, c1) in enumerate(((0, P), (P, 3 * P))):
                    last = nc.scalar.activation(Pb[:, h, c0:c1], PS[:, h, c0:c1], ACT.Exp, bias=sbias[:, t * BH + h:t * BH + h + 1],
                                                scale=float(QKH) ** -0.5, accum_out=ssum[:, t * BH + h:t * BH + h + 1])
                last.then_inc(S("att_exp"), 1)
            for u, bank in enumerate(PTB):
                if u % 2 == 0:
                    act.wait_ge(S("att_pt"), u + 1)
                    n = min(512, BH * 384 - 512 * u)
                    nc.scalar.activation(PT.rearrange("p a b -> p (a b)")[:, 512 * u:512 * u + n], PS[:, bank, 0:n],
                                         ACT.Copy).then_inc(S("att_pt_even"), 1)
            mem_softmax(1, 4)
            evict("mix1")
            act.wait_ge(S("x_sum"), 3)
            square("x3")
            evict("x3")
            act.wait_ge(S("top2"), 1)
            nc.scalar.activation(gt2[:, 2:4], gt2[:, 0:2], ACT.Exp).then_inc(S("gate2_exp"), 1)
            act.wait_ge(S("routed"), 1)
            passes = act.value_load(cnt_i[0:1, 0:1], min_val=1, max_val=PASSES)

            act.wait_ge(S("xe_ready"), 1)
            nc.scalar.activation(xhi[:, :, 0:CAP], xe, ACT.Copy).then_inc(S("xhi_ready"), 1)
            with act.Fori(0, passes) as p:
                with act.Fori(0, NE) as e:
                    swiglu(p * NE + e, 1)
            act.wait_ge(S("through"), passes * (NE * PER) + NS)
            nc.scalar.activation(y.rearrange("p (a b) -> p a b", a=2), PS[:, 4:6, :], ACT.Copy).then_inc(S("y_ready"), 1)

        @block.tensor
        def _(pe):
            mm = nc.tensor.matmul

            def tr(dst, src):
                return nc.tensor.transpose(dst, src, ident[0:src.shape[0], 0:src.shape[0]])

            def slot(name, *shape):
                n = item[name]
                pe.wait_ge(S(f"slot_full{place[n]}"), filled_at[n])
                at = place[n] * SLOT
                return ring[:, at:at + int(np.prod(shape))].rearrange("p (k n) -> p k n", k=shape[0])

            def transposes(name):
                _, src, bank, _ = TR[tidx[name]]
                for b in range(4):
                    for k in (2 * b, 2 * b + 1):
                        for t in range(NT):
                            last = tr(PS[:, bank + b, (k % 2) * SEQ + t * P:(k % 2) * SEQ + (t + 1) * P], src[:, t, k * P:(k + 1) * P])
                    last.then_inc(S("transposed"), 1)

            def evicted(name):
                n = 2 * sum(1 for t in TR[:tidx[name] + 1] if t[3])
                pe.wait_ge(S("evicted_even"), n)
                pe.wait_ge(S("evicted_odd"), n)

            def natural(banks, src, w, n, nk=KD, c0=0):
                for t in range(NT):
                    bank, at = banks[t]
                    for k in range(nk):
                        last = mm(PS[:, bank, at:at + n], lhsT=src[:, k, t * P:(t + 1) * P], rhs=w[:, k, c0:c0 + n],
                                  start=(k == 0), stop=(k == nk - 1))
                return last

            def mem_attention(l, kT_, qT_, q_sem, q_val):
                pe.wait_ge(S(q_sem), q_val)
                pe.wait_ge(S("memkT"), 2)
                for par in range(2):
                    for t in range(NT):
                        for pair in range(2):
                            last = mm(PS[:, 4 + 2 * t + par, pair * 256:(pair + 1) * 256],
                                      lhsT=qT_[par * MD:(par + 1) * MD, pair, t * P:(t + 1) * P],
                                      rhs=kT_[par * MD:(par + 1) * MD, pair, :], start=True, stop=True)
                last.then_inc(S("mem_scores"), 1)

            def mem_attention_out(l):
                pe.wait_ge(S("mem_exp"), l + 1)
                for t in range(NT):
                    for hh in range(2):
                        for h in (2 * hh, 2 * hh + 1):
                            for m in range(2):
                                last = tr(PS[:, 2 * t + hh, ((h % 2) * 2 + m) * P:((h % 2) * 2 + m + 1) * P], mP[:, t, h, m * P:(m + 1) * P])
                        last.then_inc(S("mem_pt"), 1)
                pe.wait_ge(S("mem_pt_even"), 2 * (l + 1))
                pe.wait_ge(S("mem_pt_odd"), 2 * (l + 1))
                for t in range(NT):
                    for h in range(MH):
                        for m in range(2):
                            last = mm(PS[:, 4, (t * MH + h) * MD:(t * MH + h + 1) * MD], lhsT=mPT[:, t, h, m, :],
                                      rhs=memv[:, l, m, h * MD:(h + 1) * MD], start=(m == 0), stop=(m == 1))
                last.then_inc(S("mem_out"), 1)

            def project_out(names):
                for hh, name in enumerate(names):
                    w = slot(name, KD, HD)
                    natural([(4 + hh, 0), (6 + hh, 0)], xT, w, HD).then_inc(S("through"), 1)

            pe.wait_ge(S("ident"), 1)
            pe.wait_ge(S("gain_in"), 16 * 20)
            tr(PS[:, 7, 0:NG], grow)
            mm(PS[:, 6, 0:2 * QKH], lhsT=ones[0:1, :], rhs=hrow, start=True, stop=True).then_inc(S("gains_t"), 1)
            pe.wait_ge(S("scaled"), nidx["mem"] + 1)
            transposes("mem")
            pe.wait_ge(S("scaled"), nidx["x0"] + 1)
            pe.wait_ge(S("gains"), 2)
            transposes("x0")
            evicted("mem")
            for l in range(2):
                w = slot(f"memkv{l}", KD, 2 * MW)
                natural([(2 * l, 0), (2 * l + 1, 0)], memT[:, l], w, 2 * MW).then_inc(S("through"), 1)
            evicted("x0")
            w = slot("gmq", KD, 2 * AH + MW)
            for half in range(2):
                for k in range(KD):
                    mm(PS[0:AH, 4, half * SEQ:(half + 1) * SEQ], lhsT=w[:, k, half * AH:(half + 1) * AH], rhs=xT[:, k, :],
                       start=(k == 0), stop=(k == KD - 1))
            natural([(5, 0), (5, MW)], xT, w, MW, c0=2 * AH).then_inc(S("through"), 1)
            for name, bank in (("q", 6), ("k", 0)):
                if name == "k":
                    pe.wait_ge(S("memv"), 2)
                w = slot(name, KD, aqw)
                for h in range(AH):
                    for k in range(KD):
                        last = mm(PS[0:AQ, bank + h // 2, (h % 2) * SEQ:(h % 2 + 1) * SEQ], lhsT=w[:, k, h * AQ:(h + 1) * AQ],
                                  rhs=xT[:, k, :], start=(k == 0), stop=(k == KD - 1))
                last.then_inc(S("through"), 1)
            for name, banks in (("v0", (2, 3)), ("v1", (4, 5)), ("o0", (6, 7)), ("o1", (0, 1))):
                if name == "v1":
                    pe.wait_ge(S("mqS"), 1)
                if name == "o0":
                    pe.wait_ge(S("qT"), 1)
                if name == "o1":
                    pe.wait_ge(S("kT"), 1)
                w = slot(name, KD, hv)
                natural([(b, 0) for b in banks], xT, w, hv).then_inc(S("through"), 1)
            pe.wait_ge(S("v_out"), 2)
            for l in range(2):
                pe.wait_ge(S("scaled"), nidx[f"mk{l}"] + 1)
                for pair in range(2):
                    for t in range(NT):
                        last = tr(PS[:, 2 + l, pair * SEQ + t * P:pair * SEQ + (t + 1) * P], kS[:, l, t, pair * P:(pair + 1) * P])
                last.then_inc(S("memk_t"), 1)
            pe.wait_ge(S("scaled"), nidx["mq0"] + 1)
            for pair in range(2):
                for t in range(NT):
                    last = tr(PS[:, 4, pair * SEQ + t * P:pair * SEQ + (t + 1) * P], mqS[:, t, pair * P:(pair + 1) * P])
            last.then_inc(S("mq_t"), 1)
            pe.wait_ge(S("gate_em"), 1)
            for r, src in enumerate((ga, gem)):
                for t in range(NT):
                    c = (r * NT + t) * AH
                    last = tr(PS[:, 5, c:c + AH], src[:, t * P:(t + 1) * P])
            last.then_inc(S("gate_t"), 1)
            pe.wait_ge(S("og"), 2)
            pe.wait_ge(S("memkT"), 2)
            pe.wait_ge(S("gate_neg"), 1)
            pe.wait_ge(S("consts"), 10)
            for h in range(AH):
                mm(PS[:, h, 0:SEQ], lhsT=sel[:, h, :], rhs=gneg, start=True, stop=False, skip_group_check=True)
                mm(PS[:, h, SEQ:SEQ + P], lhsT=sel[:, h, :], rhs=gneg[:, P:SEQ], start=False, stop=False, skip_group_check=True)
                mm(PS[:, h, 0:P], lhsT=ident[:, :], rhs=mask_kq[:, :], start=False, stop=False, skip_group_check=True)
                mm(PS[:, h, SEQ:SEQ + P], lhsT=ident[:, :], rhs=mask_kq[:, :], start=False, stop=True,
                   skip_group_check=True).then_inc(S("decay_arg"), 1)
            pe.wait_ge(S("mqT"), 1)
            pe.wait_ge(S("gN"), 1)
            for h in range(AH):
                mm(PS[:, 4 + h, 0:SEQ], lhsT=kT[0:AQ, h, 0:P], rhs=qT[0:AQ, h, :], start=True, stop=True)
                mm(PS[:, 4 + h, SEQ:SEQ + P], lhsT=kT[0:AQ, h, P:SEQ], rhs=qT[0:AQ, h, P:SEQ], start=True,
                   stop=True).then_inc(S("kq"), 1)
            for h in range(AH):
                pe.wait_ge(S("weights"), h + 1)
                if h == 0:
                    pe.wait_ge(S("decay"), AH)
                mm(PS[:, h, 0:VW], lhsT=PmT[:, h, 0:P], rhs=v1[:, 0, h, :], start=True, stop=True)
                mm(PS[:, h, 256:256 + VW], lhsT=PmT[:, h, P:SEQ], rhs=v1[:, 0, h, :], start=True, stop=False)
                mm(PS[:, h, 256:256 + VW], lhsT=PmT[:, h, SEQ:SEQ + P], rhs=v1[:, 1, h, :], start=False,
                   stop=True).then_inc(S("num"), 1)
            mem_attention(0, memkT[:, 0], mqT, "mqT", 1)
            pe.wait_ge(S("h_out"), 1)
            mem_attention_out(0)
            pe.wait_ge(S("mixed"), 1)
            transposes("mix0")
            evicted("mix0")
            project_out(("aout0", "aout1"))
            pe.wait_ge(S("scaled"), nidx["x1"] + 1)
            transposes("x1")
            def three(out_, xh, xl, wh, wl, first, last):
                mm(out_, lhsT=xh, rhs=wh, start=first, stop=False)
                mm(out_, lhsT=xh, rhs=wl, start=False, stop=False)
                return mm(out_, lhsT=xl, rhs=wh, start=False, stop=last)

            def cut_weights(i, n, r=None):
                pe.wait_ge(S("lows"), count(i, PER, r, 3, cuts_before(i) + n + 1))
                return n % CUTS

            def gate_up(i, b, nt, r=None):
                for h in range(2):
                    j = cut_weights(i, gu_item(b) + h, r)
                    for k in range(KH):
                        for t in range(nt):
                            x_ = slice(t * P, (t + 1) * P)
                            last = three(PS[:, t, :], xhi[:, h * KH + k, x_], xlo[:, h * KH + k, x_], whi[:, j, k * W:(k + 1) * W],
                                         wlo[:, j, k * W:(k + 1) * W], h == 0 and k == 0, h == 1 and k == KH - 1)
                    last.then_inc(S("through"), 1)

            def down(i, b, nt, r=None):
                j = cut_weights(i, dn_item(b), r)
                pe.wait_ge(S("h_low"), count(i, NB, r, 1, blocks_before(i) + b + 1))
                for kk in range(2):
                    for t in range(nt):
                        for hh in range(2):
                            x_, c0 = slice(t * P, (t + 1) * P), kk * D + hh * HD
                            last = three(PS[:, 4 + 2 * t + hh, :], hhi[:, kk, x_], hlo[:, kk, x_], whi[:, j, c0:c0 + HD],
                                         wlo[:, j, c0:c0 + HD], b == 0 and kk == 0, b == NB - 1 and kk == 1)
                last.then_inc(S("through"), 1)

            def turn_hidden(i, b, nt, r=None):
                pe.wait_ge(S("h_ready"), count(i, NB, r, 1, blocks_before(i) + b + 1))
                for kk in range(2):
                    for t in range(nt):
                        last = tr(PS[:, 3, kk * SEQ + t * P:kk * SEQ + (t + 1) * P], hn[:, t, kk * P:(kk + 1) * P])
                last.then_inc(S("h_turned"), 1)

            def swiglu(i, nt, after_first=None, after_last=None, at_end=None):
                gate_up(i, 0, nt)
                if after_first:
                    after_first()
                turn_hidden(i, 0, nt)
                gate_up(i, 1, nt)
                down(i, 0, nt)
                turn_hidden(i, 1, nt)
                with pe.Fori(0, len(REST)) as r:
                    for b in (2, 3):
                        gate_up(i, b, nt, r)
                        down(i, b - 1, nt, r)
                        turn_hidden(i, b, nt, r)
                for b in (NB - 2, NB - 1):
                    gate_up(i, b, nt)
                    if b == NB - 1 and after_last:
                        after_last()
                    down(i, b - 1, nt)
                    turn_hidden(i, b, nt)
                if at_end:
                    at_end()
                down(i, NB - 1, nt)

            pe.wait_ge(S("x1_low"), 4)
            swiglu(None, NT)
            pe.wait_ge(S("scaled"), nidx["x2"] + 1)
            transposes("x2")
            evicted("x2")
            w = slot("dkv", KD, KVL + ROPE)
            natural([(4, 0), (5, 0)], xTk, w, KVL + ROPE).then_inc(S("through"), 1)
            w = slot("cq", KD, QL)
            natural([(6, 0), (7, 0)], xT, w, QL).then_inc(S("through"), 1)
            w = slot("mq", KD, MW)
            natural([(0, 0), (0, MW)], xT, w, MW).then_inc(S("through"), 1)
            pe.wait_ge(S("scaled"), nidx["ckv"] + 1)
            for k in range(2):
                for t in range(NT):
                    last = tr(PS[:, 1, k * SEQ + t * P:k * SEQ + (t + 1) * P], zS[:, t, k * P:(k + 1) * P])
            last.then_inc(S("lat_t"), 1)
            pe.wait_ge(S("scaled"), nidx["cq"] + 1)
            for k in range(3):
                for t in range(NT):
                    last = tr(PS[:, 2 + k // 2, (k % 2) * SEQ + t * P:(k % 2) * SEQ + (t + 1) * P], cqS[:, t, k * P:(k + 1) * P])
            last.then_inc(S("lat_t"), 1)
            pe.wait_ge(S("scaled"), nidx["mq1"] + 1)
            for pair in range(2):
                for t in range(NT):
                    last = tr(PS[:, 4, pair * SEQ + t * P:pair * SEQ + (t + 1) * P], mqS1[:, t, pair * P:(pair + 1) * P])
            last.then_inc(S("lat_t"), 1)
            pe.wait_ge(S("lat_out"), 3)
            for u, (kind, t, g, bank) in enumerate(UNITS):
                if u == 0:
                    w = slot("ukv", 2, BH * (NOPE + VH))
                if u == 6:
                    w = slot("uq", 3, BH * QKH)
                if u >= 8:
                    pe.wait_ge(S("unit_out"), u - 8 + 1)
                src, nk, n = (ckvT, 2, 2 * (NOPE + VH)) if kind == "kv" else (cqT, 3, 2 * QKH)
                for k in range(nk):
                    last = mm(PS[:, bank, 0:n], lhsT=src[:, k, t * P:(t + 1) * P], rhs=w[:, k, g * n:(g + 1) * n],
                              start=(k == 0), stop=(k == nk - 1))
                last.then_inc(S("through") if u % 6 == 5 else S("unit"), 1)
            for u, (dst, rws, bank) in enumerate(KQT):
                who, part = ("k", u) if u < 6 else ("q", u - 6)
                if part == 0:
                    pe.wait_ge(S("roped"), 1 if who == "k" else 2)
                if u == 0:
                    pe.wait_ge(S("unit_out"), 12)
                if u >= 8:
                    pe.wait_ge(S("kq_even" if u % 2 == 0 else "kq_odd"), (u - 8) // 2 + 1)
                src = (kF if who == "k" else qF).rearrange("p (t h) n -> p t h n", t=NT)
                for h in (2 * (part % 3), 2 * (part % 3) + 1):
                    for t in range(NT):
                        v = src[:, t, h, 0:NOPE] if part < 3 else src[:, t, h, NOPE:QKH]
                        last = tr(PS[0:rws, bank, (h % 2) * SEQ + t * P:(h % 2) * SEQ + (t + 1) * P], v)
                last.then_inc(S("kq_t"), 1)
            pe.wait_ge(S("kq_even"), 6)
            pe.wait_ge(S("kq_odd"), 6)
            for h in range(BH):
                for t, (c0, c1) in enumerate(((0, P), (P, 3 * P))):
                    nk = (t + 1) * P
                    mm(PS[:, h, c0:c1], lhsT=qTn[:, h, t * P:(t + 1) * P], rhs=kTn[:, h, 0:nk], start=True, stop=False)
                    mm(PS[:, h, c1 - P:c1], lhsT=ident[:, :], rhs=mask_qk[:, :], start=False, stop=False)
                    last = mm(PS[:, h, c0:c1], lhsT=qTr[:, h, t * P:(t + 1) * P], rhs=kTr[:, h, 0:nk], start=False, stop=True)
                last.then_inc(S("att_scores"), 1)
            for u, bank in enumerate(PTB):
                for f in range(4 * u, min(4 * u + 4, 3 * BH)):
                    h, b = f // 3, f % 3
                    if b == 0 or f == 4 * u:
                        pe.wait_ge(S("att_exp"), BH if u >= 2 else h + 1)
                    last = tr(PS[:, bank, (f % 4) * P:(f % 4 + 1) * P], Pb[:, h, b * P:(b + 1) * P])
                last.then_inc(S("att_pt"), 1)
            pe.wait_ge(S("att_pt_even"), 3)
            pe.wait_ge(S("att_pt_odd"), 2)
            for t in range(NT):
                for h in range(BH):
                    c = t * BH + h
                    for m in range(t + 1):
                        last = mm(PS[:, 3 + c // 4, (c % 4) * VH:(c % 4 + 1) * VH], lhsT=PT[:, h, (t + m) * P:(t + m + 1) * P],
                                  rhs=vF[:, m, h, :], start=(m == 0), stop=(m == t))
            last.then_inc(S("att_out"), 1)
            pe.wait_ge(S("att_mixed"), 1)
            mem_attention(1, memkT[:, 1], mqT1, "lat_out", 3)
            mem_attention_out(1)
            pe.wait_ge(S("mixed"), 2)
            transposes("mix1")
            evicted("mix1")
            project_out(("bout0", "bout1"))
            pe.wait_ge(S("scaled"), nidx["x3"] + 1)
            transposes("x3")
            evicted("x3")
            pe.wait_ge(S("router_in"), 16)
            natural([(2, 0), (2, NE)], xT, router, NE).then_inc(S("logits"), 1)
            pe.wait_ge(S("chosen"), 1)
            mm(PS[:, 3, 0:NE], lhsT=before[:, :], rhs=chosen[:, 0], start=True, stop=True)
            mm(PS[:, 3, NE:2 * NE], lhsT=ones[:, :], rhs=chosen[:, 0], start=True, stop=False)
            mm(PS[:, 3, NE:2 * NE], lhsT=before[:, :], rhs=chosen[:, 1], start=False, stop=True)
            mm(PS[:, 3, 2 * NE:3 * NE], lhsT=ones[:, :], rhs=chosen[:, 0], start=True, stop=False)
            mm(PS[:, 3, 2 * NE:3 * NE], lhsT=ones[:, :], rhs=chosen[:, 1], start=False, stop=True).then_inc(S("ranks"), 1)

            def gather(last_sem="gathered"):
                for k in range(KD):
                    for t in range(NT):
                        last = mm(PS[:, 6 + k // 4, (k % 4) * CAP:(k % 4 + 1) * CAP], lhsT=xn[:, t, k * P:(k + 1) * P],
                                  rhs=Sx[:, t, :], start=(t == 0), stop=(t == NT - 1))
                last.then_inc(S("gathered"), 1)

            def combine(i):
                pe.wait_ge(S("y_ready"), i + 1)
                pe.wait_ge(S("G_ready"), i + 1)
                for t in range(NT):
                    for hh in range(2):
                        last = mm(PS[:, (6, 1)[t] + hh, :], lhsT=G[:, t, :], rhs=y[:, hh * HD:(hh + 1) * HD],
                                  start=True, stop=True)
                    last.then_inc(S("combined"), 1)

            pe.wait_ge(S("G_ready"), 1)
            for hh in range(2):
                mm(PS[:, 4 + hh, :], lhsT=G[:, 0, :], rhs=xn[:, 0, hh * HD:(hh + 1) * HD], start=True, stop=True)
            pe.wait_ge(S("routed"), 1)
            passes = pe.value_load(cnt_i[0:1, 0:1], min_val=1, max_val=PASSES)
            pe.wait_ge(S("dispatch"), 1)
            gather()
            with pe.Fori(0, passes) as p:
                with pe.Fori(0, NE) as e:
                    i = p * NE + e

                    def next_tokens():
                        pe.wait_ge(S("dispatch"), i + 2)
                        pe.wait_ge(S("added"), i * NT + NT)
                        gather()

                    def turn_gates():
                        for t in range(NT):
                            last = tr(PS[:, 2, t * P:(t + 1) * P], Sw[:, t, :])
                        last.then_inc(S("G_turned"), 1)

                    pe.wait_ge(S("xlo_ready"), i + 1)
                    swiglu(i, 1, lambda: combine(i), next_tokens, turn_gates)
            pe.wait_ge(S("xlo_ready"), passes * NE + 1)
            combine(passes * NE)

        @block.vector
        def _(dve):
            v = nc.vector
            chain = [0]

            def then(ins):
                chain[0] += 1
                ins.then_inc(S("dve_step"), 1)
                dve.wait_ge(S("dve_step"), chain[0])

            def norm(name, gain=None):
                e, (src, dst, w), g = nidx[name], nview[name], groups(name)
                dst = src if dst is None else dst
                if name not in OWN_SUMS:
                    dve.wait_ge(S("squares"), squares_no[name])
                    v.tensor_reduce(shaped(sums(name), name), sq_of(name), AX.X, ALU.add).then_inc(S("sums"), 1)
                dve.wait_ge(S("rstds"), e + 1)
                if gain is not None:
                    for k in range(g):
                        last = v.scalar_tensor_tensor(out=dst[:, k], in0=src[:, k], scalar=rstd[:, e % 2, k:k + 1], in1=gain,
                                                      op0=ALU.mult, op1=ALU.mult)
                elif w == D:
                    for t in range(NT):
                        last = v.tensor_scalar(dst[:, t], src[:, t], rstd[:, e % 2, t:t + 1], None, ALU.mult)
                else:
                    last = v.tensor_tensor(dst, src, bcast(shaped(rstd[:, e % 2, :], name), w), ALU.mult)
                last.then_inc(S("scaled"), 1)

            def evict(name):
                i, (_, _, bank, dsts) = tidx[name], TR[tidx[name]]
                for b in (1, 3):
                    dve.wait_ge(S("transposed"), 4 * i + b + 1)
                    for dst, g in dsts:
                        for k in (2 * b, 2 * b + 1):
                            s, src = k_gain(name, g, k), PS[:, bank + b, (k % 2) * SEQ:(k % 2 + 1) * SEQ]
                            if s is None:
                                last = v.tensor_copy(dst[:, k, :], src)
                            else:
                                last = v.tensor_scalar(dst[:, k, :], src, s, None, ALU.mult)
                    last.then_inc(S("evicted_odd"), 1)

            def lo_of(i, n, r=None):
                dve.wait_ge(S("highs"), count(i, PER, r, 3, cuts_before(i) + n + 1))
                h = ((E0 if i is not None else 0) + n) % SLOTS
                v.tensor_tensor(wlo[:, n % CUTS, :], ring[:, h * SLOT:(h + 1) * SLOT], whi[:, n % CUTS, :].bitcast(F32),
                                ALU.subtract).then_inc(S("lows"), 1)

            def block(i, b, nt, r=None):
                for n in cut_item(b):
                    lo_of(i, n, r)
                dve.wait_ge(S("silu"), count(i, NB, r, 1, blocks_before(i) + b + 1))
                v.tensor_tensor(hn[:, 0:nt], PS[:, 0:nt, FB:2 * FB], sil[:, 0:nt], ALU.mult).then_inc(S("h_ready"), 1)
                if 3 * b + 3 < PER:
                    lo_of(i, 3 * b + 3, r)
                if b == 0 and i is not None:
                    add(i, "added")
                if b == 1 and i is not None:
                    for t in range(NT):
                        v.tensor_scalar(Sx[:, t], iota, keys[:, t, bass.ds(i + 1, 1)], None, ALU.is_equal)
                        last = v.tensor_scalar(Sw[:, t], iota, keys[:, t, bass.ds(i, 1)], combs[:, t, bass.ds(i, 1)],
                                               ALU.is_equal, ALU.mult)
                    last.then_inc(S("dispatch"), 1)
                if b == NB - 1 and i is not None:
                    gathered(i + 1)
                dve.wait_ge(S("h_high"), count(i, NB, r, 1, blocks_before(i) + b + 1))
                src = PS[:, 3, :].rearrange("p (a s) -> p a s", a=2)
                v.tensor_tensor(hlo[:, :, 0:nt * P], src[:, :, 0:nt * P], hhi[:, :, 0:nt * P].bitcast(F32),
                                ALU.subtract).then_inc(S("h_low"), 1)

            def swiglu(i, nt):
                lo_of(i, 0)
                for b in (0, 1):
                    block(i, b, nt)
                with dve.Fori(0, len(REST)) as r:
                    for b in (2, 3):
                        block(i, b, nt, r)
                for b in (NB - 2, NB - 1):
                    block(i, b, nt)

            def mem_max(l, bank):
                dve.wait_ge(S("mem_scores"), l + 1)
                for t in range(NT):
                    src = PS[:, bank + 2 * t:bank + 2 * t + 2, :].rearrange("p par (pair m) -> p pair par m", pair=2)
                    last = v.tensor_reduce(smax[:, t * MH:(t + 1) * MH].rearrange("p (a b) -> p a b", a=2), src, AX.X, ALU.max)
                then(last)
                v.tensor_scalar(sbias[:, 0:8], smax[:, 0:8], -float(MD) ** -0.5, None, ALU.mult).then_inc(S("mem_max"), 1)

            def mem_turned(l):
                for b in range(2):
                    dve.wait_ge(S("mem_pt"), 4 * l + 2 * b + 2)
                    v.tensor_copy(mPT[:, b, 2:4].rearrange("p h m q -> p (h m q)"), PS[:, 2 * b + 1, :]).then_inc(S("mem_pt_odd"), 1)

            def mem_out(l):
                dve.wait_ge(S("mem_exp"), l + 1)
                then(v.reciprocal(srec[:, 0:8], ssum[:, 0:8]))
                dve.wait_ge(S("mem_out"), l + 1)
                v.tensor_tensor(nat(mix[:, :, D - MW:D], MD), PS[:, 4, :].rearrange("p (t h n) -> p t h n", t=NT, h=MH),
                                bcast(srec[:, 0:8].rearrange("p (a b) -> p a b", a=NT), MD), ALU.mult).then_inc(S("mixed"), 1)

            def add_out(n):
                dve.wait_ge(S("through"), n)
                last = v.tensor_tensor(xres[:, :, :].rearrange("p t (a b) -> p (t a) b", a=2), PS[:, 4:8, :],
                                       xres[:, :, :].rearrange("p t (a b) -> p (t a) b", a=2), ALU.add)
                last.then_inc(S("x_sum"), 1)

            norm("mem")
            norm("x0")
            dve.wait_ge(S("gains_t"), 1)
            v.tensor_copy(gains[:, :], PS[:, 7, 0:NG]).then_inc(S("gains"), 1)
            v.tensor_copy(hg[:, :], PS[:, 6, 0:2 * QKH]).then_inc(S("gains"), 1)
            dve.wait_ge(S("gains"), 2)
            evict("mem")
            evict("x0")
            dve.wait_ge(S("kS"), 2)
            norm("mk0")
            norm("mk1")
            dve.wait_ge(S("gate_in"), 2)
            v.scalar_tensor_tensor(out=gt, in0=gf, scalar=-1.0, in1=gf, op0=ALU.mult, op1=ALU.max).then_inc(S("gate_abs"), 1)
            v.memset(gone, 1.0)
            then(v.tensor_scalar(gf, gf, 0.0, None, ALU.min))
            dve.wait_ge(S("gate_exp"), 2)
            then(v.tensor_tensor(glf, gf, gt, ALU.subtract))
            then(v.tensor_tensor_scan(gG, gone, glf, 0.0, ALU.mult, ALU.add))
            then(v.tensor_tensor(ga, gi, gG, ALU.subtract))
            then(v.tensor_tensor_scan(gM, ga, ga, 0.0, ALU.max, ALU.max))
            v.tensor_tensor(gm, gG, gM, ALU.add).then_inc(S("gate_m"), 1)
            v.tensor_scalar(gneg, gM, -1.0, None, ALU.mult).then_inc(S("gate_neg"), 1)
            norm("mq0")
            dve.wait_ge(S("through"), through("k"))
            for b in range(2):
                last = v.tensor_scalar(kT[0:AQ, 2 * b:2 * b + 2, :], PS[0:AQ, b, :].rearrange("p (h s) -> p h s", h=2),
                                       float(AQ) ** -0.5, None, ALU.mult)
            last.then_inc(S("kT"), 1)
            v.memset(v1[:, :, :, AV:VW], 1.0)
            for half in range(2):
                dve.wait_ge(S("through"), through(f"v{half}"))
                for t in range(NT):
                    last = v.tensor_copy(v1[:, t, 2 * half:2 * half + 2, 0:AV],
                                         PS[:, 2 + 2 * half + t, 0:hv].rearrange("p (h n) -> p h n", h=2))
                last.then_inc(S("v_out"), 1)
            for l in range(2):
                dve.wait_ge(S("memk_t"), l + 1)
                g = gcol[f"memk{l}"]
                v.tensor_scalar(memkT[:, l], PS[:, 2 + l, :].rearrange("p (a s) -> p a s", a=2), gains[:, g:g + 1], None,
                                ALU.mult).then_inc(S("memkT"), 1)
            dve.wait_ge(S("mq_t"), 1)
            g = gcol["memq0"]
            v.tensor_scalar(mqT, PS[:, 4, :].rearrange("p (a s) -> p a s", a=2), gains[:, g:g + 1], None,
                            ALU.mult).then_inc(S("mqT"), 1)
            dve.wait_ge(S("gate_t"), 1)
            v.tensor_copy(gN[:, :, :, :].rearrange("p a b c -> p (a b c)"), PS[:, 5, 0:2 * NT * AH]).then_inc(S("gN"), 1)
            dve.wait_ge(S("scaled"), nidx["mq0"] + 1)
            for h in range(AH):
                dve.wait_ge(S("decay"), h + 1)
                dve.wait_ge(S("kq"), h + 1)
                v.tensor_tensor(PmT[:, h, :], PS[:, 4 + h, 0:384], Dm[:, h, :], ALU.mult).then_inc(S("weights"), 1)
            dve.wait_ge(S("num"), AH)
            dv = den[:, :].rearrange("p (t h) -> p t h", t=NT)
            src = PS[:, 0:AH, :].rearrange("p h (t n) -> p t h n", t=NT)
            then(v.tensor_copy(dv, src[:, :, :, AV]))
            then(v.scalar_tensor_tensor(out=dv, in0=dv, scalar=-1.0, in1=dv, op0=ALU.mult, op1=ALU.max))
            then(v.tensor_tensor(dv, dv, gN[:, 1], ALU.max))
            then(v.reciprocal(den[:, :], den[:, :]))
            hview = nat(mix[:, :, 0:avw], AV)
            for t in range(NT):
                last = v.tensor_tensor(hview[:, t], src[:, t, :, 0:AV], bcast(dv[:, t], AV), ALU.mult)
            last.then_inc(S("h_out"), 1)
            mem_max(0, 4)
            mem_turned(0)
            norm("hm")
            dve.wait_ge(S("scaled"), nidx["hm"] + 1)
            dve.wait_ge(S("og"), 2)
            v.tensor_tensor(mix[:, :, 0:avw], mix[:, :, 0:avw], og, ALU.mult)
            mem_out(0)
            evict("mix0")
            add_out(through("aout1"))
            dve.wait_ge(S("x_sum"), 1)
            norm("x1")
            for k in range(KD):
                if k % 2 == 0:
                    dve.wait_ge(S("x1_high"), k // 2 + 1)
                last = v.scalar_tensor_tensor(out=xlo[:, k, :], in0=PS[:, k // 2, (k % 2) * SEQ:(k % 2 + 1) * SEQ],
                                              scalar=k_gain("x1", "ffn0", k), in1=xhi[:, k, :].bitcast(F32),
                                              op0=ALU.mult, op1=ALU.subtract)
                if k % 2 == 1:
                    last.then_inc(S("x1_low"), 1)
            TWO_PI = 2.0 * np.pi
            part, left = [], TWO_PI
            for n in range(3):
                step = 2.0 ** (np.floor(np.log2(left)) - 7)
                part.append(float(np.floor(left / step) * step))
                left -= part[-1]
            part.append(float(np.float32(left)))
            HALF_TURN = 3.1415925
            dve.wait_ge(S("pos_in"), 16)
            dve.wait_ge(S("freqs"), 1)
            then(v.tensor_copy(posf[:, :], posi[:, :]))
            for t in range(NT):
                last = v.tensor_scalar(rot[:, 0, t], invf[:, :], posf[:, t:t + 1], None, ALU.mult)
            then(last)
            then(v.tensor_scalar(roti[:, :, :], rot[:, 0], float(1.0 / TWO_PI), None, ALU.mult))
            then(v.tensor_copy(rot[:, 1], roti[:, :, :]))
            for c in part:
                then(v.scalar_tensor_tensor(out=rot[:, 0], in0=rot[:, 1], scalar=-c, in1=rot[:, 0], op0=ALU.mult, op1=ALU.add))
            v.tensor_scalar(rot[:, 2], rot[:, 0], HALF_TURN, -HALF_TURN, ALU.min, ALU.max)
            then(v.tensor_scalar(rot[:, 3], rot[:, 0], float(np.pi / 2), None, ALU.add))
            then(v.tensor_scalar(rot[:, 1], rot[:, 3], float(np.pi), -TWO_PI, ALU.is_gt, ALU.mult))
            then(v.tensor_tensor(rot[:, 3], rot[:, 3], rot[:, 1], ALU.add))
            v.tensor_scalar(rot[:, 3], rot[:, 3], HALF_TURN, -HALF_TURN, ALU.min, ALU.max).then_inc(S("angles"), 1)
            swiglu(None, NT)
            add_out(FFN0 + PER)
            dve.wait_ge(S("x_sum"), 2)
            norm("x2")
            evict("x2")
            dve.wait_ge(S("zS"), 1)
            kF4 = kF.rearrange("p (t h) n -> p t h n", t=NT)
            qF4 = qF.rearrange("p (t h) n -> p t h n", t=NT)

            def per_head(ap, n):
                dims = [list(d) for d in ap.ap]
                return bass.AP(ap.tensor, ap.offset, dims[:-1] + [[0, n]] + dims[-1:])

            for t in range(NT):
                last = v.tensor_copy(kF4[:, t, :, NOPE:QKH], per_head(zS[:, t, KVL:KVL + ROPE], BH))
            last.then_inc(S("k_rope_in"), 1)
            norm("ckv")
            norm("cq")
            norm("mq1")
            for n, (dst, name, view, nk) in enumerate((
                    (ckvT, "kv_a", PS[:, 1:2, :], 2), (cqT, "q_a", PS[:, 2:4, :], 3), (mqT1, "memq1", PS[:, 4:5, :], 2))):
                dve.wait_ge(S("lat_t"), n + 1)
                for k in range(nk):
                    g = gcol[name] + (k if n < 2 else 0)
                    last = v.tensor_scalar(dst[:, k], view[:, k // 2, (k % 2) * SEQ:(k % 2 + 1) * SEQ], gains[:, g:g + 1], None, ALU.mult)
                last.then_inc(S("lat_out"), 1)
            dve.wait_ge(S("sincos"), 2)
            sin, cos = rot[:, 4], rot[:, 5]
            tmp = xT[:, :, :].rearrange("p a b -> p (a b)")[:, 0:4 * NT * BH * HR].rearrange(
                "p (q t h n) -> p q t h n", q=4, t=NT, h=BH)
            for name, full, g0 in (("kh", kF4, 0), ("qh", qF4, QKH)):
                norm(name, hg[:, g0:g0 + QKH])
                dve.wait_ge(S("scaled"), nidx[name] + 1)
                x1, x2 = full[:, :, :, NOPE:NOPE + HR], full[:, :, :, NOPE + HR:QKH]
                for q, (a, b) in enumerate(((x1, cos), (x2, sin), (x2, cos), (x1, sin))):
                    last = v.tensor_tensor(tmp[:, q], a, per_head(b, BH), ALU.mult)
                then(last)
                v.tensor_tensor(x1, tmp[:, 0], tmp[:, 1], ALU.subtract)
                v.tensor_tensor(x2, tmp[:, 2], tmp[:, 3], ALU.add).then_inc(S("roped"), 1)
            for u, (dst, n, bank) in enumerate(KQT):
                if u % 2 == 1:
                    dve.wait_ge(S("kq_t"), u + 1)
                    v.tensor_copy(dst, PS[0:n, bank, :].rearrange("p (h s) -> p h s", h=2)).then_inc(S("kq_odd"), 1)
            dve.wait_ge(S("att_scores"), BH)
            v.tensor_reduce(smax[:, 0:BH], PS[:, 0:BH, 0:P], AX.X, ALU.max)
            then(v.tensor_reduce(smax[:, BH:2 * BH], PS[:, 0:BH, P:3 * P], AX.X, ALU.max))
            v.tensor_scalar(sbias[:, 0:2 * BH], smax[:, 0:2 * BH], -float(QKH) ** -0.5, None, ALU.mult).then_inc(S("att_max"), 1)
            for u, bank in enumerate(PTB):
                if u % 2 == 1:
                    dve.wait_ge(S("att_pt"), u + 1)
                    v.tensor_copy(PT.rearrange("p a b -> p (a b)")[:, 512 * u:512 * u + 512], PS[:, bank, :]).then_inc(S("att_pt_odd"), 1)
            dve.wait_ge(S("att_exp"), BH)
            then(v.reciprocal(srec[:, 0:2 * BH], ssum[:, 0:2 * BH]))
            dve.wait_ge(S("att_out"), 1)
            for t in range(NT):
                blocks = PS[:, 3:6, :].rearrange("p a b -> p (a b)")[:, t * BH * VH:(t + 1) * BH * VH]
                last = v.tensor_tensor(mix[:, t, 0:BH * VH].rearrange("p (h n) -> p h n", h=BH),
                                       blocks.rearrange("p (h n) -> p h n", h=BH), bcast(srec[:, t * BH:(t + 1) * BH], VH), ALU.mult)
            last.then_inc(S("att_mixed"), 1)
            mem_max(1, 4)
            mem_turned(1)
            mem_out(1)
            evict("mix1")
            add_out(through("bout1"))
            dve.wait_ge(S("x_sum"), 3)
            norm("x3")
            evict("x3")
            dve.wait_ge(S("logits"), 1)
            dve.wait_ge(S("iota"), 1)
            then(v.tensor_copy(lg, PS[:, 2, 0:NT * NE].rearrange("p (t n) -> p t n", t=NT)))
            for t in range(NT):
                last = v.max(m8[:, t], lg[:, t])
            then(last)
            for t in range(NT):
                v.tensor_tensor(gt2[:, t:t + 1], m8[:, t, 1:2], m8[:, t, 0:1], ALU.subtract)
                last = v.max_index(idx8[:, t], m8[:, t], lg[:, t])
            last.then_inc(S("top2"), 1)
            dve.wait_ge(S("top2"), 1)
            then(v.tensor_copy(idxf, idx8))
            for t in range(NT):
                v.tensor_scalar(oh1[:, t], iota[:, 0:NE], idxf[:, t, 0:1], None, ALU.is_equal)
                last = v.tensor_scalar(oh2[:, t], iota[:, 0:NE], idxf[:, t, 1:2], None, ALU.is_equal)
            then(last)
            v.tensor_tensor(chosen, oh1, oh2, ALU.add).then_inc(S("chosen"), 1)
            dve.wait_ge(S("gate2_exp"), 1)
            then(v.tensor_scalar(gt2[:, 4:6], gt2[:, 2:4], 1.0, None, ALU.add))
            then(v.reciprocal(gt2[:, 6:8], gt2[:, 4:6]))
            then(v.tensor_tensor(gt2[:, 8:10], gt2[:, 6:8], gt2[:, 2:4], ALU.mult))
            for t in range(NT):
                last = v.tensor_scalar(oh1[:, t], oh1[:, t], gt2[:, 6 + t:7 + t], None, ALU.mult)
            then(last)
            for t in range(NT):
                for q in range(PASSES + 1):
                    last = v.scalar_tensor_tensor(out=combs[:, t, q * NE:(q + 1) * NE], in0=oh2[:, t], scalar=gt2[:, 8 + t:9 + t],
                                                  in1=oh1[:, t], op0=ALU.mult, op1=ALU.add)
            dve.wait_ge(S("chosen"), 1)
            dve.wait_ge(S("ranks"), 1)
            then(v.scalar_tensor_tensor(out=keys[:, :, 0:NE], in0=PS[:, 3, 0:NT * NE].rearrange("p (t n) -> p t n", t=NT),
                                        scalar=4096.0, in1=chosen, op0=ALU.add, op1=ALU.mult))
            then(v.tensor_scalar(keys[:, :, 0:NE], keys[:, :, 0:NE], -4096.0, None, ALU.add))
            for q in range(1, PASSES + 1):
                last = v.tensor_scalar(keys[:, :, q * NE:(q + 1) * NE], keys[:, :, 0:NE], -float(q * CAP), None, ALU.add)
            then(last)
            then(v.tensor_reduce(gt2[:, 10:11], PS[:, 3, 2 * NE:3 * NE], AX.X, ALU.max))
            then(v.tensor_scalar(gt2[:, 11:12], gt2[:, 10:11], float(CAP), 1.0, ALU.is_gt, ALU.add))
            for q in range(2, PASSES):
                then(v.scalar_tensor_tensor(out=gt2[:, 11:12], in0=gt2[:, 10:11], scalar=float(q * CAP), in1=gt2[:, 11:12],
                                            op0=ALU.is_gt, op1=ALU.add))
            v.tensor_copy(cnt_i[:, :], gt2[:, 11:12]).then_inc(S("routed"), 1)
            for t in range(NT):
                last = v.tensor_scalar(Sx[:, t], iota, keys[:, t, 0:1], None, ALU.is_equal)
            last.then_inc(S("dispatch"), 1)
            dve.wait_ge(S("routed"), 1)
            passes = dve.value_load(cnt_i[0:1, 0:1], min_val=1, max_val=PASSES)

            def gathered(i):
                dve.wait_ge(S("gathered"), i + 1)
                for b in range(2):
                    g = gcol["ffn1"] + 4 * b
                    last = v.tensor_tensor(xe[:, 4 * b:4 * b + 4, :], PS[:, 6 + b, 0:4 * CAP].rearrange("p (k n) -> p k n", k=4),
                                           bcast(gains[:, g:g + 4], CAP), ALU.mult)
                last.then_inc(S("xe_ready"), 1)
                dve.wait_ge(S("xhi_ready"), i + 1)
                v.tensor_tensor(xlo[:, :, 0:CAP], xe, xhi[:, :, 0:CAP].bitcast(F32), ALU.subtract).then_inc(S("xlo_ready"), 1)

            def add(i, sem):
                for t in range(NT):
                    dve.wait_ge(S("combined"), i * NT + (t + 1))
                    xv = xres[:, t].rearrange("p (a b) -> p a b", a=2)
                    v.tensor_tensor(xv, PS[:, (6, 1)[t]:(6, 1)[t] + 2, :], xv, ALU.add).then_inc(S(sem), 1)

            gathered(0)
            with dve.Fori(0, passes) as p:
                with dve.Fori(0, NE) as e:
                    i = p * NE + e
                    swiglu(i, 1)
                    dve.wait_ge(S("G_turned"), i + 1)
                    v.tensor_copy(G, PS[:, 2, 0:SEQ].rearrange("p (t s) -> p t s", t=NT)).then_inc(S("G_ready"), 1)
            add(passes * NE, "x_final")


_NAMES = ["x", "mem", "positions", "a_norm", "a_w_in", "a_gate_bias", "a_head_norm", "a_w_out", "b_norm", "b_w_in",
          "b_q_a_norm", "b_w_uq", "b_q_head_norm", "b_w_out", "kv_norm", "w_dkv", "kv_a_norm", "w_ukv", "k_head_norm",
          "mem_norm", "mem_w_kv", "mem_q_norm", "mem_k_norm", "ffn_norm", "dense_w_gate_up", "dense_w_down",
          "moe_router", "moe_w_gate_up", "moe_w_down"]


def kernel(**inputs):
    import concourse.bacc as bacc
    from concourse.bass_utils import run_bass_kernel_spmd

    nc = bacc.Bacc("TRN2", target_bir_lowering=False, num_devices=1)
    arrays, views = {}, {}
    for name in _NAMES:
        a = np.ascontiguousarray(inputs[name])
        arrays[f"in_{name}"] = a
        views[name] = nc.dram_tensor(f"in_{name}", a.shape, mybir.dt.from_np(a.dtype), kind="ExternalInput").ap()
    shape = arrays["in_x"].shape
    out = nc.dram_tensor("out_x", shape, F32, kind="ExternalOutput").ap()
    build(nc, views, out)
    r = run_bass_kernel_spmd(nc, [arrays], core_ids=[0])
    return r.results[0]["out_x"]
```

```python
from contextlib import ExitStack

import numpy as np

import concourse.bass as bass
from concourse import mybir

ALU = mybir.AluOpType
ACT = mybir.ActivationFunctionType
AX = mybir.AxisListType
F32 = mybir.dt.float32
FR = mybir.dt.float32r
I32 = mybir.dt.int32
U32 = mybir.dt.uint32

P = 128
EPS = 1e-6
SLOTS = 6
SLOT = 2048
POOL_COLS = 384
CUTS = 3
CAP = 128
NEG = -float(2.0 ** 100)
ROPE_THETA = 10000.0


def build(nc, T, out):
    SEQ, D = T["x"].shape[1:]
    NT = SEQ // P
    KD = D // P
    NMEM = T["mem"].shape[1]
    AH = T["a_gate_bias"].shape[1] // 2
    AV = T["a_head_norm"].shape[1] // AH
    MH, MD = 4, T["mem_q_norm"].shape[1]
    MW = MH * MD
    AIN = T["a_w_in"].shape[2]
    AQ = (AIN - 2 * AH * AV - 2 * AH - MW) // (2 * AH)
    QL = T["b_q_a_norm"].shape[1]
    KVL = T["kv_a_norm"].shape[0]
    QKH = T["b_q_head_norm"].shape[1]
    BH = T["b_w_uq"].shape[2] // QKH
    ROPE = T["w_dkv"].shape[1] - KVL
    NOPE = QKH - ROPE
    VH = T["w_ukv"].shape[1] // BH - NOPE
    FF = T["dense_w_down"].shape[1]
    NE = T["moe_router"].shape[2]
    HR = ROPE // 2
    assert NT == 2 and KD == 8 and NMEM == SEQ and MW == 256 and AH == 4 and BH == 6 and NOPE == P and VH == P
    PASSES = -(-SEQ // CAP)
    assert CAP == P

    x_d, mem_d = T["x"][0], T["mem"][0]

    def rows(w):
        return w.rearrange("(k p) n -> p k n", p=P)

    def cols(w, a, b):
        return rows(w)[:, :, a:b]

    aw, bw = T["a_w_in"][0], T["b_w_in"][0]
    aqw, avw = AH * AQ, AH * AV
    o_k, o_v, o_o, o_g = aqw, 2 * aqw, 2 * aqw + avw, 2 * aqw + 2 * avw
    hv = avw // 2
    HD = D // 2
    stream = [
        ("memkv0", cols(T["mem_w_kv"][0], 0, 2 * MW)), ("memkv1", cols(T["mem_w_kv"][1], 0, 2 * MW)),
        ("gmq", cols(aw, o_g, AIN)), ("q", cols(aw, 0, aqw)), ("k", cols(aw, o_k, o_v)),
        ("v0", cols(aw, o_v, o_v + hv)), ("v1", cols(aw, o_v + hv, o_o)),
        ("o0", cols(aw, o_o, o_o + hv)), ("o1", cols(aw, o_o + hv, o_g)),
        ("aout0", cols(T["a_w_out"][0], 0, HD)), ("aout1", cols(T["a_w_out"][0], HD, D)),
    ]
    FB = 2 * P
    NB = FF // FB
    PER = 3 * NB
    KH = KD // 2
    W = 2 * FB
    FFN = [("gu", 0, 0), ("gu", 0, 1)]
    for b in range(1, NB):
        FFN += [("gu", b, 0), ("gu", b, 1), ("dn", b - 1, 0)]
    FFN.append(("dn", NB - 1, 0))
    assert NB % 2 == 0 and PER % SLOTS == 0 and PER % CUTS == 0 and len(FFN) == PER

    def gu_item(b):
        return max(3 * b - 1, 0)

    def dn_item(b):
        return min(3 * b + 4, PER - 1)

    def ffn_parts(gu, dn, n):
        kind, b, h = FFN[n]
        if kind == "gu":
            return [(cols(gu, g * FF + b * FB, g * FF + (b + 1) * FB)[:, h * KH:(h + 1) * KH, :],
                     KH, slice(0, KH), slice(g * FB, (g + 1) * FB)) for g in range(2)]
        return [(rows(dn)[:, 2 * b + kk:2 * b + kk + 1, :], 2, slice(kk, kk + 1), slice(0, D)) for kk in range(2)]

    FFN0 = len(stream)
    stream += [(f"ffn{n}", None) for n in range(PER)]
    stream += [
        ("dkv", rows(T["w_dkv"])), ("cq", cols(bw, 0, QL)), ("mq", cols(bw, QL, QL + MW)),
        ("ukv", rows(T["w_ukv"])), ("uq", rows(T["b_w_uq"][0])),
        ("bout0", cols(T["b_w_out"][0], 0, HD)), ("bout1", cols(T["b_w_out"][0], HD, D)),
    ]
    NS = len(stream)
    item = {name: n for n, (name, _) in enumerate(stream)}
    place, before_it, filled_at = [], [], []
    at, occupant, fills = -2 * FFN0 % SLOTS, [None] * SLOTS, [0] * SLOTS
    for n, (name, view) in enumerate(stream):
        halves = [at] if view is None else [at, at + 1]
        place.append(at)
        before_it.append(sorted({occupant[h] for h in halves if occupant[h] is not None}))
        fills[at] += 32 if view is None else 16
        filled_at.append(fills[at])
        for h in halves:
            occupant[h] = n
        at = (at + len(halves)) % SLOTS
    E0 = at
    BASE_FILLS = fills
    EXPERT_FILLS = 32 * PER // SLOTS
    assert place[FFN0] == 0

    with ExitStack() as ctx:
        def sb(name, shape, dt=F32):
            return ctx.enter_context(nc.sbuf_tensor(name, shape, dt))

        sems = {}

        def S(name):
            if name not in sems:
                sems[name] = ctx.enter_context(nc.semaphore(name))
            return sems[name]

        PS = ctx.enter_context(nc.psum_tensor("PS", [P, 8, 512], F32))
        ring = sb("ring", [P, SLOTS * SLOT])
        whi = sb("whi", [P, CUTS, SLOT], FR)
        wlo = sb("wlo", [P, CUTS, SLOT], FR)
        xhi = sb("xhi", [P, KD, SEQ], FR)
        xlo = sb("xlo", [P, KD, SEQ], FR)
        hhi = sb("hhi", [P, 2, SEQ], FR)
        hlo = sb("hlo", [P, 2, SEQ], FR)
        xres = sb("xres", [P, NT, D])
        xn = sb("xn", [P, NT, D])
        xT = sb("xT", [P, KD, SEQ])
        mix = sb("mix", [P, NT, D])
        memkT = sb("memkT", [P, 2, 2, NMEM])
        memv = sb("memv", [P, 2, NT, MW])
        ident = sb("ident", [P, P])
        ones = sb("ones", [P, P])
        mask_kq = sb("mask_kq", [P, P])
        mask_qk = sb("mask_qk", [P, P])
        before = sb("before", [P, P])
        sel = sb("sel", [AH, AH, P])
        NG = 7 * KD + avw // P + QL // P + KVL // P + 4
        gains = sb("gains", [P, NG])
        hg = sb("hg", [P, 2 * QKH])
        bias_i = sb("bias_i", [AH, 1])
        bias_f = sb("bias_f", [AH, 1])
        nhalf = sb("nhalf", [P, 16])
        sumsq = sb("sumsq", [P, 2, 16])
        meansq = sb("meansq", [P, 2, 16])
        rstd = sb("rstd", [P, 2, 16])
        rx = sb("rx", [P, NT])
        posi = sb("posi", [P, NT], I32)
        posf = sb("posf", [P, NT])
        invf = sb("invf", [P, HR])
        rot = sb("rot", [P, 6, NT, HR])
        roti = sb("roti", [P, NT, HR], I32)
        smax = sb("smax", [P, 16])
        ssum = sb("ssum", [P, 16])
        srec = sb("srec", [P, 16])
        sbias = sb("sbias", [P, 16])
        router = sb("router", [P, KD, NE])
        arena = sb("arena", [P, 10240])

        def carve(at, *shape):
            n = int(np.prod(shape))
            v = arena[:, at:at + n]
            if len(shape) == 1:
                return v
            names = "abcd"[:len(shape)]
            return v.rearrange(f"p ({' '.join(names)}) -> p {' '.join(names)}",
                               **{c: s for c, s in zip(names, shape)})

        memS = carve(0, NT, D)
        memT = carve(2048, 2, KD, NMEM)
        kS = carve(0, 2, NT, MW)
        mqS = carve(1024, NT, MW)
        mqT = carve(1536, 2, SEQ)
        qT = carve(2048, AH, SEQ)
        kT = carve(3072, AH, SEQ)
        VW = AV + 1
        A0 = 6144
        v1 = carve(A0, NT, AH, VW)
        og = carve(A0 + NT * AH * VW, NT, avw)
        assert A0 + NT * AH * VW + NT * avw <= 9728
        grow = arena[0:NG, A0:A0 + P]
        hrow = arena[0:1, A0 + P:A0 + P + 2 * QKH]
        gat = arena[0:AH, 4096:4096 + 8 * SEQ].rearrange("p (a b) -> p a b", a=8)
        gi, gf, gt, glf, gG, ga, gM, gone = (gat[:, r] for r in range(8))
        gm, gem, gneg = gf, gt, glf
        gN = sb("gN", [P, 2, NT, AH])
        den = sb("den", [P, NT * AH])
        xflat = xn[:, :, :].rearrange("p a b -> p (a b)")
        Dm = mix[:, :, :].rearrange("p a b -> p (a b)")[:, 0:AH * 384].rearrange("p (a b) -> p a b", a=AH)
        PmT = xflat[:, 0:AH * 384].rearrange("p (a b) -> p a b", a=AH)
        mP = xn[:, :, :].rearrange("p a (h m) -> p a h m", h=MH)
        mPT = xT[:, :, :].rearrange("p a b -> p (a b)").rearrange("p (t h m q) -> p t h m q", t=NT, h=MH, m=2)
        sil = carve(0, NT, FB)
        hn = carve(NT * FB, NT, FB)
        xTk = carve(0, KD, SEQ)
        qF = carve(0, NT * BH, QKH)
        cqS = carve(2688, NT, QL)
        mqS1 = carve(3456, NT, MW)
        ckvT = carve(3968, 2, SEQ)
        cqT = carve(4480, 3, SEQ)
        kTn = carve(2304, BH, SEQ)
        kTr = arena[0:ROPE, 3840:3840 + BH * SEQ].rearrange("p (h s) -> p h s", h=BH)
        kF = carve(5760, NT * BH, QKH)
        zS = carve(8064, NT, KVL + ROPE)
        mqT1 = carve(8704, 2, SEQ)
        qTn = xT[:, 0:BH, :]
        qTr = xflat[0:ROPE, 0:BH * SEQ].rearrange("p (h s) -> p h s", h=BH)
        vF = mix[:, :, 0:BH * VH].rearrange("p t (h b) -> p t h b", b=VH)
        Pb = carve(5760, BH, 384)
        PT = carve(0, BH, 384)
        o = 2 * NT * FB
        Sx = carve(o, NT, CAP); o += NT * CAP
        combe = carve(o, NT); o += NT
        zeros = carve(o, P); o += P
        gate = carve(o, 1); o += 1
        g1row = arena[0:1, o:o + D]; o += D
        xe_ = slice(0, CAP)
        yhi, ylo = xhi[:, :, P:2 * P], xlo[:, :, P:2 * P]
        NC = (PASSES + 1) * NE
        iota = carve(o, CAP); o += CAP
        iotai = arena[:, o:o + CAP].bitcast(I32); o += CAP
        lg = carve(o, NT, NE); o += NT * NE
        m8 = carve(o, NT, 8); o += NT * 8
        idxf = carve(o, NT, 8); o += NT * 8
        idx8 = arena[:, o:o + NT * 8].bitcast(U32).rearrange("p (a b) -> p a b", a=NT); o += NT * 8
        oh1 = carve(o, NT, NE); o += NT * NE
        oh2 = carve(o, NT, NE); o += NT * NE
        chosen = carve(o, NT, NE); o += NT * NE
        keys = carve(o, NT, NC); o += NT * NC
        combs = carve(o, NT, NC); o += NT * NC
        gt2 = carve(o, 16); o += 16
        assert o <= 9728
        cnt_i = sb("cnt_i", [P, 1], I32)
        G = sb("G", [P, NT, P], FR)

        NORMS = ["mem", "x0", "mk0", "mk1", "mq0", "hm", "x1", "x2", "ckv", "cq", "mq1", "kh", "qh", "x3"]
        nidx = {n: i for i, n in enumerate(NORMS)}

        def nat(v, W):
            return v.rearrange("p a (h w) -> p a h w", w=W)

        nview = {
            "mem": (memS, memS, D), "x0": (xres[:, :, :], xn[:, :, :], D),
            "mk0": (nat(kS[:, 0], MD), None, MD), "mk1": (nat(kS[:, 1], MD), None, MD),
            "mq0": (nat(mqS, MD), None, MD), "hm": (nat(mix[:, :, 0:avw], AV), None, AV),
            "x1": (xres[:, :, :], xn[:, :, :], D), "x2": (xres[:, :, :], xn[:, :, :], D),
            "ckv": (zS[:, :, 0:KVL], None, KVL), "cq": (cqS, None, QL), "mq1": (nat(mqS1, MD), None, MD),
            "kh": (kF, None, QKH), "qh": (qF, None, QKH), "x3": (xres[:, :, :], xn[:, :, :], D),
        }

        LATE = ("x1", "x2", "x3")
        OWN_SUMS = ("mem", "x0", "x1", "x2", "kh", "qh", "x3")
        squares_no, m = {}, 0
        for name in NORMS:
            m += name not in OWN_SUMS
            squares_no[name] = m

        def sums(name):
            return sumsq[:, nidx[name] % 2, :]

        def groups(name):
            v = nview[name][0]
            return int(np.prod(v.shape[1:-1]))

        def shaped(tile, name):
            v = nview[name][0]
            t = tile[:, 0:groups(name)]
            if len(v.shape) == 4:
                t = t.rearrange("p (a b) -> p a b", a=v.shape[1])
            return t

        def sq_of(name):
            v = nview[name][0]
            n = int(np.prod(v.shape[1:]))
            at = {"hm": 2048, "mk0": 9728, "mk1": 9728, "mq0": 9728}.get(name, 9472)
            assert at + n <= arena.shape[1]
            base = arena[:, at:at + n]
            if len(v.shape) == 4:
                return base.rearrange("p (a b c) -> p a b c", a=v.shape[1], b=v.shape[2])
            return base.rearrange("p (a b) -> p a b", a=v.shape[1])

        def bcast(ap, n):
            return bass.AP(ap.tensor, ap.offset, [list(d) for d in ap.ap] + [[0, n]])

        gcol = {}
        at = 0
        for name, n in (("a_norm", KD), ("b_norm", KD), ("kv_norm", KD), ("mem0", KD), ("mem1", KD), ("ffn0", KD),
                        ("ffn1", KD), ("head", avw // P), ("q_a", QL // P), ("kv_a", KVL // P),
                        ("memq0", 1), ("memq1", 1), ("memk0", 1), ("memk1", 1)):
            gcol[name] = at
            at += n
        assert at == NG

        TR = [
            ("mem", memS, 0, [(memT[:, 0], "mem0"), (memT[:, 1], "mem1")]),
            ("x0", xn, 4, [(xT, "a_norm")]),
            ("mix0", mix, 0, [(xT, "head")]),
            ("x1", xres, 0, []),
            ("x2", xres, 0, [(xTk, "kv_norm"), (xT, "b_norm")]),
            ("mix1", mix, 0, [(xT, None)]),
            ("x3", xres, 0, [(xT, "ffn1")]),
        ]
        tidx = {t[0]: i for i, t in enumerate(TR)}

        block = ctx.enter_context(nc.Block())

        UNITS = [(kind, t, g) for kind in ("kv", "q") for t in range(NT) for g in range(BH // 2)]
        UNITS = [(kind, t, g, u % 4) for u, (kind, t, g) in enumerate(UNITS)]
        KQT = [(full[:, 2 * g:2 * g + 2, :], n, 0) for a, b in ((kTn, kTr), (qTn, qTr))
               for full, n in ((a, P), (b, ROPE)) for g in range(BH // 2)]
        KQT = [(dst, n, u % 8) for u, (dst, n, _) in enumerate(KQT)]
        PTB = [6, 7, 0, 1, 2]
        REST = range(2, NB - 2, 2)

        def count(i, per_ffn, r, per_block, const):
            if r is not None:
                const = r * (2 * per_block) + const
            return const if i is None or isinstance(i, int) else i * per_ffn + const

        def early(i):
            return i is None or isinstance(i, int)

        def hcols(b, nt):
            return slice(0, SEQ) if nt == NT else slice(b % 2 * P, b % 2 * P + P)

        def cuts_before(i):
            return 0 if i is None else PER

        def blocks_before(i):
            return 0 if i is None else NB

        def items_before(i):
            return FFN0 if i is None else NS

        def cut_item(b):
            return [n for n in (3 * b + 1, 3 * b + 2) if n < PER]

        def k_gain(name, g, k):
            if g is None or (g == "head" and k >= avw // P):
                return None
            return gains[:, gcol[g] + k:gcol[g] + k + 1]

        def through(name):
            return item[name] + 1

        @block.sync
        def _(sp):
            def fill_big(h, view):
                k, n = view.shape[1:]
                sp.dma_start(ring[:, h * SLOT:h * SLOT + k * n].rearrange("p (k n) -> p k n", k=k), view).then_inc(S(f"slot_full{h}"), 16)

            def fill_ffn(h, gu, dn, n):
                for view, k, ks, ns in ffn_parts(gu, dn, n):
                    dst = ring[:, h * SLOT:(h + 1) * SLOT].rearrange("p (k n) -> p k n", k=k)
                    sp.dma_start(dst[:, ks, ns], view).then_inc(S(f"slot_full{h}"), 16)

            for t in range(NT):
                sp.dma_start(memS[:, t], mem_d[t * P:(t + 1) * P]).then_inc(S(f"mem_in{t}"), 16)
            sp.dma_start(xres[:, :, :], x_d.rearrange("(t p) d -> p t d", p=P)).then_inc(S("x_in"), 16)
            for name, v in (("a_norm", T["a_norm"][0]), ("b_norm", T["b_norm"][0]), ("kv_norm", T["kv_norm"]),
                            ("mem0", T["mem_norm"].rearrange("l d -> (l d)")), ("ffn0", T["ffn_norm"].rearrange("l d -> (l d)")),
                            ("head", T["a_head_norm"][0]), ("q_a", T["b_q_a_norm"][0]), ("kv_a", T["kv_a_norm"])):
                k = v.shape[0] // P
                sp.dma_start(grow[gcol[name]:gcol[name] + k, :], v.rearrange("(k p) -> k p", p=P)).then_inc(S("gain_in"), 16)
            for name, v in (("memq0", T["mem_q_norm"]), ("memk0", T["mem_k_norm"])):
                for h in range(2):
                    sp.dma_start(grow[gcol[name]:gcol[name] + 2, h * MD:(h + 1) * MD], v).then_inc(S("gain_in"), 16)
            sp.dma_start(hrow[:, 0:QKH], T["k_head_norm"].rearrange("(a n) -> a n", a=1)).then_inc(S("gain_in"), 16)
            sp.dma_start(hrow[:, QKH:2 * QKH], T["b_q_head_norm"]).then_inc(S("gain_in"), 16)
            fill_big(place[0], stream[0][1])
            gb = T["a_gate_bias"].rearrange("a n -> n a")
            sp.dma_start(bias_i[:, :], gb[0:AH]).then_inc(S("bias_in"), 16)
            sp.dma_start(bias_f[:, :], gb[AH:2 * AH]).then_inc(S("bias_in"), 16)
            for n in (1, 2):
                fill_big(place[n], stream[n][1])
            sp.dma_start(posi[:, :], T["positions"][0].rearrange("(t p) -> p t", p=P),
                         allow_slow_non_contiguous=True).then_inc(S("pos_in"), 16)
            sp.dma_start(router[:, :, :], rows(T["moe_router"][0])).then_inc(S("router_in"), 16)
            for n, (name, view) in enumerate(stream):
                if n < 3:
                    continue
                for m in before_it[n]:
                    if stream[m][1] is None:
                        sp.wait_ge(S("lows"), m - FFN0 + 1)
                        sp.wait_ge(S("pool_lows"), m - FFN0 + 1)
                    else:
                        sp.wait_ge(S("through"), m + 1)
                if view is None:
                    fill_ffn(place[n], T["dense_w_gate_up"][0], T["dense_w_down"][0], n - FFN0)
                else:
                    fill_big(place[n], view)

            def load_experts(p, first=0):
                with sp.Fori(first, NE) as e:
                    gu = T["moe_w_gate_up"][0][bass.ds(e, 1), :, :].rearrange("e d n -> (e d) n")
                    dn = T["moe_w_down"][0][bass.ds(e, 1), :, :].rearrange("e d n -> (e d) n")
                    i = e if p is None else p * NE + e
                    for n in range(PER):
                        sp.wait_ge(S("lows"), i * PER + (PER + n - SLOTS + 1))
                        sp.wait_ge(S("pool_lows"), i * PER + (PER + n - SLOTS + 1))
                        fill_ffn((E0 + n) % SLOTS, gu, dn, n)

            for n in range(PER):
                if n < SLOTS:
                    sp.wait_ge(S("through"), occupant[(E0 + n) % SLOTS] + 1)
                else:
                    sp.wait_ge(S("lows"), PER + n - SLOTS + 1)
                    sp.wait_ge(S("pool_lows"), PER + n - SLOTS + 1)
                fill_ffn((E0 + n) % SLOTS, T["moe_w_gate_up"][0][0], T["moe_w_down"][0][0], n)
                if n == SLOTS - 1:
                    sp.dma_start(g1row, T["ffn_norm"][1:2]).then_inc(S("g1_in"), 16)
            load_experts(None, 1)
            sp.wait_ge(S("routed"), 1)
            passes = sp.value_load(cnt_i[0:1, 0:1], min_val=1, max_val=PASSES)
            with sp.If(passes > 1):
                with sp.Fori(1, passes) as p:
                    load_experts(p)
            for t in range(NT):
                sp.wait_ge(S("x_final"), t + 1)
                sp.dma_start(out[0].rearrange("(t p) d -> p t d", p=P)[:, t], xres[:, t]).then_inc(S("stored"), 16)
            sp.wait_ge(S("stored"), 16 * NT)

        @block.gpsimd
        def _(pool):
            c = S("consts")
            pool.memset(ident[:, :], 0.0).then_inc(c, 1)
            pool.memset(ones[:, :], 1.0).then_inc(c, 1)
            pool.memset(nhalf[:, :], -0.5).then_inc(c, 1)
            pool.wait_ge(c, 3)
            pool.affine_select(out=ident[:, :], in_=ident[:, :], compare_op=ALU.not_equal, fill=1.0, base=0,
                               pattern=[[-1, P]], channel_multiplier=1).then_inc(S("ident"), 1)

            def rstd_of(name):
                e, g = nidx[name], groups(name)
                if e > 1:
                    pool.wait_ge(S("scaled"), e - 1)
                pool.wait_ge(S("sums"), e + 1)
                pool.tensor_scalar(meansq[:, e % 2, 0:g], sums(name)[:, 0:g], EPS, None, ALU.add).then_inc(S("mean_eps"), 1)
                pool.wait_ge(S("mean_eps"), e + 1)
                pool.tensor_tensor(rstd[:, e % 2, 0:g], meansq[:, e % 2, 0:g], nhalf[:, 0:g], ALU.pow).then_inc(S("rstds"), 1)

            rstd_of("mem")
            rstd_of("x0")
            pool.memset(mask_kq[:, :], 0.0).then_inc(c, 1)
            pool.memset(mask_qk[:, :], 0.0).then_inc(c, 1)
            pool.memset(sel[:, :, :], 0.0).then_inc(c, 1)
            pool.wait_ge(c, 6)
            pool.affine_select(out=mask_kq[:, :], in_=mask_kq[:, :], compare_op=ALU.is_ge, fill=NEG, base=0,
                               pattern=[[1, P]], channel_multiplier=-1).then_inc(c, 1)
            pool.affine_select(out=mask_qk[:, :], in_=mask_qk[:, :], compare_op=ALU.is_ge, fill=NEG, base=0,
                               pattern=[[-1, P]], channel_multiplier=1).then_inc(c, 1)
            pool.affine_select(out=before[:, :], in_=ones[:, :], compare_op=ALU.is_gt, fill=0.0, base=0,
                               pattern=[[1, P]], channel_multiplier=-1).then_inc(c, 1)
            pool.affine_select(out=sel[:, :, :], in_=sel[:, :, :], compare_op=ALU.not_equal, fill=1.0, base=0,
                               pattern=[[-1, AH], [0, P]], channel_multiplier=1).then_inc(c, 1)
            rstd_of("mk0")
            rstd_of("mk1")
            rstd_of("mq0")
            inv = (1.0 / np.float32(ROPE_THETA) ** (np.arange(0, ROPE, 2, dtype=np.float32) / np.float32(ROPE))
                   ).astype(np.float32)
            for j in range(HR):
                last = pool.memset(invf[:, j:j + 1], float(inv[j]))
            last.then_inc(S("freqs"), 1)
            rstd_of("hm")
            def lo_of(i, n, r=None):
                pool.wait_ge(S("highs"), count(i, PER, r, 3, cuts_before(i) + n + 1))
                h = ((E0 if i is not None else 0) + n) % SLOTS
                m = SLOT - POOL_COLS
                pool.tensor_tensor(wlo[:, n % CUTS, m:SLOT], ring[:, h * SLOT + m:(h + 1) * SLOT], whi[:, n % CUTS, m:SLOT].bitcast(F32),
                                   ALU.subtract).then_inc(S("pool_lows"), 1)

            for n in range(CUTS):
                lo_of(None, n)
            rstd_of("x1")

            def swiglu(i):
                if i is not None and not isinstance(i, int):
                    for n in range(CUTS):
                        lo_of(i, n)
                with pool.Fori(0, PER // SLOTS - 1) as r:
                    for n in range(CUTS, CUTS + SLOTS):
                        lo_of(i, n, r)
                for n in range(PER - CUTS, PER):
                    lo_of(i, n)

            swiglu(None)
            for name in ("x2", "ckv", "cq", "mq1", "kh", "qh"):
                rstd_of(name)
            for n in range(CUTS - 1):
                lo_of(0, n)
            rstd_of("x3")
            lo_of(0, CUTS - 1)
            pool.iota(iotai, pattern=[[1, CAP]], base=0, channel_multiplier=0).then_inc(S("iota_i"), 1)
            pool.wait_ge(S("iota_i"), 1)
            pool.tensor_copy(iota, iotai).then_inc(S("iota"), 1)
            pool.memset(gate, 0.0).then_inc(S("zeros"), 1)
            pool.memset(zeros, 0.0).then_inc(S("zeros"), 1)
            pool.wait_ge(S("routed"), 1)
            passes = pool.value_load(cnt_i[0:1, 0:1], min_val=1, max_val=PASSES)
            swiglu(0)
            with pool.Fori(1, passes * NE) as i:
                swiglu(i)

        @block.scalar
        def _(act):
            def square(name):
                e, (v, dst, w) = nidx[name], nview[name]
                if e > 1:
                    act.wait_ge(S("rstds"), e - 1)
                if name not in OWN_SUMS:
                    if squares_no[name] > 1:
                        act.wait_ge(S("sums"), e)
                    nc.scalar.activation(sq_of(name), v, ACT.Square, scale=float(w) ** -0.5).then_inc(S("squares"), 1)
                    return
                n = groups(name) * w
                junk = {"mem": arena[:, 2048:2048 + n], "kh": whi[:, 0:2, :].rearrange("p a b -> p (a b)")[:, 0:n],
                        "qh": wlo[:, 0:2, :].rearrange("p a b -> p (a b)")[:, 0:n]}.get(name, xflat)
                for g in range(groups(name)):
                    if name == "mem":
                        act.wait_ge(S(f"mem_in{g}"), 16)
                    if name in LATE:
                        act.wait_ge(S("x_sum"), NT * LATE.index(name) + g + 1)
                    last = nc.scalar.activation(junk[:, g * w:(g + 1) * w], v[:, g], ACT.Square, scale=float(w) ** -0.5, accum_out=sums(name)[:, g:g + 1])
                last.then_inc(S("sums"), 1)

            def y_high():
                nc.scalar.activation(yhi, PS[:, 4:6, :].rearrange("p a (k n) -> p (a k) n", n=P), ACT.Copy,
                                     scale=gate[:, 0:1]).then_inc(S("y_high"), 1)

            def x_high(i):
                act.wait_ge(S("gathered"), i + 1)
                nc.scalar.activation(xhi[:, :, xe_], PS[:, 6:8, :].rearrange("p a (k n) -> p (a k) n", n=CAP),
                                     ACT.Copy).then_inc(S("xhi_ready"), 1)

            def hi_of(i, n, r=None):
                const = items_before(i) + n - CUTS + 1
                if n >= CUTS or not early(i):
                    act.wait_ge(S("through"), count(i, PER, r, 3, const))
                h = ((E0 if i is not None else 0) + n) % SLOTS
                base = filled_at[FFN0 + n] if i is None else BASE_FILLS[h] + 32 * (n // SLOTS + 1)
                act.wait_ge(S(f"slot_full{h}"), count(i, EXPERT_FILLS, r, 16, base))
                nc.scalar.activation(whi[:, n % CUTS, :], ring[:, h * SLOT:(h + 1) * SLOT], ACT.Copy).then_inc(S("highs"), 1)

            def block(i, b, nt, r=None):
                for n in cut_item(b):
                    if b > 0 or not early(i):
                        hi_of(i, n, r)
                if b == 0 and i is not None:
                    act.wait_ge(S("through"), count(i, PER, r, 3, NS))
                    y_high()
                act.wait_ge(S("through"), count(i, PER, r, 3, items_before(i) + gu_item(b) + 2))
                for t in range(nt):
                    last = nc.scalar.activation(sil[:, t], PS[:, t, 0:FB], ACT.Silu, scale=1.0 if i is not None else rx[:, t:t + 1])
                last.then_inc(S("silu"), 1)
                if 3 * b + 3 < PER:
                    hi_of(i, 3 * b + 3, r)
                if b == NB - 1 and i is not None:
                    x_high(i + 1)
                act.wait_ge(S("h_turned"), count(i, NB, r, 1, blocks_before(i) + b + 1))
                src = PS[:, 3, :].rearrange("p (a s) -> p a s", a=2)
                nc.scalar.activation(hhi[:, :, hcols(b, nt)], src[:, :, 0:nt * P], ACT.Copy).then_inc(S("h_high"), 1)

            def swiglu(i, nt):
                if not early(i):
                    hi_of(i, 0)
                for b in (0, 1):
                    block(i, b, nt)
                with act.Fori(0, len(REST)) as r:
                    for b in (2, 3):
                        block(i, b, nt, r)
                for b in (NB - 2, NB - 1):
                    block(i, b, nt)

            def evict(name):
                i, (_, _, bank, dsts) = tidx[name], TR[tidx[name]]
                for b in (0, 2):
                    act.wait_ge(S("transposed"), 4 * i + b + 1)
                    for dst, g in dsts:
                        for k in (2 * b, 2 * b + 1):
                            s = k_gain(name, g, k)
                            last = nc.scalar.activation(dst[:, k, :], PS[:, bank + b, (k % 2) * SEQ:(k % 2 + 1) * SEQ], ACT.Copy,
                                                        scale=1.0 if s is None else s)
                    last.then_inc(S("evicted_even"), 1)

            def mem_softmax(l, bank):
                for t in range(NT):
                    for h in range(MH):
                        if t == 0 and h == 0:
                            act.wait_ge(S("mem_max"), l + 1)
                        c = t * MH + h
                        last = nc.scalar.activation(mP[:, t, h], PS[:, bank + 2 * t + h % 2, (h // 2) * 256:(h // 2 + 1) * 256],
                                                    ACT.Exp, bias=sbias[:, c:c + 1], scale=float(MD) ** -0.5,
                                                    accum_out=ssum[:, c:c + 1])
                last.then_inc(S("mem_exp"), 1)

            def mem_turned(l, tb):
                for b in range(2):
                    act.wait_ge(S("mem_pt"), 4 * l + 2 * b + 1)
                    nc.scalar.activation(mPT[:, b, 0:2].rearrange("p h m q -> p (h m q)"), PS[:, tb + 2 * b, :],
                                         ACT.Copy).then_inc(S("mem_pt_even"), 1)

            square("mem")
            act.wait_ge(S("x_in"), 16)
            square("x0")
            act.wait_ge(S("gains"), 2)
            evict("mem")
            evict("x0")
            for l in range(2):
                act.wait_ge(S("through"), through(f"memkv{l}"))
                act.wait_ge(S("transposed"), 4)
                nc.scalar.activation(kS[:, l], PS[:, 2 * l:2 * l + 2, 0:MW], ACT.Copy).then_inc(S("kS"), 1)
                nc.scalar.activation(memv[:, l], PS[:, 2 * l:2 * l + 2, MW:2 * MW], ACT.Copy).then_inc(S("memv"), 1)
            act.wait_ge(S("kS"), 2)
            square("mk0")
            square("mk1")
            act.wait_ge(S("through"), through("gmq"))
            act.wait_ge(S("bias_in"), 32)
            nc.scalar.activation(gi, PS[0:AH, 4, 0:SEQ], ACT.Identity, bias=bias_i[:, :]).then_inc(S("gate_in"), 1)
            nc.scalar.activation(gf, PS[0:AH, 4, SEQ:2 * SEQ], ACT.Identity, bias=bias_f[:, :]).then_inc(S("gate_in"), 1)
            nc.scalar.activation(mqS, PS[:, 5, :].rearrange("p (t n) -> p t n", t=NT), ACT.Copy).then_inc(S("mqS"), 1)
            act.wait_ge(S("gate_abs"), 1)
            nc.scalar.activation(gt, gt, ACT.Exp, scale=-1.0).then_inc(S("gate_exp"), 1)
            act.wait_ge(S("gate_exp"), 1)
            nc.scalar.activation(gt, gt, ACT.Ln, bias=1.0).then_inc(S("gate_exp"), 1)
            act.wait_ge(S("mqS"), 1)
            square("mq0")
            act.wait_ge(S("through"), through("q"))
            for b in range(2):
                last = nc.scalar.activation(qT[0:AQ, 2 * b:2 * b + 2, :], PS[0:AQ, 6 + b, :].rearrange("p (h s) -> p h s", h=2), ACT.Copy)
            last.then_inc(S("qT"), 1)
            for half in range(2):
                act.wait_ge(S("through"), through(f"o{half}"))
                for t in range(NT):
                    last = nc.scalar.activation(og[:, t, half * hv:(half + 1) * hv], PS[:, (6, 0)[half] + t, 0:hv], ACT.Sigmoid)
                last.then_inc(S("og"), 1)
            act.wait_ge(S("gate_m"), 1)
            nc.scalar.activation(gem, gm, ACT.Exp, scale=-1.0).then_inc(S("gate_em"), 1)
            act.wait_ge(S("gN"), 1)
            for h in range(AH):
                act.wait_ge(S("decay_arg"), h + 1)
                for s0, c0, c1 in ((0, 0, SEQ), (1, SEQ, SEQ + P)):
                    last = nc.scalar.activation(Dm[:, h, c0:c1], PS[:, h, c0:c1], ACT.Exp, bias=gN[:, 0, s0, h:h + 1])
                last.then_inc(S("decay"), 1)
            mem_softmax(0, 4)
            act.wait_ge(S("h_out"), 1)
            square("hm")
            mem_turned(0, 4)
            evict("mix0")
            for n in range(CUTS):
                hi_of(None, n)
            for k in range(KD):
                if k % 2 == 0:
                    act.wait_ge(S("transposed"), 4 * tidx["x1"] + k // 2 + 1)
                last = nc.scalar.activation(xhi[:, k, :], PS[:, k // 2, (k % 2) * SEQ:(k % 2 + 1) * SEQ], ACT.Copy,
                                            scale=k_gain("x1", "ffn0", k))
                if k % 2 == 1:
                    last.then_inc(S("x1_high"), 1)
            square("x1")
            act.wait_ge(S("scaled"), nidx["x1"] + 1)

            swiglu(None, NT)
            act.wait_ge(S("angles"), 1)
            nc.scalar.activation(rot[:, 4], rot[:, 2], ACT.Sin).then_inc(S("sincos"), 1)
            nc.scalar.activation(rot[:, 5], rot[:, 3], ACT.Sin).then_inc(S("sincos"), 1)
            evict("x2")
            square("x2")
            act.wait_ge(S("scaled"), nidx["x2"] + 1)
            for name, dst, src, sem in (("dkv", zS, PS[:, 4:6, 0:KVL + ROPE], "zS"), ("cq", cqS, PS[:, 6:8, 0:QL], "cqS"),
                                        ("mq", mqS1, PS[:, 0, :].rearrange("p (t n) -> p t n", t=NT), "mqS")):
                act.wait_ge(S("through"), through(name))
                for t in range(NT):
                    last = nc.scalar.activation(dst[:, t], src[:, t], ACT.Copy, scale=rx[:, t:t + 1])
                last.then_inc(S(sem), 1)
                act.wait_ge(S(sem), 2 if name == "mq" else 1)
                square({"dkv": "ckv", "cq": "cq", "mq": "mq1"}[name])
            for u, (kind, t, g, bank) in enumerate(UNITS):
                if u % 6 == 5:
                    act.wait_ge(S("through"), through("ukv" if u == 5 else "uq"))
                else:
                    act.wait_ge(S("unit"), u + 1 - u // 6)
                if kind == "kv":
                    src = PS[:, bank, :].rearrange("p (h a n) -> p h a n", h=2, a=2)
                    kdst = kF.rearrange("p (t h) n -> p t h n", t=NT)[:, t, 2 * g:2 * g + 2, 0:NOPE]
                    nc.scalar.activation(kdst, src[:, :, 0], ACT.Copy)
                    last = nc.scalar.activation(vF[:, t, 2 * g:2 * g + 2], src[:, :, 1], ACT.Copy)
                else:
                    dst = qF.rearrange("p (t h) n -> p t h n", t=NT)[:, t, 2 * g:2 * g + 2]
                    nc.scalar.activation(dst, PS[:, bank, 0:2 * QKH].rearrange("p (h n) -> p h n", h=2), ACT.Copy)
                    if u == 6:
                        act.wait_ge(S("rstds"), nidx["qh"] - 1)
                    for h in range(2):
                        c = t * BH + 2 * g + h
                        last = nc.scalar.activation(wlo[:, 0:2, :].rearrange("p a b -> p (a b)")[:, c * QKH:(c + 1) * QKH],
                                                    PS[:, bank, h * QKH:(h + 1) * QKH], ACT.Square, scale=float(QKH) ** -0.5,
                                                    accum_out=sums("qh")[:, c:c + 1])
                last.then_inc(S("sums" if u == 11 else "unit_out"), 1)
                if u == 2:
                    mem_softmax(1, 4)
                if u == 5:
                    mem_turned(1, 4)
                    act.wait_ge(S("unit_out"), 6)
                    act.wait_ge(S("k_rope_in"), 1)
                    square("kh")
            for u, (dst, rws, bank) in enumerate(KQT):
                if u % 2 == 0:
                    act.wait_ge(S("kq_t"), u + 1)
                    nc.scalar.activation(dst, PS[0:rws, bank, :].rearrange("p (h s) -> p h s", h=2), ACT.Copy).then_inc(S("kq_even"), 1)
            for h in range(BH):
                if h % (BH // 2) == 0:
                    act.wait_ge(S("att_max"), h // (BH // 2) + 1)
                for t, (c0, c1) in enumerate(((0, P), (P, 3 * P))):
                    last = nc.scalar.activation(Pb[:, h, c0:c1], PS[:, h, c0:c1], ACT.Exp, bias=sbias[:, t * BH + h:t * BH + h + 1],
                                                scale=float(QKH) ** -0.5, accum_out=ssum[:, t * BH + h:t * BH + h + 1])
                last.then_inc(S("att_exp"), 1)
            for u, bank in enumerate(PTB):
                if u % 2 == 0:
                    act.wait_ge(S("att_pt"), u + 1)
                    n = min(512, BH * 384 - 512 * u)
                    nc.scalar.activation(PT.rearrange("p a b -> p (a b)")[:, 512 * u:512 * u + n], PS[:, bank, 0:n],
                                         ACT.Copy).then_inc(S("att_pt_even"), 1)
            evict("mix1")
            for n in range(CUTS - 1):
                hi_of(0, n)
            square("x3")
            evict("x3")
            hi_of(0, CUTS - 1)
            act.wait_ge(S("top2"), 1)
            nc.scalar.activation(gt2[:, 2:4], gt2[:, 0:2], ACT.Exp).then_inc(S("gate2_exp"), 1)
            act.wait_ge(S("routed"), 1)
            passes = act.value_load(cnt_i[0:1, 0:1], min_val=1, max_val=PASSES)

            x_high(0)
            swiglu(0, 1)
            with act.Fori(1, passes * NE) as i:
                swiglu(i, 1)
            act.wait_ge(S("through"), passes * (NE * PER) + NS)
            y_high()

        @block.tensor
        def _(pe):
            mm = nc.tensor.matmul

            def tr(dst, src):
                return nc.tensor.transpose(dst, src, ident[0:src.shape[0], 0:src.shape[0]])

            def slot(name, *shape):
                n = item[name]
                pe.wait_ge(S(f"slot_full{place[n]}"), filled_at[n])
                at = place[n] * SLOT
                return ring[:, at:at + int(np.prod(shape))].rearrange("p (k n) -> p k n", k=shape[0])

            def transposes(name):
                _, src, bank, _ = TR[tidx[name]]
                if name in LATE:
                    sums_ = NT * LATE.index(name)
                    pe.wait_ge(S("x_sum"), sums_ + 1)
                for b in range(4):
                    for k in (2 * b, 2 * b + 1):
                        for t in range(NT):
                            if name in LATE and b == 0 and k == 0 and t == 1:
                                pe.wait_ge(S("x_sum"), sums_ + NT)
                            last = tr(PS[:, bank + b, (k % 2) * SEQ + t * P:(k % 2) * SEQ + (t + 1) * P], src[:, t, k * P:(k + 1) * P])
                    last.then_inc(S("transposed"), 1)

            def evicted(name):
                n = 2 * sum(1 for t in TR[:tidx[name] + 1] if t[3])
                pe.wait_ge(S("evicted_even"), n)
                pe.wait_ge(S("evicted_odd"), n)

            def natural(banks, src, w, n, nk=KD, c0=0):
                for t in range(NT):
                    bank, at = banks[t]
                    for k in range(nk):
                        last = mm(PS[:, bank, at:at + n], lhsT=src[:, k, t * P:(t + 1) * P], rhs=w[:, k, c0:c0 + n],
                                  start=(k == 0), stop=(k == nk - 1))
                return last

            def mem_attention(l, kT_, qT_, q_sem, q_val):
                pe.wait_ge(S(q_sem), q_val)
                pe.wait_ge(S("memkT"), 2)
                for par in range(2):
                    for t in range(NT):
                        for pair in range(2):
                            last = mm(PS[:, 4 + 2 * t + par, pair * 256:(pair + 1) * 256],
                                      lhsT=qT_[par * MD:(par + 1) * MD, pair, t * P:(t + 1) * P],
                                      rhs=kT_[par * MD:(par + 1) * MD, pair, :], start=True, stop=True)
                last.then_inc(S("mem_scores"), 1)

            def mem_turn(l, tb):
                pe.wait_ge(S("mem_exp"), l + 1)
                for t in range(NT):
                    for hh in range(2):
                        for h in (2 * hh, 2 * hh + 1):
                            for m in range(2):
                                last = tr(PS[:, tb + 2 * t + hh, ((h % 2) * 2 + m) * P:((h % 2) * 2 + m + 1) * P], mP[:, t, h, m * P:(m + 1) * P])
                        last.then_inc(S("mem_pt"), 1)

            def mem_attention_out(l, tb):
                pe.wait_ge(S("mem_pt_even"), 2 * (l + 1))
                pe.wait_ge(S("mem_pt_odd"), 2 * (l + 1))
                for t in range(NT):
                    for h in range(MH):
                        for m in range(2):
                            last = mm(PS[:, 4, (t * MH + h) * MD:(t * MH + h + 1) * MD], lhsT=mPT[:, t, h, m, :],
                                      rhs=memv[:, l, m, h * MD:(h + 1) * MD], start=(m == 0), stop=(m == 1))
                last.then_inc(S("mem_out"), 1)

            def project_out(names):
                ws = [slot(name, KD, HD) for name in names]
                for t in range(NT):
                    for hh in range(2):
                        for k in range(KD):
                            last = mm(PS[:, 4 + 2 * t + hh, :], lhsT=xT[:, k, t * P:(t + 1) * P], rhs=ws[hh][:, k, :],
                                      start=(k == 0), stop=(k == KD - 1))
                        if t == NT - 1:
                            last.then_inc(S("through"), 1)
                    if t == 0:
                        last.then_inc(S("projected"), 1)

            pe.wait_ge(S("ident"), 1)
            pe.wait_ge(S("scaled"), nidx["mem"] + 1)
            transposes("mem")
            pe.wait_ge(S("gain_in"), 16 * 14)
            tr(PS[:, 7, 0:NG], grow)
            mm(PS[:, 6, 0:2 * QKH], lhsT=ones[0:1, :], rhs=hrow, start=True, stop=True).then_inc(S("gains_t"), 1)
            pe.wait_ge(S("scaled"), nidx["x0"] + 1)
            pe.wait_ge(S("gains"), 2)
            transposes("x0")
            evicted("mem")
            for l in range(2):
                w = slot(f"memkv{l}", KD, 2 * MW)
                natural([(2 * l, 0), (2 * l + 1, 0)], memT[:, l], w, 2 * MW).then_inc(S("through"), 1)
            evicted("x0")
            w = slot("gmq", KD, 2 * AH + MW)
            for half in range(2):
                for k in range(KD):
                    mm(PS[0:AH, 4, half * SEQ:(half + 1) * SEQ], lhsT=w[:, k, half * AH:(half + 1) * AH], rhs=xT[:, k, :],
                       start=(k == 0), stop=(k == KD - 1))
            natural([(5, 0), (5, MW)], xT, w, MW, c0=2 * AH).then_inc(S("through"), 1)
            for name, bank in (("q", 6), ("k", 0)):
                if name == "k":
                    pe.wait_ge(S("memv"), 2)
                w = slot(name, KD, aqw)
                for h in range(AH):
                    for k in range(KD):
                        last = mm(PS[0:AQ, bank + h // 2, (h % 2) * SEQ:(h % 2 + 1) * SEQ], lhsT=w[:, k, h * AQ:(h + 1) * AQ],
                                  rhs=xT[:, k, :], start=(k == 0), stop=(k == KD - 1))
                last.then_inc(S("through"), 1)
            for name, banks in (("v0", (2, 3)), ("v1", (4, 5)), ("o0", (6, 7)), ("o1", (0, 1))):
                if name == "v1":
                    pe.wait_ge(S("mqS"), 1)
                if name == "o0":
                    pe.wait_ge(S("qT"), 1)
                if name == "o1":
                    pe.wait_ge(S("kT"), 1)
                w = slot(name, KD, hv)
                natural([(b, 0) for b in banks], xT, w, hv).then_inc(S("through"), 1)
            pe.wait_ge(S("v_out"), 2)
            for l in range(2):
                pe.wait_ge(S("scaled"), nidx[f"mk{l}"] + 1)
                for pair in range(2):
                    for t in range(NT):
                        last = tr(PS[:, 2 + l, pair * SEQ + t * P:pair * SEQ + (t + 1) * P], kS[:, l, t, pair * P:(pair + 1) * P])
                last.then_inc(S("memk_t"), 1)
            pe.wait_ge(S("scaled"), nidx["mq0"] + 1)
            for pair in range(2):
                for t in range(NT):
                    last = tr(PS[:, 4, pair * SEQ + t * P:pair * SEQ + (t + 1) * P], mqS[:, t, pair * P:(pair + 1) * P])
            last.then_inc(S("mq_t"), 1)
            pe.wait_ge(S("gate_em"), 1)
            for r, src in enumerate((ga, gem)):
                for t in range(NT):
                    c = (r * NT + t) * AH
                    last = tr(PS[:, 5, c:c + AH], src[:, t * P:(t + 1) * P])
            last.then_inc(S("gate_t"), 1)
            pe.wait_ge(S("og"), 2)
            pe.wait_ge(S("memkT"), 2)
            pe.wait_ge(S("gate_neg"), 1)
            pe.wait_ge(S("consts"), 10)
            for h in range(AH):
                mm(PS[:, h, 0:SEQ], lhsT=sel[:, h, :], rhs=gneg, start=True, stop=False, skip_group_check=True)
                mm(PS[:, h, SEQ:SEQ + P], lhsT=sel[:, h, :], rhs=gneg[:, P:SEQ], start=False, stop=False, skip_group_check=True)
                mm(PS[:, h, 0:P], lhsT=ident[:, :], rhs=mask_kq[:, :], start=False, stop=False, skip_group_check=True)
                mm(PS[:, h, SEQ:SEQ + P], lhsT=ident[:, :], rhs=mask_kq[:, :], start=False, stop=True,
                   skip_group_check=True).then_inc(S("decay_arg"), 1)
            pe.wait_ge(S("mqT"), 1)
            pe.wait_ge(S("gN"), 1)
            for h in range(AH):
                mm(PS[:, 4 + h, 0:SEQ], lhsT=kT[0:AQ, h, 0:P], rhs=qT[0:AQ, h, :], start=True, stop=True)
                mm(PS[:, 4 + h, SEQ:SEQ + P], lhsT=kT[0:AQ, h, P:SEQ], rhs=qT[0:AQ, h, P:SEQ], start=True,
                   stop=True).then_inc(S("kq"), 1)
            for h in range(AH):
                pe.wait_ge(S("weights"), h + 1)
                if h == 0:
                    pe.wait_ge(S("decay"), AH)
                mm(PS[:, h, 0:VW], lhsT=PmT[:, h, 0:P], rhs=v1[:, 0, h, :], start=True, stop=True)
                mm(PS[:, h, 256:256 + VW], lhsT=PmT[:, h, P:SEQ], rhs=v1[:, 0, h, :], start=True, stop=False)
                mm(PS[:, h, 256:256 + VW], lhsT=PmT[:, h, SEQ:SEQ + P], rhs=v1[:, 1, h, :], start=False,
                   stop=True).then_inc(S("num"), 1)
            mem_attention(0, memkT[:, 0], mqT, "mqT", 1)
            mem_turn(0, 4)
            mem_attention_out(0, 4)
            pe.wait_ge(S("mixed"), 1)
            transposes("mix0")
            evicted("mix0")
            project_out(("aout0", "aout1"))
            transposes("x1")
            def three(out_, xh, xl, wh, wl, first, last):
                mm(out_, lhsT=xh, rhs=wh, start=first, stop=False)
                mm(out_, lhsT=xh, rhs=wl, start=False, stop=False)
                return mm(out_, lhsT=xl, rhs=wh, start=False, stop=last)

            def cut_weights(i, n, r=None):
                pe.wait_ge(S("pool_lows"), count(i, PER, r, 3, cuts_before(i) + n + 1))
                pe.wait_ge(S("lows"), count(i, PER, r, 3, cuts_before(i) + n + 1))
                return n % CUTS

            def gate_up(i, b, nt, r=None):
                for h in range(2):
                    j = cut_weights(i, gu_item(b) + h, r)
                    for k in range(KH):
                        if i is None and b == 0 and k % 2 == 0:
                            pe.wait_ge(S("x1_low"), max((h * KH + k) // 2 + 1, NT))
                        for t in range(nt):
                            x_ = slice(t * P, (t + 1) * P)
                            last = three(PS[:, t, :], xhi[:, h * KH + k, x_], xlo[:, h * KH + k, x_], whi[:, j, k * W:(k + 1) * W],
                                         wlo[:, j, k * W:(k + 1) * W], h == 0 and k == 0, h == 1 and k == KH - 1)
                    last.then_inc(S("through"), 1)

            def down(i, b, nt, r=None):
                j = cut_weights(i, dn_item(b), r)
                pe.wait_ge(S("h_low"), count(i, NB, r, 1, blocks_before(i) + b + 1))
                for kk in range(2):
                    for t in range(nt):
                        for hh in range(2):
                            c0, h0 = kk * D + hh * HD, hcols(b, nt).start + t * P
                            x_ = slice(h0, h0 + P)
                            last = three(PS[:, 4 + 2 * t + hh, :], hhi[:, kk, x_], hlo[:, kk, x_], whi[:, j, c0:c0 + HD],
                                         wlo[:, j, c0:c0 + HD], b == 0 and kk == 0, b == NB - 1 and kk == 1)
                last.then_inc(S("through"), 1)

            def turn_hidden(i, b, nt, r=None):
                pe.wait_ge(S("h_ready"), count(i, NB, r, 1, blocks_before(i) + b + 1))
                for kk in range(2):
                    for t in range(nt):
                        last = tr(PS[:, 3, kk * SEQ + t * P:kk * SEQ + (t + 1) * P], hn[:, t, kk * P:(kk + 1) * P])
                last.then_inc(S("h_turned"), 1)

            def swiglu(i, nt, after_first=None, after_loop=None, after_last=None):
                gate_up(i, 0, nt)
                if after_first:
                    after_first()
                turn_hidden(i, 0, nt)
                gate_up(i, 1, nt)
                down(i, 0, nt)
                turn_hidden(i, 1, nt)
                with pe.Fori(0, len(REST)) as r:
                    for b in (2, 3):
                        gate_up(i, b, nt, r)
                        down(i, b - 1, nt, r)
                        turn_hidden(i, b, nt, r)
                if after_loop:
                    after_loop()
                for b in (NB - 2, NB - 1):
                    gate_up(i, b, nt)
                    if b == NB - 1 and after_last:
                        after_last()
                        turn_hidden(i, b, nt)
                        down(i, b - 1, nt)
                        continue
                    down(i, b - 1, nt)
                    turn_hidden(i, b, nt)
                down(i, NB - 1, nt)

            swiglu(None, NT)
            transposes("x2")
            evicted("x2")
            w = slot("dkv", KD, KVL + ROPE)
            natural([(4, 0), (5, 0)], xTk, w, KVL + ROPE).then_inc(S("through"), 1)
            w = slot("cq", KD, QL)
            natural([(6, 0), (7, 0)], xT, w, QL).then_inc(S("through"), 1)
            w = slot("mq", KD, MW)
            natural([(0, 0), (0, MW)], xT, w, MW).then_inc(S("through"), 1)
            pe.wait_ge(S("scaled"), nidx["ckv"] + 1)
            for k in range(2):
                for t in range(NT):
                    last = tr(PS[:, 1, k * SEQ + t * P:k * SEQ + (t + 1) * P], zS[:, t, k * P:(k + 1) * P])
            last.then_inc(S("lat_t"), 1)
            pe.wait_ge(S("scaled"), nidx["cq"] + 1)
            for k in range(3):
                for t in range(NT):
                    last = tr(PS[:, 2 + k // 2, (k % 2) * SEQ + t * P:(k % 2) * SEQ + (t + 1) * P], cqS[:, t, k * P:(k + 1) * P])
            last.then_inc(S("lat_t"), 1)
            pe.wait_ge(S("scaled"), nidx["mq1"] + 1)
            for pair in range(2):
                for t in range(NT):
                    last = tr(PS[:, 4, pair * SEQ + t * P:pair * SEQ + (t + 1) * P], mqS1[:, t, pair * P:(pair + 1) * P])
            last.then_inc(S("lat_t"), 1)
            mem_attention(1, memkT[:, 1], mqT1, "lat_out", 3)
            for u, (kind, t, g, bank) in enumerate(UNITS):
                if u == 0:
                    w = slot("ukv", 2, BH * (NOPE + VH))
                if u == 6:
                    w = slot("uq", 3, BH * QKH)
                if u >= 4:
                    pe.wait_ge(S("unit_out"), u - 4 + 1)
                if u == 6:
                    mem_turn(1, 4)
                if u == 8:
                    mem_attention_out(1, 4)
                src, nk, n = (ckvT, 2, 2 * (NOPE + VH)) if kind == "kv" else (cqT, 3, 2 * QKH)
                for k in range(nk):
                    last = mm(PS[:, bank, 0:n], lhsT=src[:, k, t * P:(t + 1) * P], rhs=w[:, k, g * n:(g + 1) * n],
                              start=(k == 0), stop=(k == nk - 1))
                last.then_inc(S("through") if u % 6 == 5 else S("unit"), 1)
            for u, (dst, rws, bank) in enumerate(KQT):
                who, part = ("k", u) if u < 6 else ("q", u - 6)
                if part == 0:
                    pe.wait_ge(S("roped"), 1 if who == "k" else 2)
                if u == 0:
                    pe.wait_ge(S("unit_out"), 11)
                    pe.wait_ge(S("rstds"), nidx["qh"] + 1)
                if u >= 8:
                    pe.wait_ge(S("kq_even" if u % 2 == 0 else "kq_odd"), (u - 8) // 2 + 1)
                src = (kF if who == "k" else qF).rearrange("p (t h) n -> p t h n", t=NT)
                for h in (2 * (part % 3), 2 * (part % 3) + 1):
                    for t in range(NT):
                        v = src[:, t, h, 0:NOPE] if part < 3 else src[:, t, h, NOPE:QKH]
                        last = tr(PS[0:rws, bank, (h % 2) * SEQ + t * P:(h % 2) * SEQ + (t + 1) * P], v)
                last.then_inc(S("kq_t"), 1)
            pe.wait_ge(S("kq_even"), 6)
            pe.wait_ge(S("kq_odd"), 6)
            for h in range(BH):
                for t, (c0, c1) in enumerate(((0, P), (P, 3 * P))):
                    nk = (t + 1) * P
                    mm(PS[:, h, c0:c1], lhsT=qTn[:, h, t * P:(t + 1) * P], rhs=kTn[:, h, 0:nk], start=True, stop=False)
                    mm(PS[:, h, c1 - P:c1], lhsT=ident[:, :], rhs=mask_qk[:, :], start=False, stop=False)
                    last = mm(PS[:, h, c0:c1], lhsT=qTr[:, h, t * P:(t + 1) * P], rhs=kTr[:, h, 0:nk], start=False, stop=True)
                last.then_inc(S("att_scores"), 1)
            for u, bank in enumerate(PTB):
                for f in range(4 * u, min(4 * u + 4, 3 * BH)):
                    h, b = f // 3, f % 3
                    if b == 0 or f == 4 * u:
                        pe.wait_ge(S("att_exp"), BH if u >= 2 else h + 1)
                    last = tr(PS[:, bank, (f % 4) * P:(f % 4 + 1) * P], Pb[:, h, b * P:(b + 1) * P])
                last.then_inc(S("att_pt"), 1)
            pe.wait_ge(S("att_pt_even"), 3)
            pe.wait_ge(S("att_pt_odd"), 2)
            for t in range(NT):
                for h in range(BH):
                    c = t * BH + h
                    for m in range(t + 1):
                        last = mm(PS[:, 3 + c // 4, (c % 4) * VH:(c % 4 + 1) * VH], lhsT=PT[:, h, (t + m) * P:(t + m + 1) * P],
                                  rhs=vF[:, m, h, :], start=(m == 0), stop=(m == t))
            last.then_inc(S("att_out"), 1)
            pe.wait_ge(S("mixed"), 2)
            pe.wait_ge(S("att_mixed"), 1)
            transposes("mix1")
            evicted("mix1")
            project_out(("bout0", "bout1"))
            transposes("x3")
            evicted("x3")
            pe.wait_ge(S("router_in"), 16)
            natural([(2, 0), (2, NE)], xT, router, NE).then_inc(S("logits"), 1)
            pe.wait_ge(S("chosen"), 1)
            mm(PS[:, 3, 0:NE], lhsT=before[:, :], rhs=chosen[:, 0], start=True, stop=True)
            mm(PS[:, 3, NE:2 * NE], lhsT=ones[:, :], rhs=chosen[:, 0], start=True, stop=False)
            mm(PS[:, 3, NE:2 * NE], lhsT=before[:, :], rhs=chosen[:, 1], start=False, stop=True)
            mm(PS[:, 3, 2 * NE:3 * NE], lhsT=ones[:, :], rhs=chosen[:, 0], start=True, stop=False)
            mm(PS[:, 3, 2 * NE:3 * NE], lhsT=ones[:, :], rhs=chosen[:, 1], start=False, stop=True).then_inc(S("ranks"), 1)

            def gather():
                for k in range(KD):
                    for t in range(NT):
                        last = mm(PS[:, 6 + k // 4, (k % 4) * CAP:(k % 4 + 1) * CAP], lhsT=xn[:, t, k * P:(k + 1) * P],
                                  rhs=Sx[:, t, :], start=(t == 0), stop=(t == NT - 1))
                last.then_inc(S("gathered"), 1)

            def combine(i):
                pe.wait_ge(S("y_low"), i + 1)
                pe.wait_ge(S("G_ready"), i + 1)
                for t in range(NT):
                    for hh in range(2):
                        for part in (yhi, ylo):
                            last = mm(PS[:, (6, 1)[t] + hh, :].rearrange("p (k n) -> p k n", n=P), lhsT=G[:, t, :],
                                      rhs=part[:, hh * KH:(hh + 1) * KH, :], start=part is yhi, stop=part is ylo)
                    last.then_inc(S("combined"), 1)

            pe.wait_ge(S("g1_in"), 16)
            for hh in range(2):
                last = mm(PS[:, 6 + hh, :], lhsT=ones[0:1, :], rhs=g1row[:, hh * HD:(hh + 1) * HD], start=True, stop=True)
            last.then_inc(S("g1_rows"), 1)
            pe.wait_ge(S("zeros"), 2)
            for hh in range(2):
                mm(PS[:, 4 + hh, :], lhsT=zeros, rhs=xT[:, 0:2, :].rearrange("p a b -> p (a b)"), start=True, stop=True)
            pe.wait_ge(S("routed"), 1)
            passes = pe.value_load(cnt_i[0:1, 0:1], min_val=1, max_val=PASSES)
            pe.wait_ge(S("dispatch"), 1)
            pe.wait_ge(S("x3_gained"), 1)
            gather()
            def expert(i):
                def next_tokens():
                    pe.wait_ge(S("dispatch"), i + 2)
                    pe.wait_ge(S("added"), i * NT + NT)
                    gather()

                def turn_gates():
                    pe.wait_ge(S("added"), i * NT + NT)
                    for t in range(NT):
                        tr(PS[:, 2, t * P:(t + 1) * P], Sx[:, t, :])
                    for t in range(NT):
                        last = mm(PS[:, 2, SEQ:SEQ + 1], lhsT=Sx[:, t, :], rhs=combe[:, t:t + 1], start=(t == 0), stop=(t == NT - 1))
                    last.then_inc(S("G_turned"), 1)

                pe.wait_ge(S("xlo_ready"), i + 1)
                swiglu(i, 1, lambda: combine(i), turn_gates, next_tokens)

            expert(0)
            with pe.Fori(1, passes * NE) as i:
                expert(i)
            pe.wait_ge(S("xlo_ready"), passes * NE + 1)
            combine(passes * NE)

        @block.vector
        def _(dve):
            v = nc.vector
            chain = [0]

            def then(ins):
                chain[0] += 1
                ins.then_inc(S("dve_step"), 1)
                dve.wait_ge(S("dve_step"), chain[0])

            def norm(name, gain=None, meanwhile=None):
                e, (src, dst, w), g = nidx[name], nview[name], groups(name)
                dst = src if dst is None else dst
                if name not in OWN_SUMS:
                    dve.wait_ge(S("squares"), squares_no[name])
                    v.tensor_reduce(shaped(sums(name), name), sq_of(name), AX.X, ALU.add).then_inc(S("sums"), 1)
                if meanwhile:
                    meanwhile()
                dve.wait_ge(S("rstds"), e + 1)
                if name in LATE:
                    v.tensor_copy(rx[:, :], rstd[:, e % 2, 0:NT]).then_inc(S("scaled"), 1)
                    return
                if gain is not None:
                    for k in range(g):
                        last = v.scalar_tensor_tensor(out=dst[:, k], in0=src[:, k], scalar=rstd[:, e % 2, k:k + 1], in1=gain,
                                                      op0=ALU.mult, op1=ALU.mult)
                elif w == D:
                    for t in range(NT):
                        last = v.tensor_scalar(dst[:, t], src[:, t], rstd[:, e % 2, t:t + 1], None, ALU.mult)
                else:
                    last = v.tensor_tensor(dst, src, bcast(shaped(rstd[:, e % 2, :], name), w), ALU.mult)
                last.then_inc(S("scaled"), 1)

            def evict(name):
                i, (_, _, bank, dsts) = tidx[name], TR[tidx[name]]
                for b in (1, 3):
                    dve.wait_ge(S("transposed"), 4 * i + b + 1)
                    for dst, g in dsts:
                        for k in (2 * b, 2 * b + 1):
                            s, src = k_gain(name, g, k), PS[:, bank + b, (k % 2) * SEQ:(k % 2 + 1) * SEQ]
                            if s is None:
                                last = v.tensor_copy(dst[:, k, :], src)
                            else:
                                last = v.tensor_scalar(dst[:, k, :], src, s, None, ALU.mult)
                    last.then_inc(S("evicted_odd"), 1)

            def lo_of(i, n, r=None):
                dve.wait_ge(S("highs"), count(i, PER, r, 3, cuts_before(i) + n + 1))
                h = ((E0 if i is not None else 0) + n) % SLOTS
                m = SLOT - POOL_COLS
                v.tensor_tensor(wlo[:, n % CUTS, 0:m], ring[:, h * SLOT:h * SLOT + m], whi[:, n % CUTS, 0:m].bitcast(F32),
                                ALU.subtract).then_inc(S("lows"), 1)

            def block(i, b, nt, r=None):
                for n in cut_item(b):
                    if b > 0 or not early(i):
                        lo_of(i, n, r)
                    if b == 1 and n == 3 * b + 1 and i is not None:
                        add(i, "added", 0)
                if b == 0 and i is not None:
                    y_low(i)
                dve.wait_ge(S("silu"), count(i, NB, r, 1, blocks_before(i) + b + 1))
                for t in range(nt):
                    up = PS[:, t, FB:2 * FB]
                    if i is None:
                        last = v.scalar_tensor_tensor(out=hn[:, t], in0=up, scalar=rx[:, t:t + 1], in1=sil[:, t], op0=ALU.mult, op1=ALU.mult)
                    else:
                        last = v.tensor_tensor(hn[:, t], up, sil[:, t], ALU.mult)
                last.then_inc(S("h_ready"), 1)
                if 3 * b + 3 < PER:
                    lo_of(i, 3 * b + 3, r)
                if b == NB - 1 and i is not None:
                    gathered(i + 1)
                dve.wait_ge(S("h_high"), count(i, NB, r, 1, blocks_before(i) + b + 1))
                src = PS[:, 3, :].rearrange("p (a s) -> p a s", a=2)
                v.tensor_tensor(hlo[:, :, hcols(b, nt)], src[:, :, 0:nt * P], hhi[:, :, hcols(b, nt)].bitcast(F32),
                                ALU.subtract).then_inc(S("h_low"), 1)

            def y_low(i):
                dve.wait_ge(S("y_high"), i + 1)
                v.scalar_tensor_tensor(out=ylo, in0=PS[:, 4:6, :].rearrange("p a (k n) -> p (a k) n", n=P), scalar=gate[:, 0:1],
                                       in1=yhi.bitcast(F32), op0=ALU.mult, op1=ALU.subtract).then_inc(S("y_low"), 1)

            def next_dispatch(i):
                dve.wait_ge(S("G_turned"), i + 1)
                v.tensor_copy(G[:, :, :], PS[:, 2, 0:SEQ].rearrange("p (t s) -> p t s", t=NT)).then_inc(S("G_ready"), 1)
                v.tensor_copy(gate, PS[:, 2, SEQ:SEQ + 1])
                for t in range(NT):
                    last = v.tensor_scalar(Sx[:, t], iota, keys[:, t, bass.ds(i + 1, 1)], None, ALU.is_equal)
                v.tensor_copy(combe, combs[:, :, bass.ds(i + 1, 1)].rearrange("p t a -> p (t a)")).then_inc(S("dispatch"), 1)

            def swiglu(i, nt):
                if not early(i):
                    lo_of(i, 0)
                for b in (0, 1):
                    block(i, b, nt)
                if i is not None:
                    add(i, "added", 1)
                with dve.Fori(0, len(REST)) as r:
                    for b in (2, 3):
                        block(i, b, nt, r)
                if i is not None:
                    next_dispatch(i)
                for b in (NB - 2, NB - 1):
                    block(i, b, nt)

            def mem_max(l, bank):
                dve.wait_ge(S("mem_scores"), l + 1)
                for t in range(NT):
                    src = PS[:, bank + 2 * t:bank + 2 * t + 2, :].rearrange("p par (pair m) -> p pair par m", pair=2)
                    last = v.tensor_reduce(smax[:, t * MH:(t + 1) * MH].rearrange("p (a b) -> p a b", a=2), src, AX.X, ALU.max)
                then(last)
                v.tensor_scalar(sbias[:, 0:8], smax[:, 0:8], -float(MD) ** -0.5, None, ALU.mult).then_inc(S("mem_max"), 1)

            def mem_turned(l, tb):
                for b in range(2):
                    dve.wait_ge(S("mem_pt"), 4 * l + 2 * b + 2)
                    v.tensor_copy(mPT[:, b, 2:4].rearrange("p h m q -> p (h m q)"), PS[:, tb + 2 * b + 1, :]).then_inc(S("mem_pt_odd"), 1)

            def mem_out(l):
                dve.wait_ge(S("mem_exp"), l + 1)
                then(v.reciprocal(srec[:, 0:8], ssum[:, 0:8]))
                dve.wait_ge(S("mem_out"), l + 1)
                v.tensor_tensor(nat(mix[:, :, D - MW:D], MD), PS[:, 4, :].rearrange("p (t h n) -> p t h n", t=NT, h=MH),
                                bcast(srec[:, 0:8].rearrange("p (a b) -> p a b", a=NT), MD), ALU.mult).then_inc(S("mixed"), 1)

            def add_out(n, l=None):
                for t in range(NT):
                    if t == 0 and l is not None:
                        dve.wait_ge(S("projected"), l + 1)
                    else:
                        dve.wait_ge(S("through"), n)
                    xv = xres[:, t].rearrange("p (a b) -> p a b", a=2)
                    v.tensor_tensor(xv, PS[:, 4 + 2 * t:6 + 2 * t, :], xv, ALU.add).then_inc(S("x_sum"), 1)

            norm("mem")
            norm("x0")
            dve.wait_ge(S("gains_t"), 1)
            v.tensor_copy(gains[:, :], PS[:, 7, 0:NG]).then_inc(S("gains"), 1)
            v.tensor_copy(hg[:, :], PS[:, 6, 0:2 * QKH]).then_inc(S("gains"), 1)
            dve.wait_ge(S("gains"), 2)
            evict("mem")
            evict("x0")
            dve.wait_ge(S("kS"), 2)
            norm("mk0")
            norm("mk1")
            dve.wait_ge(S("gate_in"), 2)
            v.scalar_tensor_tensor(out=gt, in0=gf, scalar=-1.0, in1=gf, op0=ALU.mult, op1=ALU.max).then_inc(S("gate_abs"), 1)
            v.memset(gone, 1.0)
            then(v.tensor_scalar(gf, gf, 0.0, None, ALU.min))
            dve.wait_ge(S("gate_exp"), 2)
            then(v.tensor_tensor(glf, gf, gt, ALU.subtract))
            then(v.tensor_tensor_scan(gG, gone, glf, 0.0, ALU.mult, ALU.add))
            then(v.tensor_tensor(ga, gi, gG, ALU.subtract))
            then(v.tensor_tensor_scan(gM, ga, ga, 0.0, ALU.max, ALU.max))
            v.tensor_tensor(gm, gG, gM, ALU.add).then_inc(S("gate_m"), 1)
            v.tensor_scalar(gneg, gM, -1.0, None, ALU.mult).then_inc(S("gate_neg"), 1)
            norm("mq0")
            dve.wait_ge(S("through"), through("k"))
            for b in range(2):
                last = v.tensor_scalar(kT[0:AQ, 2 * b:2 * b + 2, :], PS[0:AQ, b, :].rearrange("p (h s) -> p h s", h=2),
                                       float(AQ) ** -0.5, None, ALU.mult)
            last.then_inc(S("kT"), 1)
            v.memset(v1[:, :, :, AV:VW], 1.0)
            for half in range(2):
                dve.wait_ge(S("through"), through(f"v{half}"))
                for t in range(NT):
                    last = v.tensor_copy(v1[:, t, 2 * half:2 * half + 2, 0:AV],
                                         PS[:, 2 + 2 * half + t, 0:hv].rearrange("p (h n) -> p h n", h=2))
                last.then_inc(S("v_out"), 1)
            for l in range(2):
                dve.wait_ge(S("memk_t"), l + 1)
                g = gcol[f"memk{l}"]
                v.tensor_scalar(memkT[:, l], PS[:, 2 + l, :].rearrange("p (a s) -> p a s", a=2), gains[:, g:g + 1], None,
                                ALU.mult).then_inc(S("memkT"), 1)
            dve.wait_ge(S("mq_t"), 1)
            g = gcol["memq0"]
            v.tensor_scalar(mqT, PS[:, 4, :].rearrange("p (a s) -> p a s", a=2), gains[:, g:g + 1], None,
                            ALU.mult).then_inc(S("mqT"), 1)
            dve.wait_ge(S("gate_t"), 1)
            v.tensor_copy(gN[:, :, :, :].rearrange("p a b c -> p (a b c)"), PS[:, 5, 0:2 * NT * AH]).then_inc(S("gN"), 1)
            dve.wait_ge(S("scaled"), nidx["mq0"] + 1)
            for h in range(AH):
                dve.wait_ge(S("decay"), h + 1)
                dve.wait_ge(S("kq"), h + 1)
                v.tensor_tensor(PmT[:, h, :], PS[:, 4 + h, 0:384], Dm[:, h, :], ALU.mult).then_inc(S("weights"), 1)
            mem_max(0, 4)
            dve.wait_ge(S("num"), AH)
            dv = den[:, :].rearrange("p (t h) -> p t h", t=NT)
            src = PS[:, 0:AH, :].rearrange("p h (t n) -> p t h n", t=NT)
            then(v.tensor_copy(dv, src[:, :, :, AV]))
            then(v.scalar_tensor_tensor(out=dv, in0=dv, scalar=-1.0, in1=dv, op0=ALU.mult, op1=ALU.max))
            then(v.tensor_tensor(dv, dv, gN[:, 1], ALU.max))
            then(v.reciprocal(den[:, :], den[:, :]))
            hview = nat(mix[:, :, 0:avw], AV)
            for t in range(NT):
                last = v.tensor_tensor(hview[:, t], src[:, t, :, 0:AV], bcast(dv[:, t], AV), ALU.mult)
            last.then_inc(S("h_out"), 1)
            norm("hm", meanwhile=lambda: mem_turned(0, 4))
            dve.wait_ge(S("scaled"), nidx["hm"] + 1)
            dve.wait_ge(S("og"), 2)
            v.tensor_tensor(mix[:, :, 0:avw], mix[:, :, 0:avw], og, ALU.mult)
            mem_out(0)
            evict("mix0")
            for n in range(CUTS):
                lo_of(None, n)
            add_out(through("aout1"), 0)
            for k in range(KD):
                if k % 2 == 0:
                    dve.wait_ge(S("x1_high"), k // 2 + 1)
                last = v.scalar_tensor_tensor(out=xlo[:, k, :], in0=PS[:, k // 2, (k % 2) * SEQ:(k % 2 + 1) * SEQ],
                                              scalar=k_gain("x1", "ffn0", k), in1=xhi[:, k, :].bitcast(F32),
                                              op0=ALU.mult, op1=ALU.subtract)
                if k % 2 == 1:
                    last.then_inc(S("x1_low"), 1)
            norm("x1")
            TWO_PI = 2.0 * np.pi
            part, left = [], TWO_PI
            for n in range(3):
                step = 2.0 ** (np.floor(np.log2(left)) - 7)
                part.append(float(np.floor(left / step) * step))
                left -= part[-1]
            part.append(float(np.float32(left)))
            HALF_TURN = 3.1415925
            dve.wait_ge(S("pos_in"), 16)
            dve.wait_ge(S("freqs"), 1)
            then(v.tensor_copy(posf[:, :], posi[:, :]))
            for t in range(NT):
                last = v.tensor_scalar(rot[:, 0, t], invf[:, :], posf[:, t:t + 1], None, ALU.mult)
            then(last)
            then(v.tensor_scalar(roti[:, :, :], rot[:, 0], float(1.0 / TWO_PI), None, ALU.mult))
            then(v.tensor_copy(rot[:, 1], roti[:, :, :]))
            for c in part:
                then(v.scalar_tensor_tensor(out=rot[:, 0], in0=rot[:, 1], scalar=-c, in1=rot[:, 0], op0=ALU.mult, op1=ALU.add))
            v.tensor_scalar(rot[:, 2], rot[:, 0], HALF_TURN, -HALF_TURN, ALU.min, ALU.max)
            then(v.tensor_scalar(rot[:, 3], rot[:, 0], float(np.pi / 2), None, ALU.add))
            then(v.tensor_scalar(rot[:, 1], rot[:, 3], float(np.pi), -TWO_PI, ALU.is_gt, ALU.mult))
            then(v.tensor_tensor(rot[:, 3], rot[:, 3], rot[:, 1], ALU.add))
            v.tensor_scalar(rot[:, 3], rot[:, 3], HALF_TURN, -HALF_TURN, ALU.min, ALU.max).then_inc(S("angles"), 1)
            swiglu(None, NT)
            add_out(FFN0 + PER)
            evict("x2")
            norm("x2")
            dve.wait_ge(S("zS"), 1)
            kF4 = kF.rearrange("p (t h) n -> p t h n", t=NT)
            qF4 = qF.rearrange("p (t h) n -> p t h n", t=NT)

            def per_head(ap, n):
                dims = [list(d) for d in ap.ap]
                return bass.AP(ap.tensor, ap.offset, dims[:-1] + [[0, n]] + dims[-1:])

            for t in range(NT):
                last = v.tensor_copy(kF4[:, t, :, NOPE:QKH], per_head(zS[:, t, KVL:KVL + ROPE], BH))
            last.then_inc(S("k_rope_in"), 1)
            norm("ckv")
            norm("cq")
            norm("mq1")
            for n, (dst, name, view, nk) in enumerate((
                    (ckvT, "kv_a", PS[:, 1:2, :], 2), (cqT, "q_a", PS[:, 2:4, :], 3), (mqT1, "memq1", PS[:, 4:5, :], 2))):
                dve.wait_ge(S("lat_t"), n + 1)
                for k in range(nk):
                    g = gcol[name] + (k if n < 2 else 0)
                    last = v.tensor_scalar(dst[:, k], view[:, k // 2, (k % 2) * SEQ:(k % 2 + 1) * SEQ], gains[:, g:g + 1], None, ALU.mult)
                last.then_inc(S("lat_out"), 1)
            mem_max(1, 4)
            mem_turned(1, 4)
            mem_out(1)
            dve.wait_ge(S("sincos"), 2)
            sin, cos = rot[:, 4], rot[:, 5]
            tmp = xT[:, :, :].rearrange("p a b -> p (a b)")[:, 0:4 * NT * BH * HR].rearrange(
                "p (q t h n) -> p q t h n", q=4, t=NT, h=BH)
            for name, full, g0 in (("kh", kF4, 0), ("qh", qF4, QKH)):
                norm(name, hg[:, g0:g0 + QKH])
                dve.wait_ge(S("scaled"), nidx[name] + 1)
                x1, x2 = full[:, :, :, NOPE:NOPE + HR], full[:, :, :, NOPE + HR:QKH]
                for q, (a, b) in enumerate(((x1, cos), (x2, sin), (x2, cos), (x1, sin))):
                    last = v.tensor_tensor(tmp[:, q], a, per_head(b, BH), ALU.mult)
                then(last)
                v.tensor_tensor(x1, tmp[:, 0], tmp[:, 1], ALU.subtract)
                v.tensor_tensor(x2, tmp[:, 2], tmp[:, 3], ALU.add).then_inc(S("roped"), 1)
            for u, (dst, n, bank) in enumerate(KQT):
                if u % 2 == 1:
                    dve.wait_ge(S("kq_t"), u + 1)
                    v.tensor_copy(dst, PS[0:n, bank, :].rearrange("p (h s) -> p h s", h=2)).then_inc(S("kq_odd"), 1)
            HB = BH // 2
            by_tile = [x[:, 0:2 * BH].rearrange("p (t h) -> p t h", t=NT) for x in (smax, sbias)]
            for half in range(2):
                hs = slice(half * HB, (half + 1) * HB)
                dve.wait_ge(S("att_scores"), (half + 1) * HB)
                v.tensor_reduce(by_tile[0][:, 0, hs], PS[:, hs, 0:P], AX.X, ALU.max)
                then(v.tensor_reduce(by_tile[0][:, 1, hs], PS[:, hs, P:3 * P], AX.X, ALU.max))
                v.tensor_scalar(by_tile[1][:, :, hs], by_tile[0][:, :, hs], -float(QKH) ** -0.5, None, ALU.mult).then_inc(S("att_max"), 1)
            for u, bank in enumerate(PTB):
                if u % 2 == 1:
                    dve.wait_ge(S("att_pt"), u + 1)
                    v.tensor_copy(PT.rearrange("p a b -> p (a b)")[:, 512 * u:512 * u + 512], PS[:, bank, :]).then_inc(S("att_pt_odd"), 1)
            dve.wait_ge(S("att_exp"), BH)
            then(v.reciprocal(srec[:, 0:2 * BH], ssum[:, 0:2 * BH]))
            dve.wait_ge(S("att_out"), 1)
            for t in range(NT):
                blocks = PS[:, 3:6, :].rearrange("p a b -> p (a b)")[:, t * BH * VH:(t + 1) * BH * VH]
                last = v.tensor_tensor(mix[:, t, 0:BH * VH].rearrange("p (h n) -> p h n", h=BH),
                                       blocks.rearrange("p (h n) -> p h n", h=BH), bcast(srec[:, t * BH:(t + 1) * BH], VH), ALU.mult)
            last.then_inc(S("att_mixed"), 1)
            evict("mix1")
            for n in range(CUTS - 1):
                lo_of(0, n)
            add_out(through("bout1"), 1)
            evict("x3")
            norm("x3")
            dve.wait_ge(S("logits"), 1)
            dve.wait_ge(S("scaled"), nidx["x3"] + 1)
            dve.wait_ge(S("iota"), 1)
            for t in range(NT):
                last = v.tensor_scalar(lg[:, t], PS[:, 2, t * NE:(t + 1) * NE], rx[:, t:t + 1], None, ALU.mult)
            then(last)
            for t in range(NT):
                last = v.max(m8[:, t], lg[:, t])
            then(last)
            for t in range(NT):
                v.tensor_tensor(gt2[:, t:t + 1], m8[:, t, 1:2], m8[:, t, 0:1], ALU.subtract)
                last = v.max_index(idx8[:, t], m8[:, t], lg[:, t])
            last.then_inc(S("top2"), 1)
            dve.wait_ge(S("top2"), 1)
            then(v.tensor_copy(idxf, idx8))
            for t in range(NT):
                v.tensor_scalar(oh1[:, t], iota[:, 0:NE], idxf[:, t, 0:1], None, ALU.is_equal)
                last = v.tensor_scalar(oh2[:, t], iota[:, 0:NE], idxf[:, t, 1:2], None, ALU.is_equal)
            then(last)
            v.tensor_tensor(chosen, oh1, oh2, ALU.add).then_inc(S("chosen"), 1)
            dve.wait_ge(S("gate2_exp"), 1)
            then(v.tensor_scalar(gt2[:, 4:6], gt2[:, 2:4], 1.0, None, ALU.add))
            then(v.reciprocal(gt2[:, 6:8], gt2[:, 4:6]))
            then(v.tensor_tensor(gt2[:, 8:10], gt2[:, 6:8], gt2[:, 2:4], ALU.mult))
            for t in range(NT):
                last = v.tensor_scalar(oh1[:, t], oh1[:, t], gt2[:, 6 + t:7 + t], None, ALU.mult)
            then(last)
            for t in range(NT):
                for q in range(PASSES + 1):
                    last = v.scalar_tensor_tensor(out=combs[:, t, q * NE:(q + 1) * NE], in0=oh2[:, t], scalar=gt2[:, 8 + t:9 + t],
                                                  in1=oh1[:, t], op0=ALU.mult, op1=ALU.add)
            dve.wait_ge(S("chosen"), 1)
            dve.wait_ge(S("ranks"), 1)
            then(v.scalar_tensor_tensor(out=keys[:, :, 0:NE], in0=PS[:, 3, 0:NT * NE].rearrange("p (t n) -> p t n", t=NT),
                                        scalar=4096.0, in1=chosen, op0=ALU.add, op1=ALU.mult))
            then(v.tensor_scalar(keys[:, :, 0:NE], keys[:, :, 0:NE], -4096.0, None, ALU.add))
            for q in range(1, PASSES + 1):
                last = v.tensor_scalar(keys[:, :, q * NE:(q + 1) * NE], keys[:, :, 0:NE], -float(q * CAP), None, ALU.add)
            then(last)
            then(v.tensor_reduce(gt2[:, 10:11], PS[:, 3, 2 * NE:3 * NE], AX.X, ALU.max))
            then(v.tensor_scalar(gt2[:, 11:12], gt2[:, 10:11], float(CAP), 1.0, ALU.is_gt, ALU.add))
            for q in range(2, PASSES):
                then(v.scalar_tensor_tensor(out=gt2[:, 11:12], in0=gt2[:, 10:11], scalar=float(q * CAP), in1=gt2[:, 11:12],
                                            op0=ALU.is_gt, op1=ALU.add))
            v.tensor_copy(cnt_i[:, :], gt2[:, 11:12]).then_inc(S("routed"), 1)
            for t in range(NT):
                v.tensor_scalar(Sx[:, t], iota, keys[:, t, 0:1], None, ALU.is_equal)
            v.tensor_copy(combe, combs[:, :, 0]).then_inc(S("dispatch"), 1)
            dve.wait_ge(S("zeros"), 2)
            for t in range(NT):
                last = v.tensor_copy(G[:, t, :], zeros)
            last.then_inc(S("G_ready"), 1)
            dve.wait_ge(S("g1_rows"), 1)
            for t in range(NT):
                last = v.scalar_tensor_tensor(out=xn[:, t].rearrange("p (a b) -> p a b", a=2),
                                              in0=xres[:, t].rearrange("p (a b) -> p a b", a=2), scalar=rx[:, t:t + 1],
                                              in1=PS[:, 6:8, :], op0=ALU.mult, op1=ALU.mult)
            last.then_inc(S("x3_gained"), 1)
            lo_of(0, CUTS - 1)
            dve.wait_ge(S("routed"), 1)
            passes = dve.value_load(cnt_i[0:1, 0:1], min_val=1, max_val=PASSES)

            def gathered(i):
                dve.wait_ge(S("xhi_ready"), i + 1)
                v.tensor_tensor(xlo[:, :, xe_], PS[:, 6:8, :].rearrange("p a (k n) -> p (a k) n", n=CAP),
                                xhi[:, :, xe_].bitcast(F32), ALU.subtract).then_inc(S("xlo_ready"), 1)

            def add(i, sem, t):
                dve.wait_ge(S("combined"), i * NT + (t + 1))
                xv = xres[:, t].rearrange("p (a b) -> p a b", a=2)
                v.tensor_tensor(xv, PS[:, (6, 1)[t]:(6, 1)[t] + 2, :], xv, ALU.add).then_inc(S(sem), 1)

            gathered(0)
            swiglu(0, 1)
            with dve.Fori(1, passes * NE) as i:
                swiglu(i, 1)
            y_low(passes * NE)
            for t in range(NT):
                add(passes * NE, "x_final", t)


_NAMES = ["x", "mem", "positions", "a_norm", "a_w_in", "a_gate_bias", "a_head_norm", "a_w_out", "b_norm", "b_w_in",
          "b_q_a_norm", "b_w_uq", "b_q_head_norm", "b_w_out", "kv_norm", "w_dkv", "kv_a_norm", "w_ukv", "k_head_norm",
          "mem_norm", "mem_w_kv", "mem_q_norm", "mem_k_norm", "ffn_norm", "dense_w_gate_up", "dense_w_down",
          "moe_router", "moe_w_gate_up", "moe_w_down"]


def kernel(**inputs):
    import concourse.bacc as bacc
    from concourse.bass_utils import run_bass_kernel_spmd

    nc = bacc.Bacc("TRN2", target_bir_lowering=False, num_devices=1)
    arrays, views = {}, {}
    for name in _NAMES:
        a = np.ascontiguousarray(inputs[name])
        arrays[f"in_{name}"] = a
        views[name] = nc.dram_tensor(f"in_{name}", a.shape, mybir.dt.from_np(a.dtype), kind="ExternalInput").ap()
    shape = arrays["in_x"].shape
    out = nc.dram_tensor("out_x", shape, F32, kind="ExternalOutput").ap()
    build(nc, views, out)
    r = run_bass_kernel_spmd(nc, [arrays], core_ids=[0])
    return r.results[0]["out_x"]
```
